# Optimizing a Trainium2 kernel written in Bass

```python
import math
import jax, jax.numpy as jnp
from jax import lax
import numpy as np

D_MODEL = 1024
BATCH = 1
SEQ = 128
DEPTH = 2
DEC_BATCH = 1
DEC_SEQ = 512
PAST_LEN = 128

GRID_W = 64
N_EVEN = (DEPTH + 1) // 2
N_ODD = DEPTH // 2
A_DIM = D_MODEL // 2
A_GROUPS = 4
A_GROUP_DIM = A_DIM // A_GROUPS
CHUNK = 128
B_DIM = D_MODEL // 2
B_CONV = 31
C_DIM = D_MODEL // 2
C_HEAD_DIM = 64
C_HEADS = C_DIM // C_HEAD_DIM
DECAY_LORA = 64
ICLR_LORA = 64
GATE_LORA = 128
GN_EPS = 64e-5
HEAD_DIM = 64
D_HEADS = (D_MODEL // 2) // HEAD_DIM
D_KV_HEADS = 2
D_Q_DIM = D_HEADS * HEAD_DIM
D_KV_DIM = D_KV_HEADS * HEAD_DIM
ROPE_AXIS_DIM = HEAD_DIM // 2
ROPE_THETA = 10000.0
Q_BLOCK = 128
D_FF = 2816
FFN_CONV = 3
EPS = 1e-6

kernel_name = 'hybrid_dit_gmlp_conformer_rwkv7_gqa_step'

def rmsnorm(x, g, eps=EPS):
    xf = x.astype(jnp.float32)
    y = xf * lax.rsqrt(jnp.mean(xf * xf, -1, keepdims=True) + eps)
    return (y * g.astype(jnp.float32)).astype(x.dtype)

def layernorm(x, g, b, eps=EPS):
    xf = x.astype(jnp.float32)
    xc = xf - jnp.mean(xf, -1, keepdims=True)
    y = xc * lax.rsqrt(jnp.mean(xc * xc, -1, keepdims=True) + eps)
    return (y * g.astype(jnp.float32) + b.astype(jnp.float32)).astype(x.dtype)

def adaln(x, g, shift, scale):
    return rmsnorm(x, g) * (1 + scale) + shift

def modulation(cvec, w_mod, b_mod):
    m = jax.nn.silu(cvec) @ w_mod + b_mod
    return jnp.split(m[:, None, :], 6, axis=-1)

def dwconv(x, w, b):
    k = w.shape[0]
    y = lax.conv_general_dilated(x, w[:, None, :].astype(x.dtype), window_strides=(1,),
                                 padding=[(k // 2, k // 2)],
                                 dimension_numbers=('NWC', 'WIO', 'NWC'),
                                 feature_group_count=x.shape[-1])
    return y + b.astype(x.dtype)

def token_shift_delta(x):
    xp = jnp.pad(x, ((0, 0), (1, 1), (0, 0)))
    return 0.5 * (xp[:, :-2] + xp[:, 2:]) - x

def grid_positions(n_tokens):
    rows = n_tokens // GRID_W
    row = jnp.repeat(jnp.arange(rows), GRID_W)
    col = jnp.tile(jnp.arange(GRID_W), rows)
    return row, col

def rope_axis(x, pos):
    half = x.shape[-1] // 2
    inv = ROPE_THETA ** (-jnp.arange(half, dtype=jnp.float32) / half)
    ang = pos.astype(jnp.float32)[:, None] * inv[None, :]
    cos = jnp.cos(ang)[None, :, None, :]
    sin = jnp.sin(ang)[None, :, None, :]
    x1, x2 = x[..., :half], x[..., half:]
    return jnp.concatenate([x1 * cos - x2 * sin, x1 * sin + x2 * cos], -1)

def rope2d(x):
    row, col = grid_positions(x.shape[1])
    xf = x.astype(jnp.float32)
    y = jnp.concatenate([rope_axis(xf[..., :ROPE_AXIS_DIM], row),
                         rope_axis(xf[..., ROPE_AXIS_DIM:], col)], -1)
    return y.astype(x.dtype)

def mixer_ab(h, w_in, w_out, v_g, v_b, ws, bs, conv_w, conv_b, norm_g):
    bsz, n, _ = h.shape
    z = h @ w_in
    za = jax.nn.gelu(z[..., :2 * A_DIM])
    u, v = za[..., :A_DIM], za[..., A_DIM:]
    v = layernorm(v, v_g, v_b).reshape(bsz, n // CHUNK, CHUNK, A_GROUPS, A_GROUP_DIM)
    v = jnp.einsum('gpq,bnqgc->bnpgc', ws, v) + bs.T[None, None, :, :, None]
    ya = u * v.reshape(bsz, n, A_DIM)
    zb = z[..., 2 * A_DIM:]
    glu = zb[..., :B_DIM] * jax.nn.sigmoid(zb[..., B_DIM:])
    yb = jax.nn.silu(rmsnorm(dwconv(glu, conv_w, conv_b), norm_g))
    return jnp.concatenate([ya, yb], -1) @ w_out

def wkv_scan(s0, r, w, k, v, kk, a, reverse):
    tm = lambda t: jnp.swapaxes(t, 0, 1)

    def step(s, inp):
        r_t, w_t, k_t, v_t, kk_t, a_t = inp
        sa = jnp.einsum('bhij,bhj->bhi', s, -kk_t)
        s = s * w_t[:, :, None, :] + sa[..., None] * (kk_t * a_t)[:, :, None, :] + v_t[..., None] * k_t[:, :, None, :]
        return s, jnp.einsum('bhij,bhj->bhi', s, r_t)

    s_fin, ys = lax.scan(step, s0, (tm(r), tm(w), tm(k), tm(v), tm(kk), tm(a)), reverse=reverse)
    return s_fin, tm(ys)

def rwkv_time_mix(h, r_p, k_p, v_p, s0_f, s0_b, mu_rkv, mu_wag, w0, w1, w2, a0, a1, a2,
                  g1, g2, k_k, k_a, r_k, ln_g, ln_b):
    bsz, n, _ = h.shape
    f32 = jnp.float32
    heads = lambda t: t.astype(f32).reshape(bsz, n, C_HEADS, C_HEAD_DIM)
    r = heads(r_p + token_shift_delta(r_p) * mu_rkv[0])
    k = heads(k_p + token_shift_delta(k_p) * mu_rkv[1])
    v = heads(v_p + token_shift_delta(v_p) * mu_rkv[2])
    dh = token_shift_delta(h)
    xw = h + dh * mu_wag[0]
    xa = h + dh * mu_wag[1]
    xg = h + dh * mu_wag[2]
    g = jax.nn.sigmoid(xg @ g1) @ g2
    kk = k * k_k.astype(f32).reshape(C_HEADS, C_HEAD_DIM)
    kk = kk * lax.rsqrt(jnp.sum(kk * kk, -1, keepdims=True) + 1e-12)
    k_a_h = k_a.astype(f32).reshape(C_HEADS, C_HEAD_DIM)

    def direction(d, s0, reverse):
        logw = -jax.nn.softplus(-(w0[d] + jnp.tanh(xw @ w1[d]) @ w2[d])) - 0.5
        decay = heads(jnp.exp(-jnp.exp(logw.astype(f32))))
        a = heads(jax.nn.sigmoid(a0[d] + (xa @ a1[d]) @ a2[d]))
        kd = k * (1 + (a - 1) * k_a_h)
        s_fin, y = wkv_scan(s0.astype(f32), r, decay, kd, v, kk, a, reverse)
        return y, kd, s_fin

    y_f, kd_f, s_f = direction(0, s0_f, False)
    y_b, kd_b, s_b = direction(1, s0_b, True)
    y = y_f + y_b
    yc = y - jnp.mean(y, -1, keepdims=True)
    yn = yc * lax.rsqrt(jnp.mean(yc * yc, -1, keepdims=True) + GN_EPS)
    yn = yn.reshape(bsz, n, C_DIM) * ln_g.astype(f32) + ln_b.astype(f32)
    bonus = jnp.sum(r * (kd_f + kd_b) * r_k.astype(f32), -1, keepdims=True) * v
    out = (yn + bonus.reshape(bsz, n, C_DIM)) * g.astype(f32)
    return out.astype(h.dtype), s_f, s_b

def gqa_attention(q, k, v):
    bsz, lq, nh, hd = q.shape
    grp = nh // D_KV_HEADS
    qb = (q * (hd ** -0.5)).reshape(bsz, lq // Q_BLOCK, Q_BLOCK, D_KV_HEADS, grp, hd)
    qb = jnp.moveaxis(qb, 1, 0)

    def block(qblk):
        s = jnp.einsum('bqkgd,blkd->bkgql', qblk, k, preferred_element_type=jnp.float32)
        p = jax.nn.softmax(s, axis=-1).astype(v.dtype)
        return jnp.einsum('bkgql,blkd->bqkgd', p, v)

    o = lax.map(block, qb)
    return jnp.moveaxis(o, 0, 1).reshape(bsz, lq, nh * hd)

def mixer_cd(h, w_in, w_out, s0_f, s0_b, ctx_k, ctx_v, cp, q_g, k_g, latent):
    bsz, n, _ = h.shape
    z = h @ w_in
    r_p, k_p, v_p, q, kd, vd = jnp.split(
        z, [C_DIM, 2 * C_DIM, 3 * C_DIM, 3 * C_DIM + D_Q_DIM, 3 * C_DIM + D_Q_DIM + D_KV_DIM], axis=-1)
    yc, s_f, s_b = rwkv_time_mix(h, r_p, k_p, v_p, s0_f, s0_b, *cp)
    q = rmsnorm(q.reshape(bsz, n, D_HEADS, HEAD_DIM), q_g)
    kd = rmsnorm(kd.reshape(bsz, n, D_KV_HEADS, HEAD_DIM), k_g)
    vd = vd.reshape(bsz, n, D_KV_HEADS, HEAD_DIM)
    if latent:
        q = rope2d(q)
        keys = jnp.concatenate([ctx_k.astype(kd.dtype), rope2d(kd)], axis=1)
        vals = jnp.concatenate([ctx_v.astype(vd.dtype), vd], axis=1)
    else:
        keys, vals = kd, vd
    yd = gqa_attention(q, keys, vals)
    out = jnp.concatenate([yc, yd], -1) @ w_out
    return out, kd, vd, s_f, s_b

def conv_ffn(h, w_up, cw, cb, w_down):
    z = dwconv(h @ w_up, cw, cb)
    return (jax.nn.silu(z[..., D_FF:]) * z[..., :D_FF]) @ w_down

def setup_inputs(seed: int = 0) -> dict:
    key = jax.random.key(seed)
    ks = iter(jax.random.split(key, 64))
    f32 = jnp.float32
    nrm = lambda shape, scale: jax.random.normal(next(ks), shape, f32) * scale
    lin = lambda shape: nrm(shape, shape[-2] ** -0.5)
    gain = lambda shape: 1.0 + nrm(shape, 0.02)
    uni = lambda shape: jax.random.uniform(next(ks), shape, f32)
    return {
        'x_prompt': nrm((BATCH, SEQ, D_MODEL), 1.0),
        'x_sample': nrm((DEC_BATCH, DEC_SEQ, D_MODEL), 1.0),
        'cache_k': nrm((DEC_BATCH, N_ODD, PAST_LEN, D_KV_HEADS, HEAD_DIM), 1.0),
        'cache_v': nrm((DEC_BATCH, N_ODD, PAST_LEN, D_KV_HEADS, HEAD_DIM), 1.0),
        'state_wkv_fwd': nrm((DEC_BATCH, N_ODD, C_HEADS, C_HEAD_DIM, C_HEAD_DIM), 0.5),
        'state_wkv_bwd': nrm((DEC_BATCH, N_ODD, C_HEADS, C_HEAD_DIM, C_HEAD_DIM), 0.5),
        'c': nrm((DEC_BATCH, D_MODEL), 1.0),
        'c_ctx': nrm((D_MODEL,), 1.0),
        'mod_w': lin((DEPTH, D_MODEL, 6 * D_MODEL)),
        'mod_b': nrm((DEPTH, 6 * D_MODEL), 0.02),
        'norm1_g': gain((DEPTH, D_MODEL)),
        'norm2_g': gain((DEPTH, D_MODEL)),
        'w_out': lin((DEPTH, D_MODEL, D_MODEL)),
        'ffn_up': lin((DEPTH, D_MODEL, 2 * D_FF)),
        'ffn_conv_w': nrm((DEPTH, FFN_CONV, 2 * D_FF), FFN_CONV ** -0.5),
        'ffn_conv_b': nrm((DEPTH, 2 * D_FF), 0.02),
        'ffn_down': lin((DEPTH, D_FF, D_MODEL)),
        'final_g': gain((D_MODEL,)),
        'ab_w_in': lin((N_EVEN, D_MODEL, 2 * A_DIM + 2 * B_DIM)),
        'a_vnorm_g': gain((N_EVEN, A_DIM)),
        'a_vnorm_b': nrm((N_EVEN, A_DIM), 0.02),
        'a_ws': nrm((N_EVEN, A_GROUPS, CHUNK, CHUNK), CHUNK ** -0.5),
        'a_bs': gain((N_EVEN, A_GROUPS, CHUNK)),
        'b_conv_w': nrm((N_EVEN, B_CONV, B_DIM), B_CONV ** -0.5),
        'b_conv_b': nrm((N_EVEN, B_DIM), 0.02),
        'b_norm_g': gain((N_EVEN, B_DIM)),
        'cd_w_in': lin((N_ODD, D_MODEL, 3 * C_DIM + D_Q_DIM + 2 * D_KV_DIM)),
        'c_mu_rkv': uni((N_ODD, 3, C_DIM)),
        'c_mu_wag': uni((N_ODD, 3, D_MODEL)),
        'c_w0': nrm((N_ODD, 2, C_DIM), 0.5),
        'c_w1': lin((N_ODD, 2, D_MODEL, DECAY_LORA)),
        'c_w2': lin((N_ODD, 2, DECAY_LORA, C_DIM)),
        'c_a0': nrm((N_ODD, 2, C_DIM), 0.1),
        'c_a1': lin((N_ODD, 2, D_MODEL, ICLR_LORA)),
        'c_a2': lin((N_ODD, 2, ICLR_LORA, C_DIM)),
        'c_g1': lin((N_ODD, D_MODEL, GATE_LORA)),
        'c_g2': lin((N_ODD, GATE_LORA, C_DIM)),
        'c_k_k': 0.85 + nrm((N_ODD, C_DIM), 0.02),
        'c_k_a': gain((N_ODD, C_DIM)),
        'c_r_k': nrm((N_ODD, C_HEADS, C_HEAD_DIM), 0.1),
        'c_ln_g': gain((N_ODD, C_DIM)),
        'c_ln_b': nrm((N_ODD, C_DIM), 0.02),
        'd_q_g': gain((N_ODD, HEAD_DIM)),
        'd_k_g': gain((N_ODD, HEAD_DIM)),
    }

def reference(x_prompt, x_sample, cache_k, cache_v, state_wkv_fwd, state_wkv_bwd, c, c_ctx,
              mod_w, mod_b, norm1_g, norm2_g, w_out, ffn_up, ffn_conv_w, ffn_conv_b, ffn_down, final_g,
              ab_w_in, a_vnorm_g, a_vnorm_b, a_ws, a_bs, b_conv_w, b_conv_b, b_norm_g,
              cd_w_in, c_mu_rkv, c_mu_wag, c_w0, c_w1, c_w2, c_a0, c_a1, c_a2, c_g1, c_g2,
              c_k_k, c_k_a, c_r_k, c_ln_g, c_ln_b, d_q_g, d_k_g):
    xc, xl = x_prompt, x_sample
    z0 = jnp.zeros((x_prompt.shape[0], C_HEADS, C_HEAD_DIM, C_HEAD_DIM), jnp.float32)
    new_k, new_v, new_sf, new_sb = [], [], [], []
    for layer in range(DEPTH):
        mc = modulation(c_ctx[None, :], mod_w[layer], mod_b[layer])
        ml = modulation(c, mod_w[layer], mod_b[layer])
        hc = adaln(xc, norm1_g[layer], mc[0], mc[1])
        hl = adaln(xl, norm1_g[layer], ml[0], ml[1])
        i = layer // 2
        if layer % 2 == 0:
            ab = (ab_w_in[i], w_out[layer], a_vnorm_g[i], a_vnorm_b[i], a_ws[i], a_bs[i],
                  b_conv_w[i], b_conv_b[i], b_norm_g[i])
            oc = mixer_ab(hc, *ab)
            ol = mixer_ab(hl, *ab)
        else:
            cp = (c_mu_rkv[i], c_mu_wag[i], c_w0[i], c_w1[i], c_w2[i], c_a0[i], c_a1[i], c_a2[i],
                  c_g1[i], c_g2[i], c_k_k[i], c_k_a[i], c_r_k[i], c_ln_g[i], c_ln_b[i])
            oc, kc, vc, sfc, sbc = mixer_cd(hc, cd_w_in[i], w_out[layer], z0, z0, None, None,
                                            cp, d_q_g[i], d_k_g[i], False)
            ol, _, _, _, _ = mixer_cd(hl, cd_w_in[i], w_out[layer], state_wkv_fwd[:, i], state_wkv_bwd[:, i],
                                      cache_k[:, i], cache_v[:, i], cp, d_q_g[i], d_k_g[i], True)
            new_k.append(kc)
            new_v.append(vc)
            new_sf.append(sfc.astype(x_prompt.dtype))
            new_sb.append(sbc.astype(x_prompt.dtype))
        xc = xc + mc[2] * oc
        xl = xl + ml[2] * ol
        ffn = (ffn_up[layer], ffn_conv_w[layer], ffn_conv_b[layer], ffn_down[layer])
        xc = xc + mc[5] * conv_ffn(adaln(xc, norm2_g[layer], mc[3], mc[4]), *ffn)
        xl = xl + ml[5] * conv_ffn(adaln(xl, norm2_g[layer], ml[3], ml[4]), *ffn)
    y_prompt = rmsnorm(xc, final_g)
    y_sample = rmsnorm(xl, final_g)
    return (y_prompt, y_sample, jnp.stack(new_k, axis=1), jnp.stack(new_v, axis=1),
            jnp.stack(new_sf, axis=1), jnp.stack(new_sb, axis=1))


_drawn_inputs = setup_inputs


def setup_inputs(seed=0):
    import zlib

    import numpy as np

    out = dict(_drawn_inputs(seed))
    spreads = {}
    factors = {'cache_k': 6.185,
     'cache_v': 5.403,
     'state_wkv_fwd': 8.0,
     'state_wkv_bwd': 8.0,
     'norm2_g': 3.278,
     'ffn_conv_b': 3.621,
     'final_g': 2.869,
     'a_vnorm_g': 7.013,
     'a_vnorm_b': 7.877,
     'a_bs': 7.314,
     'b_conv_b': 4.659,
     'b_norm_g': 7.761,
     'c_ln_g': 8.0,
     'c_ln_b': 8.0,
     'd_q_g': 8.0}
    for name, (base, spread) in spreads.items():
        noise = np.random.default_rng([zlib.crc32(name.encode()), seed]).standard_normal(out[name].shape)
        drawn = base * np.exp(spread * noise) if base else spread * noise
        out[name] = __import__('jax').numpy.asarray(drawn.astype(out[name].dtype))
    for name, factor in factors.items():
        out[name] = (out[name] * factor).astype(out[name].dtype)
    return out
```

```python
from contextlib import ExitStack

import numpy as np
import concourse.bass as bass
from concourse import mybir
from concourse.alu_op_type import AluOpType as ALU

F32 = mybir.dt.float32
ACT = mybir.ActivationFunctionType
AX = mybir.AxisListType

P = 128
D = 1024
KD = D // P
CTX, LAT = 128, 512
T = CTX + LAT
NT = T // P
HALF = T // 2
DEPTH = 2
AD = 512
KA = AD // P
TAPS = 31
PAD = TAPS // 2
GLU = PAD + CTX + PAD + LAT + PAD
CONV = GLU - 2 * PAD
FF = 2816
KF = FF // P
EPS = 1e-6
GN_EPS = 64e-5
HD = 64
HP = 4
C = 64
NC = T // C
NCC = CTX // C
HEADS = 8
FFU = 1 + CTX + 1 + LAT + 1
SLOT = KF * P
E_HALF = float(np.exp(-0.5))
CUTS = [(0, CTX, 0), (CTX, HALF, 1), (HALF, T, 1)]
GROUPS = [(0, CTX, 0), (CTX, T, 1)]

PAR = {}


def _fields():
    at = 0
    for name, n in [("norm1", DEPTH * KD), ("norm2", DEPTH * KD), ("final", KD), ("mod_b", DEPTH * 48),
                    ("conv_w", DEPTH * 3 * 2 * KF), ("conv_b", DEPTH * 2 * KF), ("b_w", TAPS * KA), ("b_b", KA),
                    ("b_norm", KA), ("mu_r", KA), ("mu_k", KA), ("mu_v", KA), ("mu_w", KD), ("mu_a", KD),
                    ("mu_g", KD), ("w0", 2 * KA), ("a0", 2 * KA), ("k_k", KA), ("k_a", KA), ("r_k", KA),
                    ("ln_g", KA), ("ln_b", KA), ("qk_g", KA + 2)]:
        PAR[name] = at
        at += n
    return at


NPAR = _fields()
CONST = {"ident": 0, "ones": P, "head_ones": 2 * P, "rope_perm": 3 * P, "masks": 4 * P}
LEVELS = 6
ARENA = 36480
SCAN_STEPS = 48
SCAN_POOL = 18


class Steps:

    def __init__(self, eng, sem):
        self.eng, self.sem, self.n, self.turn = eng, sem, 0, None

    def __call__(self, ins):
        ins.then_inc(self.sem, 1)
        self.n += 1
        return ins

    def loop(self, i, per):
        self.turn, self.first, self.per = i, self.n, per

    def end(self, turns):
        assert self.n - self.first == self.per, (self.n - self.first, self.per)
        self.n, self.turn = self.first + self.per * turns, None

    def wait(self, but=0):
        if self.turn is None:
            self.eng.wait_ge(self.sem, self.n - but)
        else:
            self.eng.wait_ge(self.sem, self.turn * self.per + self.n - but)


def build(nc, io, stop=99):
    ctx = ExitStack()
    with ctx:
        def sb(name, shape, dt=F32):
            return ctx.enter_context(nc.sbuf_tensor(name, shape, dt))

        def sem(name):
            return ctx.enter_context(nc.semaphore(name))

        x = sb("x", [P, KD, T])
        par = sb("par", [P, NPAR])
        const = sb("const", [P, io["const"].shape[1]])
        mod = sb("mod", [P, 48, 2])
        amul = sb("amul", [P, 2, KD, 2])
        cvec = sb("cvec", [P, KD, 2])
        eps_c = sb("eps_c", [P, 4])
        wslot = sb("wslot", [P, 2, SLOT])
        rs = sb("rs", [P, T])
        arena = sb("arena", [P, ARENA])
        mask01 = sb("mask01", [P, T])
        ps = ctx.enter_context(nc.psum_tensor("ps", [P, 8, 512], F32))

        ident = const[:, 0:P]
        ones = const[:, P:2 * P]
        head_ones = const[:, 2 * P:3 * P]

        def pcol(name, n=0):
            return par[:, PAR[name] + n:PAR[name] + n + 1]

        def region(at, *shape):
            n = int(np.prod(shape))
            assert at + n <= ARENA, (at, n)
            v = arena[:, at:at + n]
            if len(shape) == 2:
                v = v.rearrange("p (a b) -> p a b", a=shape[0])
            if len(shape) == 3:
                v = v.rearrange("p (a b c) -> p a b c", a=shape[0], b=shape[1])
            return v

        def pair(s):
            return ps[:, 2 * s:2 * s + 2, 0:HALF]

        def cut(s, a, b):
            return ps[:, 2 * s + a // HALF, a % HALF:a % HALF + b - a]

        gate = sem("gate")
        loaded = sem("loaded")
        w_in = [sem("w_in0"), sem("w_in1")]
        product = sem("product")
        drained = [sem("drained0"), sem("drained1")]
        act_step, dve_step, pool_step = sem("act_step"), sem("dve_step"), sem("pool_step")
        out_done = sem("out_done")

        tiles = []

        def stream(dram, first, n, cols):
            base = sum(t[2] for t in tiles) // 2
            tiles.append((dram, first, n, cols))
            return base

        def take(pe, base, i, s):
            pe.wait_ge(w_in[s], i * 16 + 16 * (base + 1))
            pe.wait_ge(drained[s], i + base + 1)

        def have(eng, base, i, s):
            eng.wait_ge(product, i * 2 + 2 * base + s + 1)

        def project_pe(pe, base, n, k, src):
            with pe.Fori(0, n // 2) as i:
                for s in range(2):
                    take(pe, base, i, s)
                    w = wslot[:, s, 0:k * P].rearrange("p (k m) -> p k m", k=k)
                    for h in range(2):
                        for kk in range(k):
                            last = nc.tensor.matmul(ps[:, 2 * s + h, 0:HALF], w[:, kk, :],
                                                    src[:, kk, h * HALF:(h + 1) * HALF],
                                                    start=(kk == 0), stop=(kk == k - 1))
                    last.then_inc(product, 1)

        h = region(0, KD, T)
        sq = region(5120, KD, T)
        u = region(10240, KA, T)
        vtm = region(12800, NT, AD)
        glu = region(15360, KA, GLU)
        conv = region(18100, KA, CONV)
        ycat = region(20720, KD, T)
        wsT = region(25840, 4, P)
        vrow = region(26352, 2, AD)
        bsrow = region(27376, 4, T)
        sg = region(29936, T)
        lnst = region(30576, NT, 6)
        lnmv = region(30606, NT, 2)
        hid = region(5120, KF, T)
        up = region(19200, 2, FFU)
        yv = region(20486, 2, FFU - 2)
        sil = region(21768, FFU - 2)
        mrow = region(5120, 48 * P)

        mod_base = [None] * DEPTH

        def modulation_tiles(layer):
            mod_base[layer] = stream(io["mod_w"], 24 * layer, 24, KD * 256)

        def modulation_pe(pe, layer):
            with pe.Fori(0, 12) as i:
                for s in range(2):
                    take(pe, mod_base[layer], i, s)
                    w = wslot[:, s, 0:KD * 256].rearrange("p (k m) -> p k m", k=KD)
                    for k in range(KD):
                        last = nc.tensor.matmul(ps[0:2, 2 * s, 0:256], cvec[:, k, :], w[:, k, :],
                                                start=(k == 0), stop=(k == KD - 1))
                    last.then_inc(product, 1)
            pe.wait_ge(mrow_ready, layer + 1)
            for j in range(48):
                last = nc.tensor.transpose(ps[:, 4, 2 * j:2 * j + 2], mrow[0:2, j * P:(j + 1) * P], ident[0:2, 0:2])
            last.then_inc(mcol_ready, 1)

        def modulation_act(act, st, layer):
            with act.Fori(0, 12) as i:
                for s in range(2):
                    have(act, mod_base[layer], i, s)
                    nc.scalar.activation(mrow[0:2, bass.ds(i * 512 + s * 256, 256)], ps[0:2, 2 * s, 0:256],
                                         ACT.Copy).then_inc(drained[s], 1)
            act.drain().then_inc(mrow_ready, 1)

        def modulation_dve(dve, st, layer):
            dve.wait_ge(mcol_ready, layer + 1)
            cols = ps[:, 4, 0:96].rearrange("p (j v) -> p j v", v=2)
            bias = par[:, PAR["mod_b"] + 48 * layer:PAR["mod_b"] + 48 * (layer + 1)]
            for v in range(2):
                st(nc.vector.tensor_tensor(mod[:, :, v], cols[:, :, v], bias, ALU.add))
            st.wait()
            for n, (name, at) in enumerate([("norm1", KD), ("norm2", 4 * KD)]):
                g = par[:, PAR[name] + KD * layer:PAR[name] + KD * (layer + 1)]
                for v in range(2):
                    st(nc.vector.scalar_tensor_tensor(out=amul[:, n, :, v], in0=mod[:, at:at + KD, v], scalar=1.0,
                                                      in1=g, op0=ALU.add, op1=ALU.mult))

        silu_ready, eps_ready = sem("silu_ready"), sem("eps_ready")
        mrow_ready, mcol_ready = sem("mrow_ready"), sem("mcol_ready")

        sq_ready, sum_ready, root_ready, rs_ready = sem("sq_ready"), sem("sum_ready"), sem("root_ready"), sem("rs_ready")
        xn_ready = sem("xn_ready")

        def rms_act(act, turn, squares, n, eps):
            for o, a in squares:
                last = nc.scalar.activation(o, a, ACT.Square)
            last.then_inc(sq_ready, 1)
            act.wait_ge(sum_ready, turn + 1)
            nc.scalar.activation(rs[:, :].rearrange("p (a b) -> p a b", a=2), pair(2), ACT.Sqrt, bias=eps_c[:, eps:eps + 1],
                                 scale=1.0 / (n * P)).then_inc(root_ready, 1)

        def rms_pe(pe, turn, n):
            pe.wait_ge(sq_ready, turn + 1)
            for hh in range(2):
                for k in range(n):
                    last = nc.tensor.matmul(ps[:, 4 + hh, 0:HALF], ones, sq[:, k, hh * HALF:(hh + 1) * HALF],
                                            start=(k == 0), stop=(k == n - 1))
            last.then_inc(sum_ready, 1)

        def rms_dve(dve, st, turn):
            dve.wait_ge(root_ready, turn + 1)
            st(nc.vector.reciprocal(rs[:, :], rs[:, :]))
            st.wait()

        def adaln_act(act, st, turn, xn, n):
            rms_act(act, turn, [(sq[:, k, :], x[:, k, :]) for k in range(KD)], KD, 0)
            for k in range(KD):
                act.wait_ge(xn_ready, KD * xn + k + 1)
                for a, b, v in GROUPS:
                    nc.scalar.activation(h[:, k, a:b], h[:, k, a:b], ACT.Identity, scale=amul[:, n, k, v:v + 1],
                                         bias=mod[:, 3 * KD * n + k, v:v + 1])

        def adaln_dve(dve, st, turn, xn):
            rms_dve(dve, st, turn)
            for k in range(KD):
                nc.vector.tensor_tensor(h[:, k, :], x[:, k, :], rs[:, :], ALU.mult).then_inc(xn_ready, 1)

        def residual_dve(dve, base, at):
            with dve.Fori(0, KD // 2) as i:
                for s in range(2):
                    have(dve, base, i, s)
                    for n, (a, b, v) in enumerate(CUTS):
                        last = nc.vector.scalar_tensor_tensor(
                            out=x[:, i * 2 + s, a:b], in0=cut(s, a, b), scalar=mod[:, i * 2 + (at + s), v:v + 1],
                            in1=x[:, i * 2 + s, a:b], op0=ALU.mult, op1=ALU.add)
                    last.then_inc(drained[s], 1)

        sg_ready, sg_used = sem("sg_ready"), sem("sg_used")
        vtm_ready, vmul_ready, vln_ready, std_ready = sem("vtm_ready"), sem("vmul_ready"), sem("vln_ready"), sem("std_ready")
        var_ready, glu_ready, conv_ready, mix_ready = sem("var_ready"), sem("glu_ready"), sem("conv_ready"), sem("mix_ready")
        mix_used, yn_ready, pads_ready, u_ready = sem("mix_used"), sem("yn_ready"), sem("pads_ready"), sem("u_ready")
        ab = {}

        def ab_tiles():
            ab["v"] = stream(io["ab_v"], 0, 2, KD * 256)
            ab["glu"] = stream(io["ab_w"], 0, 8, KD * P)
            ab["u"] = stream(io["ab_w"], 8, 4, KD * P)
            ab["out"] = stream(io["w_out"], 0, KD, KD * P)

        def ab_pe(pe):
            for s in range(2):
                pe.wait_ge(w_in[s], 16 * (ab["v"] + 1))
                w = wslot[:, s, 0:KD * 256].rearrange("p (k m) -> p k m", k=KD)
                for t in range(NT):
                    for k in range(KD):
                        last = nc.tensor.matmul(ps[:, 3 + t, s * 256:(s + 1) * 256], h[:, k, t * P:(t + 1) * P], w[:, k, :],
                                                start=(k == 0), stop=(k == KD - 1), skip_group_check=True)
                last.then_inc(product, 1)
            pe.sem_inc(drained[0], 1)
            pe.sem_inc(drained[1], 1)
            pe.wait_ge(vtm_ready, NT)
            project_pe(pe, ab["glu"], 8, KD, h)
            project_pe(pe, ab["u"], 4, KD, h)
            pe.wait_ge(vln_ready, NT)
            for g in range(4):
                if g >= 2:
                    pe.wait_ge(mix_used, g - 1)
                for t in range(NT):
                    at = (4 + 2 * (g % 2)) * 512 + t * P
                    last = nc.tensor.matmul(ps[:, at // 512, at % 512:at % 512 + P], vtm[:, t, g * P:(g + 1) * P],
                                            wsT[:, g, :], start=True, stop=True)
                last.then_inc(mix_ready, 1)

        def ab_act(act, st):
            for t in range(NT):
                if t == 0:
                    act.wait_ge(product, 2 * ab["v"] + 2)
                nc.scalar.activation(vtm[:, t, :], ps[:, 3 + t, :], ACT.Gelu_apprx_tanh).then_inc(vtm_ready, 1)
            act.wait_ge(var_ready, 1)
            nc.scalar.activation(lnmv[:, :, 1], lnmv[:, :, 1], ACT.Sqrt, bias=eps_c[:, 0:1]).then_inc(std_ready, 1)
            with act.Fori(0, 4) as i:
                have(act, ab["glu"], i, 0)
                act.wait_ge(sg_used, i + 1)
                nc.scalar.activation(sg.rearrange("p (a b) -> p a b", a=2), pair(0), ACT.Sigmoid).then_inc(sg_ready, 1)
            with act.Fori(0, 2) as i:
                for s in range(2):
                    have(act, ab["u"], i, s)
                    nc.scalar.activation(u[:, i * 2 + s, :].rearrange("p (a b) -> p a b", a=2), pair(s),
                                         ACT.Gelu_apprx_tanh).then_inc(drained[s], 1)
            act.drain().then_inc(u_ready, 1)

        def ab_dve(dve, st):
            dve.sem_inc(sg_used, 1)
            for t in range(NT):
                dve.wait_ge(vtm_ready, t + 1)
                st(nc.vector.bn_stats(lnst[:, t, :], vtm[:, t, :]))
            st.wait()
            for t in range(NT):
                last = st(nc.vector.bn_aggr(lnmv[:, t, :], lnst[:, t, :]))
            st.wait()
            dve.sem_inc(var_ready, 1)
            dve.wait_ge(std_ready, 1)
            st(nc.vector.reciprocal(lnmv[:, :, 1], lnmv[:, :, 1]))
            st.wait()
            for t in range(NT):
                nc.vector.tensor_scalar(vtm[:, t, :], vtm[:, t, :], lnmv[:, t, 0:1], lnmv[:, t, 1:2], ALU.subtract,
                                        ALU.mult).then_inc(vmul_ready, 1)
            dve.wait_ge(pads_ready, 1)
            with dve.Fori(0, 4) as i:
                have(dve, ab["glu"], i, 1)
                dve.wait_ge(sg_ready, i + 1)
                for a, b, v in CUTS:
                    o = PAD + a + PAD * v
                    last = nc.vector.tensor_tensor(glu[:, i, o:o + b - a], cut(1, a, b), sg[:, a:b], ALU.mult)
                last.then_inc(glu_ready, 1)
                dve.wait_ge(glu_ready, i + 1)
                dve.sem_inc(drained[0], 1)
                dve.sem_inc(drained[1], 1)
                dve.sem_inc(sg_used, 1)
            for k in range(KA):
                st(nc.vector.tensor_scalar(conv[:, k, :], glu[:, k, 0:CONV], pcol("b_w", k), pcol("b_b", k), ALU.mult,
                                           ALU.add))
            with dve.Fori(0, TAPS - 1) as i:
                st.loop(i, KA)
                for k in range(KA):
                    st.wait(but=KA - 1)
                    st(nc.vector.scalar_tensor_tensor(
                        out=conv[:, k, :], in0=glu[:, k, bass.ds(i + 1, CONV)],
                        scalar=par[:, bass.ds(i * KA + (PAR["b_w"] + KA + k), 1)], in1=conv[:, k, :], op0=ALU.mult, op1=ALU.add))
                st.end(TAPS - 1)
            st.wait()
            dve.sem_inc(conv_ready, 1)
            dve.wait_ge(u_ready, 1)
            for g in range(4):
                dve.wait_ge(mix_ready, g + 1)
                mixed = ps[:, 4 + 2 * (g % 2):6 + 2 * (g % 2), :].rearrange("p a b -> p (a b)")[:, 0:T]
                st(nc.vector.tensor_tensor(ycat[:, g, :], mixed, bsrow[:, g, :], ALU.add))
                st.wait()
                dve.sem_inc(mix_used, 1)
                st(nc.vector.tensor_tensor(ycat[:, g, :], ycat[:, g, :], u[:, g, :], ALU.mult))

        def ab_pool(pool, st):
            pool.memset(glu[:, :, :], 0.0).then_inc(pads_ready, 1)
            for t in range(NT):
                pool.wait_ge(vmul_ready, t + 1)
                st(pool.tensor_tensor(vtm[:, t, :], vtm[:, t, :], vrow[:, 0, :], ALU.mult))
                st.wait()
                pool.tensor_tensor(vtm[:, t, :], vtm[:, t, :], vrow[:, 1, :], ALU.add).then_inc(vln_ready, 1)

        def yb_act(act, st, turn):
            act.wait_ge(conv_ready, 1)
            rms_act(act, turn, [(sq[:, k, a:b], conv[:, k, a + PAD * v:b + PAD * v]) for k in range(KA)
                                for a, b, v in GROUPS], KA, 0)
            for k in range(KA):
                act.wait_ge(yn_ready, k + 1)
                nc.scalar.activation(ycat[:, KA + k, :], ycat[:, KA + k, :], ACT.Silu, scale=pcol("b_norm", k))

        def yb_dve(dve, st, turn):
            rms_dve(dve, st, turn)
            for k in range(KA):
                for a, b, v in GROUPS:
                    last = nc.vector.tensor_tensor(ycat[:, KA + k, a:b], conv[:, k, a + PAD * v:b + PAD * v], rs[:, a:b], ALU.mult)
                last.then_inc(yn_ready, 1)

        up_ready, mid_ready, tap_ready, sil_ready = sem("up_ready"), sem("mid_ready"), sem("tap_ready"), sem("sil_ready")
        hid_ready = sem("hid_ready")
        ffn = {}

        def ffn_tiles(layer):
            ffn[layer, "up"] = stream(io["ffn_up"], 2 * KF * layer, 2 * KF, KD * P)
            ffn[layer, "down"] = stream(io["ffn_down"], KD * layer, KD, KF * P)

        def ffn_act(act, st, layer):
            base, n0 = ffn[layer, "up"], KF * layer
            cw, cb = PAR["conv_w"] + 6 * KF * layer, PAR["conv_b"] + 2 * KF * layer
            with act.Fori(0, KF) as i:
                for s in range(2):
                    have(act, base, i, s)
                    act.wait_ge(hid_ready, i + (n0 + 1))
                    for a, b, v in CUTS:
                        last = nc.scalar.activation(up[:, s, 1 + a + v:1 + b + v], cut(s, a, b), ACT.Copy)
                    if s == 0:
                        st.loop(i, 2)
                    st(last)
                    st.wait()
                    act.sem_inc(drained[s], 1)
                    nc.scalar.activation(yv[:, s, :], up[:, s, 1:FFU - 1], ACT.Identity,
                                         scale=par[:, bass.ds(i + (cw + 2 * KF + s * KF), 1)],
                                         bias=par[:, bass.ds(i + (cb + s * KF), 1)]).then_inc(mid_ready, 1)
                act.wait_ge(tap_ready, i * 2 + 2 * n0 + 1)
                nc.scalar.activation(sil, yv[:, 0, :], ACT.Silu).then_inc(sil_ready, 1)
                st.end(KF)

        def ffn_dve(dve, st, layer):
            base, n0 = ffn[layer, "up"], KF * layer
            cw = PAR["conv_w"] + 6 * KF * layer
            if layer == 0:
                dve.sem_inc(hid_ready, 1)
            with dve.Fori(0, KF) as i:
                st.loop(i, 2)
                for s in range(2):
                    dve.wait_ge(mid_ready, i * 2 + 2 * n0 + s + 1)
                    st(nc.vector.scalar_tensor_tensor(out=yv[:, s, :], in0=up[:, s, 0:FFU - 2],
                                                      scalar=par[:, bass.ds(i + (cw + s * KF), 1)], in1=yv[:, s, :],
                                                      op0=ALU.mult, op1=ALU.add))
                    st.wait()
                    nc.vector.scalar_tensor_tensor(out=yv[:, s, :], in0=up[:, s, 2:FFU],
                                                   scalar=par[:, bass.ds(i + (cw + 4 * KF + s * KF), 1)], in1=yv[:, s, :],
                                                   op0=ALU.mult, op1=ALU.add).then_inc(tap_ready, 1)
                st.end(KF)
                dve.wait_ge(sil_ready, i + (n0 + 1))
                dve.wait_ge(tap_ready, i * 2 + 2 * n0 + 2)
                for a, b, v in GROUPS:
                    last = nc.vector.tensor_tensor(hid[:, i, a:b], sil[:, a + v:b + v], yv[:, 1, a + v:b + v], ALU.mult)
                last.then_inc(hid_ready, 1)

        def ffn_pool(pool, layer):
            for at in (0, 1 + CTX, FFU - 1):
                last = pool.memset(up[:, :, at:at + 1], 0.0)


        rkvq = region(5120, 18, T)
        rkv, qk = rkvq[:, 0:12, :], rkvq[:, 12:18, :]
        dh = region(16640, KD, T)
        ycat1 = region(0, KD, T)
        xmix = [region(21760, KD, T), region(26880, KD, T)]
        lw, la, lg = region(32000, T), region(32640, T), region(33280, T)
        vd = region(33920, NT, P)
        ck = region(34560, 2, P)
        cv = region(34816, P)
        rope = region(16640, 2, LAT)
        hsq = region(17664, T)
        rtmp = region(18304, LAT)
        shift = region(26300, KA, T)
        prob = region(18944, 2, T)
        probT = region(20224, 2, NT, LAT)
        probC = region(25344, 2, P)
        qs = region(25600, T)
        srow = region(26240, 2, 3)
        kk = region(12800, KA, T)
        U_AT = [15360 + 1280 * n for n in range(13)] + [33920, 35200]
        mats = {n: region(U_AT[j], NC, P) for n, j in
                (("A", 0), ("B", 1), ("K", 2), ("R", 3), ("Bb", 4), ("Kb", 5), ("Vb", 6), ("At", 7), ("Bt", 8),
                 ("Kt", 9), ("Vt", 10), ("MT", 4), ("PT", 5), ("NT", 6), ("QT", 11), ("X", 12), ("XT", 13), ("Y", 14),
                 ("AH", 0), ("NV", 1), ("UV", 2))}
        tmps = [region(U_AT[11], T), region(U_AT[11] + T, T), region(U_AT[12], T), region(U_AT[12] + T, T),
                region(U_AT[13], T), region(U_AT[13] + T, T), region(U_AT[14], T), region(U_AT[14] + T, T)]
        spare = wslot[:, 0, KD * P:SLOT]
        bacc = spare[:, 0:T]
        stage = spare[:, T:T + 384]
        state = spare[:, T + 384:T + 896].rearrange("p (g b m) -> p g b m", g=2, b=2)
        ubuf = spare[:, T + 896:T + 1152].rearrange("p (b m) -> p b m", b=2)
        gend = sb("gend", [P, NC])
        halves = sb("halves", [P, 2, 2 * KA])

        cd = {}
        xmix_ready, mix_done, lora_ready, vd_ready = sem("xmix_ready"), sem("mix_done"), sem("lora_ready"), sem("vd_ready")

        def cd_tiles():
            cd["in"] = stream(io["cd_w"], 0, 18, KD * P)
            cd["lora"] = stream(io["cd_w"], 18, 4, KD * P)
            cd["out"] = stream(io["w_out"], KD, KD, KD * P)

        def cd_pe(pe):
            project_pe(pe, cd["in"], 18, KD, h)
            for j, (i, s) in enumerate([(0, 0), (0, 1), (1, 0)]):
                pe.wait_ge(xmix_ready, j + 1)
                take(pe, cd["lora"], i, s)
                w = wslot[:, s, 0:KD * P].rearrange("p (k m) -> p k m", k=KD)
                for hh in range(2):
                    for k in range(KD):
                        last = nc.tensor.matmul(ps[:, 2 * s + hh, 0:HALF], w[:, k, :],
                                                xmix[j % 2][:, k, hh * HALF:(hh + 1) * HALF], start=(k == 0), stop=(k == KD - 1))
                last.then_inc(product, 1)
            pe.wait_ge(w_in[1], 16 * (cd["lora"] + 2))
            w = wslot[:, 1, 0:KD * P].rearrange("p (k m) -> p k m", k=KD)
            for t in range(NT):
                for k in range(KD):
                    last = nc.tensor.matmul(ps[:, 4 + t // 4, t % 4 * P:(t % 4 + 1) * P], h[:, k, t * P:(t + 1) * P],
                                            w[:, k, :], start=(k == 0), stop=(k == KD - 1))
            last.then_inc(product, 1)
            pe.sem_inc(drained[1], 1)

        def cd_act(act):
            with act.Fori(0, 9) as i:
                for s in range(2):
                    have(act, cd["in"], i, s)
                    nc.scalar.activation(rkvq[:, i * 2 + s, :].rearrange("p (a b) -> p a b", a=2), pair(s),
                                         ACT.Copy).then_inc(drained[s], 1)
            for i, s, dst, f in ((0, 0, lw, ACT.Tanh), (0, 1, la, ACT.Copy), (1, 0, lg, ACT.Sigmoid)):
                have(act, cd["lora"], i, s)
                nc.scalar.activation(dst.rearrange("p (a b) -> p a b", a=2), pair(s), f).then_inc(drained[s], 1)
            have(act, cd["lora"], 1, 1)
            nc.scalar.activation(vd.rearrange("p t m -> p (t m)"),
                                 ps[:, 4:6, :].rearrange("p a b -> p (a b)")[:, 0:T], ACT.Copy).then_inc(vd_ready, 1)

        def shift_sum(dve, st, out, a):
            n = a.shape[1]
            st(nc.vector.tensor_tensor(out[:, :, 1:T - 1], a[:, :, 0:T - 2], a[:, :, 2:T], ALU.add))
            st.wait()
            for c in range(n):
                st(nc.vector.tensor_copy(out[:, c, 0:CTX + 1:CTX], a[:, c, 1:CTX + 2:CTX]))
                st(nc.vector.tensor_copy(out[:, c, CTX - 1:T:LAT], a[:, c, CTX - 2:T - 1:LAT]))
            st.wait()

        def cd_dve(dve, st):
            shift_sum(dve, st, dh, h)
            st(nc.vector.scalar_tensor_tensor(out=dh[:, :, :], in0=dh[:, :, :], scalar=0.5, in1=h[:, :, :], op0=ALU.mult,
                                              op1=ALU.subtract))
            st.wait()
            for j, mu in enumerate(("mu_w", "mu_a", "mu_g")):
                if j == 2:
                    dve.wait_ge(product, 2 * cd["lora"] + 1)
                for k in range(KD):
                    last = nc.vector.scalar_tensor_tensor(out=xmix[j % 2][:, k, :], in0=dh[:, k, :], scalar=pcol(mu, k),
                                                          in1=h[:, k, :], op0=ALU.mult, op1=ALU.add)
                last.then_inc(xmix_ready, 1)
            for n, name in enumerate(("w0", "a0")):
                st(nc.vector.tensor_scalar(halves[:, n, :], par[:, PAR[name]:PAR[name] + 2 * KA], 0.5, None, ALU.mult))

        hsq_ready, hsum_ready, hroot_ready, qn_ready, perm_ready, shifted = (
            sem("hsq_ready"), sem("hsum_ready"), sem("hroot_ready"), sem("qn_ready"), sem("perm_ready"), sem("shifted"))
        NQ = KA + 2

        def qk_act(act):
            act.dma_start(rope, io["rope"]).then_inc(loaded, 16)
            with act.Fori(0, NQ) as i:
                act.wait_ge(qn_ready, i + 1)
                nc.scalar.activation(hsq, qk[:, i, :], ACT.Square).then_inc(hsq_ready, 1)
                act.wait_ge(hsum_ready, i + 1)
                nc.scalar.activation(rs[:, :].rearrange("p (a b) -> p a b", a=2), pair(0), ACT.Sqrt, bias=eps_c[:, 0:1],
                                     scale=1.0 / HD).then_inc(hroot_ready, 1)

        def head_sums(pe, src, to):
            for hh in range(2):
                last = nc.tensor.matmul(ps[:, 2 * to + hh, 0:HALF], head_ones, src[:, hh * HALF:(hh + 1) * HALF],
                                        start=True, stop=True)
            return last

        def qk_pe(pe):
            with pe.Fori(0, NQ) as i:
                pe.wait_ge(hsq_ready, i + 1)
                head_sums(pe, hsq, 0).then_inc(hsum_ready, 1)
                pe.wait_ge(qn_ready, i + 2)
                nc.tensor.matmul(ps[:, 2, 0:LAT], const[:, 3 * P:4 * P], qk[:, i, CTX:T], start=True,
                                 stop=True).then_inc(perm_ready, 1)

        def qk_dve(dve, st):
            dve.sem_inc(qn_ready, 1)
            dve.wait_ge(loaded, 16 * (LOADS + 1))
            with dve.Fori(0, NQ) as i:
                st.loop(i, 4)
                dve.wait_ge(hroot_ready, i + 1)
                st(nc.vector.reciprocal(rs[:, :], rs[:, :]))
                st.wait()
                nc.vector.scalar_tensor_tensor(out=qk[:, i, :], in0=qk[:, i, :], scalar=par[:, bass.ds(i + PAR["qk_g"], 1)],
                                               in1=rs[:, :], op0=ALU.mult, op1=ALU.mult).then_inc(qn_ready, 1)
                dve.wait_ge(perm_ready, i + 1)
                st(nc.vector.tensor_tensor(rtmp, ps[:, 2, 0:LAT], rope[:, 1, :], ALU.mult))
                st(nc.vector.tensor_tensor(qk[:, i, CTX:T], qk[:, i, CTX:T], rope[:, 0, :], ALU.mult))
                st.wait()
                st(nc.vector.tensor_tensor(qk[:, i, CTX:T], qk[:, i, CTX:T], rtmp, ALU.add))
                st.end(NQ)
            for j, mu in enumerate(("mu_r", "mu_k", "mu_v")):
                a = rkv[:, KA * j:KA * (j + 1), :]
                shift_sum(dve, st, shift, a)
                st(nc.vector.scalar_tensor_tensor(out=shift[:, :, :], in0=shift[:, :, :], scalar=0.5, in1=a, op0=ALU.mult,
                                                  op1=ALU.subtract))
                st.wait()
                for k in range(KA):
                    st(nc.vector.scalar_tensor_tensor(out=rkv[:, KA * j + k, :], in0=shift[:, k, :], scalar=pcol(mu, k),
                                                      in1=rkv[:, KA * j + k, :], op0=ALU.mult, op1=ALU.add))
                st.wait()

        qs_ready, qs_used, s_ready, max_ready, p_ready = (
            sem("qs_ready"), sem("qs_used"), sem("s_ready"), sem("max_ready"), sem("p_ready"))
        e_ready, pT_ready, pTs_ready, o_ready, o_used = (
            sem("e_ready"), sem("pT_ready"), sem("pTs_ready"), sem("o_ready"), sem("o_used"))
        UNITS = 2 * NT
        UNIT = [(e, t) for e in range(2) for t in range(NT)]

        def attn_pe(pe):
            pe.sem_inc(o_ready, 1)
            for g in range(2):
                with pe.Fori(0, 2) as j:
                    def score(n):
                        e, t = UNIT[n]
                        rows = slice(HD * e, HD * e + HD)
                        pe.wait_ge(e_ready, j * UNITS + (2 * g * UNITS + n - 2 + 2 + 1))
                        q = qs[rows, t * P:(t + 1) * P]
                        b = 2 * (n % 2)
                        if t == 0:
                            last = nc.tensor.matmul(ps[:, b, 0:CTX], q, qk[rows, KA + g, 0:CTX], start=True, stop=True)
                        else:
                            nc.tensor.matmul(ps[:, b, :], q, qk[rows, KA + g, CTX:T], start=True, stop=True)
                            last = nc.tensor.matmul(ps[:, b + 1, 0:P], q, ck[rows, g, :], start=True, stop=True)
                        last.then_inc(s_ready, 1)

                    def turn(n):
                        e, t = UNIT[n]
                        pe.wait_ge(p_ready, j * UNITS + (2 * g * UNITS + n + 1))
                        pe.wait_ge(pTs_ready, j * UNITS + (2 * g * UNITS + n + 1))
                        for b in range(1 if t == 0 else NT):
                            last = nc.tensor.transpose(ps[:, 4 + b // 4, b % 4 * P:(b % 4 + 1) * P],
                                                       prob[:, n % 2, b * P:(b + 1) * P], ident)
                        last.then_inc(pT_ready, 1)

                    def output(e):
                        rows = slice(HD * e, HD * e + HD)
                        vcols = slice(HD * g, HD * g + HD)
                        pe.wait_ge(pTs_ready, j * UNITS + (2 * g * UNITS + NT * (e + 1) + 1))
                        pe.wait_ge(o_used, j * 2 + (4 * g + e + 1))
                        nc.tensor.matmul(ps[rows, 7, 0:P], vd[:, 0, vcols], probC[:, e, :], start=True, stop=True)
                        for b in range(NT):
                            v = vd[:, 1 + b, vcols] if b < 4 else cv[:, vcols]
                            last = nc.tensor.matmul(ps[rows, 6, :], v, probT[:, e, b, :], start=(b == 0), stop=(b == NT - 1))
                        last.then_inc(o_ready, 1)

                    pe.wait_ge(qs_ready, j + (2 * g + 1))
                    score(0)
                    for n in range(UNITS):
                        if n + 1 < UNITS:
                            score(n + 1)
                        turn(n)
                        if UNIT[n][1] == NT - 1:
                            output(UNIT[n][0])

        def attn_act(act):
            act.sem_inc(e_ready, 2)
            act.sem_inc(pTs_ready, 1)
            for g in range(2):
                with act.Fori(0, 2) as j:
                    act.wait_ge(o_ready, j * 2 + (4 * g + 1))
                    nc.scalar.activation(qs, qk[:, j + 2 * g, :], ACT.Copy).then_inc(qs_ready, 1)

                    def expo(n):
                        e, t = UNIT[n]
                        act.wait_ge(max_ready, j * UNITS + (2 * g * UNITS + n + 1))
                        if n >= 2:
                            act.wait_ge(pT_ready, j * UNITS + (2 * g * UNITS + n - 1))
                        w = P if t == 0 else T
                        src = ps[:, 2 * (n % 2):2 * (n % 2) + 2, :].rearrange("p a b -> p (a b)")[:, 0:w]
                        nc.scalar.activation(prob[:, n % 2, 0:w], src, ACT.Exp, scale=0.125, bias=srow[:, n % 2, 0:1],
                                             accum_out=srow[:, n % 2, 1:2]).then_inc(e_ready, 1)

                    def copy(n):
                        e, t = UNIT[n]
                        act.wait_ge(pT_ready, j * UNITS + (2 * g * UNITS + n + 1))
                        if t == 0:
                            nc.scalar.activation(probC[:, e, :], ps[:, 4, 0:P], ACT.Copy).then_inc(pTs_ready, 1)
                        else:
                            q = slice((t - 1) * P, t * P)
                            nc.scalar.activation(probT[:, e, :, q], ps[:, 4:6, :].rearrange("p a (b q) -> p (a b) q", q=P)[:, 0:NT, :],
                                                 ACT.Copy).then_inc(pTs_ready, 1)

                    expo(0)
                    for n in range(UNITS):
                        if n + 1 < UNITS:
                            expo(n + 1)
                        copy(n)

        def attn_dve(dve, st):
            dve.sem_inc(o_used, 1)
            for g in range(2):
                with dve.Fori(0, 2) as j:
                    st.loop(j, 2 * UNITS)

                    def biggest(n):
                        e, t = UNIT[n]
                        w = P if t == 0 else T
                        dve.wait_ge(s_ready, j * UNITS + (2 * g * UNITS + n + 1))
                        src = ps[:, 2 * (n % 2):2 * (n % 2) + 2, :].rearrange("p a b -> p (a b)")[:, 0:w]
                        st(nc.vector.tensor_reduce(srow[:, n % 2, 0:1], src, AX.X, ALU.max))
                        st.wait()
                        nc.vector.tensor_scalar(srow[:, n % 2, 0:1], srow[:, n % 2, 0:1], -0.125, None,
                                                ALU.mult).then_inc(max_ready, 1)

                    def norm(n):
                        e, t = UNIT[n]
                        w = P if t == 0 else T
                        dve.wait_ge(e_ready, j * UNITS + (2 * g * UNITS + n + 1 + 2))
                        st(nc.vector.reciprocal(srow[:, n % 2, 2:3], srow[:, n % 2, 1:2]))
                        st.wait()
                        nc.vector.tensor_scalar(prob[:, n % 2, 0:w], prob[:, n % 2, 0:w], srow[:, n % 2, 2:3], None,
                                                ALU.mult).then_inc(p_ready, 1)

                    def out(e):
                        rows = slice(HD * e, HD * e + HD)
                        dve.wait_ge(o_ready, j * 2 + (4 * g + e + 2))
                        nc.vector.tensor_copy(ycat1[rows, j + (KA + 2 * g), 0:CTX], ps[rows, 7, 0:P])
                        nc.vector.tensor_copy(ycat1[rows, j + (KA + 2 * g), CTX:T], ps[rows, 6, :]).then_inc(o_used, 1)

                    biggest(0)
                    for n in range(UNITS):
                        if n + 1 < UNITS:
                            biggest(n + 1)
                        norm(n)
                        if UNIT[n][1] == NT - 1:
                            out(UNIT[n][0])
                    st.end(2)

        kk_ready, ksq_ready, ksum_ready, kroot_ready, kk_done = (
            sem("kk_ready"), sem("ksq_ready"), sem("ksum_ready"), sem("kroot_ready"), sem("kk_done"))

        def kk_act(act):
            with act.Fori(0, KA) as i:
                act.wait_ge(kk_ready, i + 1)
                nc.scalar.activation(hsq, kk[:, i, :], ACT.Square).then_inc(ksq_ready, 1)
                act.wait_ge(ksum_ready, i + 1)
                nc.scalar.activation(rs[:, :].rearrange("p (a b) -> p a b", a=2), pair(0), ACT.Sqrt,
                                     bias=eps_c[:, 2:3]).then_inc(kroot_ready, 1)

        def kk_pe(pe):
            with pe.Fori(0, KA) as i:
                pe.wait_ge(ksq_ready, i + 1)
                head_sums(pe, hsq, 0).then_inc(ksum_ready, 1)

        def kk_dve(dve, st):
            with dve.Fori(0, KA) as i:
                st.loop(i, 2)
                nc.vector.tensor_scalar(kk[:, i, :], rkv[:, i + KA, :], par[:, bass.ds(i + PAR["k_k"], 1)], None,
                                        ALU.mult).then_inc(kk_ready, 1)
                dve.wait_ge(kroot_ready, i + 1)
                st(nc.vector.reciprocal(rs[:, :], rs[:, :]))
                st.wait()
                dve.wait_ge(kk_ready, i + 1)
                st(nc.vector.tensor_tensor(kk[:, i, :], kk[:, i, :], rs[:, :], ALU.mult))
                st.wait()
                st.end(KA)

        def kk_pool(pool):
            pool.memset(mask01[:, :], 1.0).then_inc(kk_done, 1)
            pool.wait_ge(kk_done, 1)
            pool.memset(mask01[:, 0:T:C], 0.0)

        GR = [(0, 4), (4, 8), (8, NC)]
        JOBS = [("At", "act"), ("Bt", "act"), ("Kt", "act"), ("Vt", "act"), ("M", "dve"), ("MT", "dve"), ("NT", "dve"),
                ("PT", "dve"), ("QT", "dve")]
        for l in range(1, LEVELS):
            JOBS += [("Y%d" % l, "dve")] + ([("X%d" % l, "dve")] if l < LEVELS - 1 else []) + [("XT%d" % l, "dve")]
        JOBS += [("AH", "act"), ("NV", "act"), ("UV", "act")]
        NG = len(GR)
        order, counts = {}, {"act": 0, "dve": 0}
        for name, who in JOBS:
            for g in range(NG):
                counts[who] += 1
                order[name, g] = (len(order), who, counts[who])
        by_number = {v[0]: v for v in order.values()}
        SEQ = [[2, 0, 3, 1, 4, 5, 6, 7, 8, 9], [9, 1, 8, 0, 7, 6, 5, 4, 3, 2]]
        evac = {"act": sem("evac_act"), "dve": sem("evac_dve")}
        job_ready, uw_ready, th_ready, scan_ready, exp_ready = (
            sem("job_ready"), sem("uw_ready"), sem("th_ready"), sem("scan_ready"), sem("exp_ready"))
        kd_ready, bd_dve, bd_pool, gend_ready, xt_ready, zero_ready = (
            sem("kd_ready"), sem("bd_dve"), sem("bd_pool"), sem("gend_ready"), sem("xt_ready"), sem("zero_ready"))
        u_made, u_read, s_made, s_read, y_ready, y_read = (
            sem("u_made"), sem("u_read"), sem("s_made"), sem("s_read"), sem("y_ready"), sem("y_read"))
        stage_in, state_in, state_out, hp_done = sem("stage_in"), sem("state_in"), sem("state_out"), sem("hp_done")
        pool_passed = sem("pool_passed")
        gn_pe, gn_act, gn_dve, state_zero = sem("gn_pe"), sem("gn_act"), sem("gn_dve"), sem("state_zero")

        def per_chunk(a):
            return a.rearrange("p (c t) -> p c t", t=C)

        def mask(n, count):
            a = const[:, (4 + n) * P:(5 + n) * P]
            return a.unsqueeze(1).to_broadcast([P, count, P])

        def ids(count):
            return ident.unsqueeze(1).to_broadcast([P, count, P])

        STRICT, INCL, LEVEL = 0, 2, 4

        def scan_bank(name, g):
            n = order[name, g][0]
            a, b = GR[g]
            return ps[:, n % 8, 0:(b - a) * P], ps[:, n % 8, 0:(b - a) * P].rearrange("p (c m) -> p c m", m=P)

        def scan_pe(pe):
            with pe.Fori(0, HP) as i:
                for d in range(2):
                    rows = slice(HD * d, HD * d + HD)
                    if d == 0:
                        pe.wait_ge(stage_in, i * 16 + 16)
                        pe.wait_ge(hp_done, i + 1)
                    else:
                        pe.wait_ge(y_read, i * 2 + 1)
                    for n, src in enumerate((lw, la)):
                        for hh in range(2):
                            last = nc.tensor.matmul(ps[:, 2 * n + hh, 0:HALF], stage[rows, n * P:(n + 1) * P],
                                                    src[rows, hh * HALF:(hh + 1) * HALF], start=True, stop=True)
                    last.then_inc(uw_ready, 1)
                    pe.wait_ge(bd_dve, i * 2 + (d + 1))
                    pe.wait_ge(bd_pool, i * 2 + (d + 1))

                    def have_evac(name, g):
                        _, who, n = order[name, g]
                        pe.wait_ge(evac[who], (i * 2 + d) * counts[who] + n)

                    def job(name, *args, needs=(), xt=False):
                        for g, (a, b) in enumerate(GR):
                            n = order[name, g][0]
                            before = ([by_number[n - 8]] if n >= 8 else []) + [order[need, g] for need in needs]
                            for who in ("act", "dve"):
                                m = max([b[2] for b in before if b[1] == who], default=0)
                                if m:
                                    pe.wait_ge(evac[who], (i * 2 + d) * counts[who] + m)
                            if xt:
                                pe.wait_ge(xt_ready, i * (2 * NG) + (d * NG + g + 1))
                            bank = scan_bank(name, g)[1]
                            for c in range(a, b):
                                if len(args) == 1:
                                    last = nc.tensor.transpose(bank[:, c - a, :], mats[args[0]][:, c, :], ident)
                                else:
                                    last = nc.tensor.matmul(bank[:, c - a, :], mats[args[0]][:, c, :],
                                                            mats[args[1]][:, c, :], start=True, stop=True)
                            last.then_inc(job_ready, 1)

                    job("At", "A")
                    job("Bt", "Bb")
                    job("Kt", "Kb")
                    job("Vt", "Vb")
                    job("M", "A", "B")
                    job("MT", "B", "A")
                    job("NT", "K", "A")
                    job("PT", "B", "R")
                    job("QT", "K", "R")
                    for l in range(1, LEVELS):
                        xs = ["M"] if l == 1 else ["X%d" % (l - 1)]
                        ts = [] if l == 1 else ["XT%d" % (l - 1)]
                        job("Y%d" % l, "MT", "X", needs=xs + ["MT"])
                        if l < LEVELS - 1:
                            job("X%d" % l, "XT", "Y", needs=["Y%d" % l] + ts, xt=l == 1)
                        job("XT%d" % l, "Y", "XT", needs=["Y%d" % l] + ts)
                    job("AH", "At", "XT", needs=["At", "XT%d" % (LEVELS - 1)])
                    job("NV", "NT", "Vt", needs=["NT", "Vt"])
                    job("UV", "XT", "NV", needs=["NV"])
                    have_evac("UV", NG - 1)
                    have_evac("XT%d" % (LEVELS - 1), NG - 1)
                    pe.wait_ge(state_in, i * 32 + 16 * (d + 1))
                    pe.wait_ge(state_zero, i * 2 + (d + 1))
                    step = [0, 0]
                    for q, c in enumerate(SEQ[d]):
                        grp = 1 if c >= NCC else 0
                        cur = state[:, grp, step[grp] % 2, :]
                        if q >= 1:
                            last_q = q - 1 if q > 4 else q - 2
                            if last_q >= 0:
                                pe.wait_ge(s_read, (i * 2 + d) * NC + last_q + 1)
                        nc.tensor.matmul(ps[:, q % 2, 0:P], mats["AH"][:, c, :], cur, start=True, stop=True).then_inc(u_made, 1)
                        pe.wait_ge(u_read, (i * 2 + d) * NC + q + 1)
                        uu = ubuf[:, q % 2, :]
                        nc.tensor.matmul(ps[:, 2 + q % 2, 0:P], mats["Bt"][:, c, :], uu, start=True, stop=False)
                        nc.tensor.matmul(ps[:, 2 + q % 2, 0:P], mats["Kt"][:, c, :], mats["Vt"][:, c, :], start=False,
                                         stop=True).then_inc(s_made, 1)
                        yb = ps[:, 4 + c // 4, c % 4 * P:(c % 4 + 1) * P]
                        nc.tensor.matmul(yb, cur, mats["R"][:, c, :], start=True, stop=False)
                        nc.tensor.matmul(yb, uu, mats["PT"][:, c, :], start=False, stop=False)
                        last = nc.tensor.matmul(yb, mats["Vt"][:, c, :], mats["QT"][:, c, :], start=False, stop=True)
                        step[grp] += 1
                    last.then_inc(y_ready, 1)
                pe.wait_ge(y_read, i * 2 + 2)
                head_sums(pe, bacc, 2)
                for hh in range(2):
                    nc.tensor.matmul(ps[:, 6 + hh, 0:HALF], stage[:, 2 * P:3 * P], lg[:, hh * HALF:(hh + 1) * HALF],
                                     start=True, stop=True)
                for hh in range(2):
                    last = nc.tensor.matmul(ps[:, hh, 0:HALF], head_ones, ycat1[:, i, hh * HALF:(hh + 1) * HALF],
                                            start=True, stop=True)
                last.then_inc(gn_pe, 1)
                pe.wait_ge(gn_act, i * 2 + 1)
                head_sums(pe, tmps[0], 1).then_inc(gn_pe, 1)

        def scan_act(act):
            with act.Fori(0, HP) as i:
                for d in range(2):
                    act.wait_ge(uw_ready, i * 2 + (d + 1))
                    for n in range(2):
                        last = nc.scalar.activation(tmps[n].rearrange("p (a b) -> p a b", a=2), pair(n), ACT.Tanh, scale=0.5,
                                                    bias=halves[:, n, bass.ds(i + KA * d, 1)])
                    last.then_inc(th_ready, 1)
                    act.wait_ge(scan_ready, i * 2 + (d + 1))
                    nc.scalar.activation(tmps[3], tmps[3], ACT.Exp)
                    nc.scalar.activation(tmps[4], tmps[2], ACT.Exp)
                    nc.scalar.activation(tmps[5], tmps[2], ACT.Exp, scale=-1.0).then_inc(exp_ready, 1)
                    for name, who in JOBS:
                        if who != "act":
                            continue
                        for g, (a, b) in enumerate(GR):
                            act.wait_ge(job_ready, (i * 2 + d) * len(order) + order[name, g][0] + 1)
                            nc.scalar.activation(mats[name][:, a:b, :], scan_bank(name, g)[1], ACT.Copy,
                                                 scale=-1.0 if name in ("AH", "UV") else 1.0).then_inc(evac["act"], 1)
                act.wait_ge(gn_dve, i + 1)
                nc.scalar.activation(tmps[0], ycat1[:, i, :], ACT.Square).then_inc(gn_act, 1)
                act.wait_ge(gn_pe, i * 2 + 2)
                nc.scalar.activation(tmps[1].rearrange("p (a b) -> p a b", a=2), pair(1), ACT.Sqrt, bias=eps_c[:, 1:2],
                                     scale=1.0 / HD).then_inc(gn_act, 1)

        def scan_dve(dve, st):
            dve.wait_ge(zero_ready, 1)
            dve.sem_inc(hp_done, 1)
            with dve.Fori(0, HP) as i:
                st.loop(i, SCAN_STEPS)
                r, k = rkv[:, i, :], rkv[:, i + KA, :]
                for d in range(2):
                    w, a, cum, e0, e1, e2, kd, ka = tmps
                    dve.wait_ge(th_ready, i * 2 + (d + 1))
                    st(nc.vector.tensor_scalar(w, w, -0.5 * E_HALF, -0.5 * E_HALF, ALU.mult, ALU.add))
                    st(nc.vector.tensor_scalar(a, a, 0.5, 0.5, ALU.mult, ALU.add))
                    st.wait()
                    way = slice(None, None, 1 if d == 0 else -1)
                    st(nc.vector.tensor_tensor_scan(cum[:, way], mask01[:, :], w[:, way], 0.0, ALU.mult, ALU.add))
                    st.wait()
                    nc.vector.tensor_tensor(e0, cum, w, ALU.subtract).then_inc(scan_ready, 1)
                    st(nc.vector.tensor_scalar(kd, a, 1.0, par[:, bass.ds(i + PAR["k_a"], 1)], ALU.subtract, ALU.mult))
                    st(nc.vector.tensor_tensor(ka, kk[:, i, :], a, ALU.mult))
                    st.wait(but=1)
                    nc.vector.scalar_tensor_tensor(out=kd, in0=kd, scalar=1.0, in1=k, op0=ALU.add,
                                                   op1=ALU.mult).then_inc(kd_ready, 1)
                    dve.wait_ge(kd_ready, i * 2 + (d + 1))
                    dve.wait_ge(scan_ready, i * 2 + (d + 1))
                    if d == 0:
                        st(nc.vector.tensor_tensor(bacc, kd, r, ALU.mult))
                    else:
                        st(nc.vector.tensor_tensor(w, kd, r, ALU.mult))
                        st.wait()
                        st(nc.vector.tensor_tensor(bacc, bacc, w, ALU.add))
                    dve.wait_ge(exp_ready, i * 2 + (d + 1))
                    at = C - 1 if d == 0 else 0
                    st(nc.vector.tensor_copy(gend[:, :], e1[:, at:T:C]))
                    st.wait()
                    dve.sem_inc(gend_ready, 1)
                    for e in range(2):
                        rows = slice(HD * e, HD * e + HD)
                        for m, x0, x1 in (("A", kk[rows, i, :], e0), ("B", ka[rows], e2), ("R", rkv[rows, i, :], e1)):
                            st(nc.vector.tensor_tensor(mats[m][rows, :, rows], per_chunk(x0), per_chunk(x1[rows]), ALU.mult))
                    st.wait()
                    for e in range(2):
                        rows = slice(HD * e, HD * e + HD)
                        st(nc.vector.tensor_tensor(mats["Bb"][rows, :, rows], mats["B"][rows, :, rows],
                                                   gend[rows, :].unsqueeze(2).to_broadcast([HD, NC, C]), ALU.mult))
                    st.wait()
                    dve.sem_inc(bd_dve, 1)
                    for name, who in JOBS:
                        if who != "dve":
                            continue
                        for g, (c0, c1) in enumerate(GR):
                            dve.wait_ge(job_ready, (i * 2 + d) * len(order) + order[name, g][0] + 1)
                            bank, n = scan_bank(name, g)[1], c1 - c0
                            if name == "M":
                                xm = mats["X"][:, c0:c1, :]
                                st(nc.vector.tensor_tensor(xm, bank, mask(LEVEL + d, n), ALU.mult))
                                st.wait()
                                last = nc.vector.tensor_tensor(xm, xm, ids(n), ALU.add)
                            elif name in ("MT", "NT"):
                                last = nc.vector.tensor_tensor(mats[name][:, c0:c1, :], bank, mask(STRICT + d, n), ALU.mult)
                            elif name in ("PT", "QT"):
                                last = nc.vector.tensor_tensor(mats[name][:, c0:c1, :], bank, mask(INCL + d, n), ALU.mult)
                            elif name[0] == "Y":
                                last = nc.vector.tensor_tensor(mats["Y"][:, c0:c1, :], bank,
                                                               mask(LEVEL + 2 * int(name[1]) + d, n), ALU.mult)
                            else:
                                xm = mats[name[:-1]][:, c0:c1, :]
                                last = nc.vector.tensor_tensor(xm, xm, bank, ALU.subtract)
                            last.then_inc(evac["dve"], 1)
                    step = [0, 0]
                    for q, c in enumerate(SEQ[d]):
                        grp = 1 if c >= NCC else 0
                        cur, new = state[:, grp, step[grp] % 2, :], state[:, grp, (step[grp] + 1) % 2, :]
                        dve.wait_ge(u_made, (i * 2 + d) * NC + q + 1)
                        if q == 0:
                            dve.wait_ge(evac["act"], (i * 2 + d + 1) * counts["act"])
                        nc.vector.tensor_tensor(ubuf[:, q % 2, :], ps[:, q % 2, 0:P], mats["UV"][:, c, :],
                                                ALU.add).then_inc(u_read, 1)
                        dve.wait_ge(s_made, (i * 2 + d) * NC + q + 1)
                        if q >= 1:
                            dve.wait_ge(s_read, (i * 2 + d) * NC + q)
                        nc.vector.scalar_tensor_tensor(out=new, in0=cur, scalar=gend[:, c:c + 1], in1=ps[:, 2 + q % 2, 0:P],
                                                       op0=ALU.mult, op1=ALU.add).then_inc(s_read, 1)
                        step[grp] += 1
                    dve.wait_ge(y_ready, i * 2 + (d + 1))
                    ybank = ps[:, 4:7, :].rearrange("p a (c m) -> p (a c) m", m=P)
                    for e in range(2):
                        rows = slice(HD * e, HD * e + HD)
                        yv_ = per_chunk(ycat1[rows, i, :])
                        if d == 0:
                            st(nc.vector.tensor_copy(yv_, ybank[rows, 0:NC, rows]))
                        else:
                            st(nc.vector.tensor_tensor(yv_, yv_, ybank[rows, 0:NC, rows], ALU.add))
                    if d == 1:
                        st(nc.vector.tensor_scalar(bacc, bacc, par[:, bass.ds(i + PAR["r_k"], 1)], None, ALU.mult))
                    st.wait()
                    dve.sem_inc(y_read, 1)
                y = ycat1[:, i, :]
                dve.wait_ge(gn_pe, i * 2 + 1)
                nc.vector.scalar_tensor_tensor(out=y.rearrange("p (a b) -> p a b", a=2), in0=pair(0), scalar=-1.0 / HD,
                                               in1=y.rearrange("p (a b) -> p a b", a=2), op0=ALU.mult,
                                               op1=ALU.add).then_inc(gn_dve, 1)
                t2 = tmps[2].rearrange("p (a b) -> p a b", a=2)
                st(nc.vector.tensor_tensor(t2, rkv[:, i + 2 * KA, :].rearrange("p (a b) -> p a b", a=2), pair(2), ALU.mult))
                dve.wait_ge(gn_act, i * 2 + 2)
                st(nc.vector.reciprocal(tmps[1], tmps[1]))
                st.wait()
                st(nc.vector.tensor_tensor(y, y, tmps[1], ALU.mult))
                st.wait()
                st(nc.vector.tensor_scalar(y, y, par[:, bass.ds(i + PAR["ln_g"], 1)], par[:, bass.ds(i + PAR["ln_b"], 1)],
                                           ALU.mult, ALU.add))
                st.wait()
                st(nc.vector.tensor_tensor(y, y, tmps[2], ALU.add))
                st.wait()
                st(nc.vector.tensor_tensor(y.rearrange("p (a b) -> p a b", a=2), y.rearrange("p (a b) -> p a b", a=2),
                                           pair(3), ALU.mult))
                st.wait()
                dve.sem_inc(hp_done, 1)
                st.end(HP)

        def scan_pool(pool, st):
            st(pool.memset(region(U_AT[0], 7 * NC * P), 0.0))
            st.wait()
            pool.sem_inc(zero_ready, 1)

            def hold():
                pool.sem_inc(pool_passed, 1)

            with pool.Fori(0, HP) as i:
                st.loop(i, SCAN_POOL)
                pool.wait_ge(hp_done, i + 1)
                hold()
                pool.dma_start(stage, io["scan_w"][i]).then_inc(stage_in, 16)
                for d in range(2):
                    if d == 1:
                        pool.wait_ge(y_ready, i * 2 + 1)
                        hold()
                    pool.dma_start(state[:, 1, 0, :], io["state"][i * 2 + d]).then_inc(state_in, 16)
                    if d == 1:
                        pool.wait_ge(state_out, i * 32 + 16)
                        hold()
                    pool.memset(state[:, 0, 0, :], 0.0).then_inc(state_zero, 1)
                    pool.wait_ge(state_zero, i * 2 + (d + 1))
                    hold()
                    for e in range(2):
                        rows = slice(HD * e, HD * e + HD)
                        st(pool.tensor_copy(mats["Vb"][rows, :, rows], per_chunk(rkv[rows, i + 2 * KA, :])))
                        st.wait()
                        hold()
                    pool.wait_ge(kd_ready, i * 2 + (d + 1))
                    pool.wait_ge(exp_ready, i * 2 + (d + 1))
                    pool.wait_ge(gend_ready, i * 2 + (d + 1))
                    for e in range(2):
                        rows = slice(HD * e, HD * e + HD)
                        st(pool.tensor_tensor(mats["K"][rows, :, rows], per_chunk(tmps[6][rows]), per_chunk(tmps[5][rows]),
                                              ALU.mult))
                        st.wait()
                    for e in range(2):
                        rows = slice(HD * e, HD * e + HD)
                        st(pool.tensor_tensor(mats["Kb"][rows, :, rows], mats["K"][rows, :, rows],
                                              gend[rows, :].unsqueeze(2).to_broadcast([HD, NC, C]), ALU.mult))
                        st.wait()
                    pool.sem_inc(bd_pool, 1)
                    for g, (c0, c1) in enumerate(GR):
                        pool.wait_ge(evac["dve"], (i * 2 + d) * counts["dve"] + order["MT", g][2])
                        xt = mats["XT"][:, c0:c1, :]
                        st(pool.tensor_tensor(xt, mats["MT"][:, c0:c1, :], mask(LEVEL + 1 - d, c1 - c0), ALU.mult))
                        st.wait()
                        pool.tensor_tensor(xt, xt, ids(c1 - c0), ALU.add).then_inc(xt_ready, 1)
                    pool.wait_ge(y_ready, i * 2 + (d + 1))
                    pool.wait_ge(s_read, (i * 2 + d + 1) * NC)
                    hold()
                    pool.dma_start(io["new_state"][i * 2 + d], state[:, 0, 0, :]).then_inc(state_out, 16)
                pool.wait_ge(state_out, i * 32 + 32)
                hold()
                st.end(HP)
            pool.wait_ge(state_out, 32 * HP)
        def pass_gate(eng, n):
            eng.drain().then_inc(gate, 1)
            eng.wait_ge(gate, 4 * n)

        LOADS = 9
        modulation_tiles(0)
        ab_tiles()
        ffn_tiles(0)
        modulation_tiles(1)
        cd_tiles()
        ffn_tiles(1)

        y_out = sem("y_out")

        def final_dve(dve, st, turn):
            rms_dve(dve, st, turn)
            for k in range(KD):
                nc.vector.scalar_tensor_tensor(out=h[:, k, :], in0=x[:, k, :], scalar=pcol("final", k), in1=rs[:, :],
                                               op0=ALU.mult, op1=ALU.mult).then_inc(y_out, 1)

        block = ctx.enter_context(nc.Block())

        @block.sync
        def _(sp):
            for name, dst in (("par", par[:, :]), ("const", const[:, :]), ("cvec", cvec[:, :, :]), ("x_fm", x[:, :, :]),
                              ("ws_t", wsT), ("v_rows", vrow), ("bs_rows", bsrow), ("cache_k", ck), ("cache_v", cv)):
                sp.dma_start(dst, io[name]).then_inc(loaded, 16)
            at = 0
            for dram, first, n, cols in tiles:
                if at == 0:
                    for s in range(2):
                        sp.dma_start(wslot[:, s, 0:cols], dram[first + s]).then_inc(w_in[s], 16)
                with sp.Fori(1 if at == 0 else 0, n // 2) as i:
                    for s in range(2):
                        sp.wait_ge(product, i * 2 + (2 * at + s - 1))
                        sp.dma_start(wslot[:, s, 0:cols], dram[i * 2 + (first + s)]).then_inc(w_in[s], 16)
                at += n // 2

        @block.tensor
        def _(pe):
            pe.sem_inc(drained[0], 1)
            pe.sem_inc(drained[1], 1)
            pe.wait_ge(loaded, 16 * LOADS)
            pe.wait_ge(silu_ready, 1)
            modulation_pe(pe, 0)
            pass_gate(pe, 1)
            rms_pe(pe, 0, KD)
            pass_gate(pe, 2)
            ab_pe(pe)
            pass_gate(pe, 3)
            rms_pe(pe, 1, KA)
            pass_gate(pe, 4)
            project_pe(pe, ab["out"], KD, KD, ycat)
            pass_gate(pe, 5)
            rms_pe(pe, 2, KD)
            pass_gate(pe, 6)
            project_pe(pe, ffn[0, "up"], 2 * KF, KD, h)
            pass_gate(pe, 7)
            project_pe(pe, ffn[0, "down"], KD, KF, hid)
            pass_gate(pe, 8)
            modulation_pe(pe, 1)
            pass_gate(pe, 9)
            rms_pe(pe, 3, KD)
            pass_gate(pe, 10)
            cd_pe(pe)
            pass_gate(pe, 11)
            qk_pe(pe)
            pass_gate(pe, 12)
            attn_pe(pe)
            pass_gate(pe, 13)
            kk_pe(pe)
            pass_gate(pe, 14)
            scan_pe(pe)
            pass_gate(pe, 15)
            project_pe(pe, cd["out"], KD, KD, ycat1)
            pass_gate(pe, 16)
            rms_pe(pe, 4, KD)
            pass_gate(pe, 17)
            project_pe(pe, ffn[1, "up"], 2 * KF, KD, h)
            pass_gate(pe, 18)
            project_pe(pe, ffn[1, "down"], KD, KF, hid)
            pass_gate(pe, 19)
            rms_pe(pe, 5, KD)

        @block.scalar
        def _(act):
            st = Steps(act, act_step)
            act.wait_ge(loaded, 16 * LOADS)
            nc.scalar.activation(cvec[:, :, :], cvec[:, :, :], ACT.Silu).then_inc(silu_ready, 1)
            act.wait_ge(eps_ready, 3)
            modulation_act(act, st, 0)
            pass_gate(act, 1)
            adaln_act(act, st, 0, 0, 0)
            pass_gate(act, 2)
            ab_act(act, st)
            pass_gate(act, 3)
            yb_act(act, st, 1)
            pass_gate(act, 4)
            pass_gate(act, 5)
            adaln_act(act, st, 2, 1, 1)
            pass_gate(act, 6)
            ffn_act(act, st, 0)
            pass_gate(act, 7)
            pass_gate(act, 8)
            modulation_act(act, st, 1)
            pass_gate(act, 9)
            adaln_act(act, st, 3, 2, 0)
            pass_gate(act, 10)
            cd_act(act)
            pass_gate(act, 11)
            qk_act(act)
            pass_gate(act, 12)
            act.dma_start(io["new_k"], qk[0:HD, KA:KA + 2, 0:CTX]).then_inc(out_done, 16)
            act.dma_start(io["new_v"], vd[:, 0, :]).then_inc(out_done, 16)
            attn_act(act)
            act.wait_ge(out_done, 32)
            pass_gate(act, 13)
            kk_act(act)
            pass_gate(act, 14)
            scan_act(act)
            pass_gate(act, 15)
            pass_gate(act, 16)
            adaln_act(act, st, 4, 3, 1)
            pass_gate(act, 17)
            ffn_act(act, st, 1)
            pass_gate(act, 18)
            pass_gate(act, 19)
            rms_act(act, 5, [(sq[:, k, :], x[:, k, :]) for k in range(KD)], KD, 0)
            for k in range(KD):
                act.wait_ge(y_out, k + 1)
                act.dma_start(io["y"][:, k, :], h[:, k, :]).then_inc(out_done, 16)
            act.wait_ge(out_done, 16 * (KD + 2))

        @block.vector
        def _(dve):
            st = Steps(dve, dve_step)
            dve.wait_ge(loaded, 16 * LOADS)
            modulation_dve(dve, st, 0)
            pass_gate(dve, 1)
            adaln_dve(dve, st, 0, 0)
            pass_gate(dve, 2)
            ab_dve(dve, st)
            pass_gate(dve, 3)
            yb_dve(dve, st, 1)
            pass_gate(dve, 4)
            residual_dve(dve, ab["out"], 2 * KD)
            pass_gate(dve, 5)
            adaln_dve(dve, st, 2, 1)
            pass_gate(dve, 6)
            ffn_dve(dve, st, 0)
            pass_gate(dve, 7)
            residual_dve(dve, ffn[0, "down"], 5 * KD)
            pass_gate(dve, 8)
            modulation_dve(dve, st, 1)
            pass_gate(dve, 9)
            adaln_dve(dve, st, 3, 2)
            pass_gate(dve, 10)
            cd_dve(dve, st)
            pass_gate(dve, 11)
            qk_dve(dve, st)
            pass_gate(dve, 12)
            attn_dve(dve, st)
            pass_gate(dve, 13)
            kk_dve(dve, st)
            pass_gate(dve, 14)
            scan_dve(dve, st)
            pass_gate(dve, 15)
            residual_dve(dve, cd["out"], 2 * KD)
            pass_gate(dve, 16)
            adaln_dve(dve, st, 4, 3)
            pass_gate(dve, 17)
            ffn_dve(dve, st, 1)
            pass_gate(dve, 18)
            residual_dve(dve, ffn[1, "down"], 5 * KD)
            pass_gate(dve, 19)
            final_dve(dve, st, 5)

        @block.gpsimd
        def _(pool):
            st = Steps(pool, pool_step)
            for n, e in enumerate((EPS, GN_EPS, 1e-12)):
                pool.memset(eps_c[:, n:n + 1], e).then_inc(eps_ready, 1)
            pass_gate(pool, 1)
            pass_gate(pool, 2)
            ab_pool(pool, st)
            pass_gate(pool, 3)
            pass_gate(pool, 4)
            pass_gate(pool, 5)
            ffn_pool(pool, 0)
            pass_gate(pool, 6)
            pass_gate(pool, 7)
            pass_gate(pool, 8)
            pass_gate(pool, 9)
            pass_gate(pool, 10)
            pass_gate(pool, 11)
            pass_gate(pool, 12)
            pass_gate(pool, 13)
            kk_pool(pool)
            pass_gate(pool, 14)
            scan_pool(pool, st)
            pass_gate(pool, 15)
            pass_gate(pool, 16)
            ffn_pool(pool, 1)
            pass_gate(pool, 17)
            pass_gate(pool, 18)
            pass_gate(pool, 19)



def tile_out(w, k):
    return np.ascontiguousarray(w.reshape(k, P, -1, P).transpose(2, 1, 0, 3)).reshape(-1, P, k * P)


def tile_wide(w):
    return np.ascontiguousarray(w.reshape(KD, P, -1, 256).transpose(2, 1, 0, 3)).reshape(-1, P, KD * 256)


def cols(v):
    return np.asarray(v).reshape(-1, P).T


def constants():
    c = np.zeros((P, NCONST), np.float32)
    c[:, 0:P] = np.eye(P)
    c[:, P:2 * P] = 1
    half = np.arange(P) // HD
    c[:, 2 * P:3 * P] = half[:, None] == half[None, :]
    f = np.arange(P) % 32
    low = f < 16
    src = np.where(low, np.arange(P) + 16, np.arange(P) - 16)
    c[src, 3 * P + np.arange(P)] = np.where(low, -1, 1)
    at = 4 * P
    for m in masks():
        c[:, at:at + P] = np.tile(m, (2, 2))
        at += P
    assert at == NCONST
    return c


def rotation():
    f = np.arange(P) % 32
    inv = np.float32(10000.0) ** (-(f % 16).astype(np.float32) / np.float32(16))
    t = np.arange(LAT)
    pos = np.where(((np.arange(P) % 64) < 32)[:, None], (t // 64)[None, :], (t % 64)[None, :])
    ang = pos.astype(np.float32) * inv.astype(np.float32)[:, None]
    return np.stack([np.cos(ang), np.sin(ang)], 1).astype(np.float32)


def masks():
    i, j = np.arange(C)[:, None], np.arange(C)[None, :]
    out = [i < j, i > j, i <= j, i >= j]
    for l in range(LEVELS):
        b = 1 << l
        m = (i // (2 * b) == j // (2 * b)) & (i // b % 2 == 1) & (j // b % 2 == 0)
        out += [m, m.T]
    out = [m.astype(np.float32) for m in out]
    out[4], out[5] = -out[4], -out[5]
    return out


def kernel(**inputs):
    import concourse.bacc as bacc
    from concourse.bass_utils import run_bass_kernel_spmd

    a = {k: np.asarray(v) for k, v in inputs.items()}
    io = layout(a)
    nc = bacc.Bacc("TRN2", target_bir_lowering=False, num_devices=1)
    aps = {n: nc.dram_tensor("in_" + n, v.shape, mybir.dt.from_np(v.dtype), kind="ExternalInput").ap() for n, v in io.items()}
    for n, shape in OUTS.items():
        aps[n] = nc.dram_tensor("out_" + n, shape, F32, kind="ExternalOutput").ap()
    build(nc, aps)
    r = run_bass_kernel_spmd(nc, [{"in_" + n: v for n, v in io.items()}], core_ids=[0]).results[0]
    return unpack({n: np.asarray(r["out_" + n]) for n in OUTS})


def layout(a):
    io = {}
    io["x_fm"] = np.ascontiguousarray(np.concatenate([a["x_prompt"][0], a["x_sample"][0]], 0).T.reshape(KD, P, T).transpose(1, 0, 2))
    io["cvec"] = np.ascontiguousarray(np.stack([a["c_ctx"], a["c"][0]], 1).reshape(KD, P, 2).transpose(1, 0, 2))
    fields = {
        "norm1": a["norm1_g"], "norm2": a["norm2_g"], "final": a["final_g"], "mod_b": a["mod_b"],
        "conv_w": np.roll(a["ffn_conv_w"].reshape(DEPTH, 3, 2, FF), 1, 2),
        "conv_b": np.roll(a["ffn_conv_b"].reshape(DEPTH, 2, FF), 1, 1),
        "b_w": a["b_conv_w"][0], "b_b": a["b_conv_b"][0], "b_norm": a["b_norm_g"][0],
        "mu_r": a["c_mu_rkv"][0, 0], "mu_k": a["c_mu_rkv"][0, 1], "mu_v": a["c_mu_rkv"][0, 2],
        "mu_w": a["c_mu_wag"][0, 0], "mu_a": a["c_mu_wag"][0, 1], "mu_g": a["c_mu_wag"][0, 2],
        "w0": a["c_w0"][0], "a0": a["c_a0"][0], "k_k": a["c_k_k"][0], "k_a": a["c_k_a"][0], "r_k": a["c_r_k"][0],
        "ln_g": a["c_ln_g"][0], "ln_b": a["c_ln_b"][0],
        "qk_g": np.concatenate([np.tile(a["d_q_g"][0], 2 * KA), np.tile(a["d_k_g"][0], 4)]),
    }
    par = np.empty((P, NPAR), np.float32)
    for n, v in fields.items():
        v = cols(v)
        par[:, PAR[n]:PAR[n] + v.shape[1]] = v
    io["par"] = par
    io["const"] = constants()
    io["mod_w"] = np.concatenate([tile_wide(w) for w in a["mod_w"]])
    w = a["ab_w_in"][0]
    io["ab_v"] = tile_wide(w[:, AD:2 * AD])
    t = tile_out(w, KD)
    io["ab_w"] = np.concatenate([t[[12 + i // 2 if i % 2 == 0 else 8 + i // 2 for i in range(8)]], t[0:4]])
    io["w_out"] = np.concatenate([tile_out(w, KD) for w in a["w_out"]])
    up = [tile_out(w, KD) for w in a["ffn_up"]]
    io["ffn_up"] = np.concatenate([np.stack([u[KF:], u[:KF]], 1).reshape(2 * KF, P, KD * P) for u in up])
    io["ffn_down"] = np.concatenate([tile_out(w, KF) for w in a["ffn_down"]])
    io["ws_t"] = np.ascontiguousarray(a["a_ws"][0].transpose(2, 0, 1))
    io["v_rows"] = np.ascontiguousarray(np.broadcast_to(np.stack([a["a_vnorm_g"][0], a["a_vnorm_b"][0]])[None], (P, 2, AD)))
    io["bs_rows"] = np.ascontiguousarray(np.broadcast_to(np.tile(a["a_bs"][0], (1, NT))[None], (P, 4, T)))
    w = a["cd_w_in"][0]
    t = tile_out(w, KD)
    keys = [tile_out(np.concatenate([w[:, 2048 + HD * g:2048 + HD * (g + 1)]] * 2, 1), KD) for g in range(2)]
    lora = [np.concatenate([a["c_w1"][0, 0], a["c_w1"][0, 1]], 1), np.concatenate([a["c_a1"][0, 0], a["c_a1"][0, 1]], 1), a["c_g1"][0]]
    io["cd_w"] = np.concatenate([t[0:16]] + keys + [tile_out(v, KD) for v in lora] + [t[17:18]])
    ckv = a["cache_k"][0, 0].transpose(2, 1, 0)
    io["cache_k"] = np.ascontiguousarray(np.concatenate([ckv, ckv], 0))
    io["cache_v"] = np.ascontiguousarray(a["cache_v"][0, 0].reshape(CTX, P))
    io["rope"] = rotation()
    w2 = a["c_w2"][0].reshape(P, HP, P)
    a2 = a["c_a2"][0].reshape(P, HP, P)
    g2 = a["c_g2"][0].reshape(P, HP, P)
    io["scan_w"] = np.ascontiguousarray(np.stack([w2, a2, g2], 2).transpose(1, 0, 2, 3).reshape(HP, P, 3 * P))
    st = np.zeros((HP, 2, 2, HD, 2, HD), np.float32)
    for d, name in enumerate(("state_wkv_fwd", "state_wkv_bwd")):
        s = a[name][0, 0].reshape(HP, 2, HD, HD)
        for e in range(2):
            st[:, d, e, :, e, :] = s[:, e].transpose(0, 2, 1)
    io["state"] = st.reshape(2 * HP, P, P)
    return io


OUTS = {"y": (P, KD, T), "new_k": (HD, 2, CTX), "new_v": (CTX, P), "new_state": (2 * HP, P, P)}
NCONST = (4 + 4 + 2 * LEVELS) * P


def unpack(r):
    y = r["y"].transpose(1, 0, 2).reshape(D, T).T
    k = r["new_k"].transpose(2, 1, 0)[None, None]
    v = r["new_v"].reshape(1, 1, CTX, 2, HD)
    s = r["new_state"].reshape(HP, 2, 2, HD, 2, HD)
    s = np.stack([s[:, :, e, :, e, :] for e in range(2)], 2).transpose(1, 0, 2, 4, 3).reshape(2, 1, 1, HEADS, HD, HD)
    out = (y[None, :CTX], y[None, CTX:], k, v, s[0], s[1])
    return tuple(np.ascontiguousarray(o) for o in out)
```

```python
from contextlib import ExitStack

import numpy as np
import concourse.bass as bass
from concourse import mybir
from concourse.alu_op_type import AluOpType as ALU

F32 = mybir.dt.float32
F32R = mybir.dt.float32r
ACT = mybir.ActivationFunctionType
AX = mybir.AxisListType

P = 128
D = 1024
KD = D // P
CTX, LAT = 128, 512
T = CTX + LAT
NT = T // P
HALF = T // 2
DEPTH = 2
AD = 512
KA = AD // P
TAPS = 31
PAD = TAPS // 2
GLU = PAD + CTX + PAD + LAT + PAD
CONV = GLU - 2 * PAD
FF = 2816
KF = FF // P
EPS = 1e-6
GN_EPS = 64e-5
HD = 64
HP = 4
C = 64
NC = T // C
NCC = CTX // C
HEADS = 8
FFU = 1 + CTX + 1 + LAT + 1
NARROW = KD * P
KH = KF // 2
DEEP = KH * P
SLOT = DEEP + 2 * NARROW
E_HALF = float(np.exp(-0.5))
CUTS = [(0, CTX, 0), (CTX, HALF, 1), (HALF, T, 1)]
GROUPS = [(0, CTX, 0), (CTX, T, 1)]

PAR = {}


def _fields():
    at = 0
    for name, n in [("norm1", DEPTH * KD), ("norm2", DEPTH * KD), ("final", KD), ("mod_b", DEPTH * 48),
                    ("conv_w", DEPTH * 3 * 2 * KF), ("conv_b", DEPTH * 2 * KF), ("b_w", TAPS * KA), ("b_b", KA),
                    ("b_norm", KA), ("mu_r", KA), ("mu_k", KA), ("mu_v", KA), ("mu_w", KD), ("mu_a", KD),
                    ("mu_g", KD), ("w0", 2 * KA), ("a0", 2 * KA), ("k_k", KA), ("k_a", KA), ("r_k", KA),
                    ("ln_g", KA), ("ln_b", KA), ("qk_g", KA + 2)]:
        PAR[name] = at
        at += n
    return at


NPAR = _fields()
CONST = {"ident": 0, "ones": P, "head_ones": 2 * P, "rope_perm": 3 * P, "masks": 4 * P}
LEVELS = 6
ARENA = 37760
SCAN_STEPS = 49
SCAN_POOL = 12


class Steps:

    def __init__(self, eng, sem):
        self.eng, self.sem, self.n, self.turn = eng, sem, 0, None

    def __call__(self, ins):
        ins.then_inc(self.sem, 1)
        self.n += 1
        return ins

    def loop(self, i, per):
        self.turn, self.first, self.per = i, self.n, per

    def end(self, turns):
        assert self.n - self.first == self.per, (self.n - self.first, self.per)
        self.n, self.turn = self.first + self.per * turns, None

    def wait(self, but=0):
        if self.turn is None:
            self.eng.wait_ge(self.sem, self.n - but)
        else:
            self.eng.wait_ge(self.sem, self.turn * self.per + self.n - but)


def build(nc, io, stop=99):
    ctx = ExitStack()
    with ctx:
        def sb(name, shape, dt=F32):
            return ctx.enter_context(nc.sbuf_tensor(name, shape, dt))

        def sem(name):
            return ctx.enter_context(nc.semaphore(name))

        x = sb("x", [P, KD, T])
        par = sb("par", [P, NPAR])
        const = sb("const", [P, io["const"].shape[1]])
        mods = [sb("mod%d" % layer, [P, 48, 2]) for layer in range(DEPTH)]
        amuls = [sb("amul%d" % layer, [P, 2, KD, 2]) for layer in range(DEPTH)]
        cvec = sb("cvec", [P, KD, 2])
        eps_c = sb("eps_c", [P, 4])
        wslot_at = -(-nc.sbuf_base // 32) * 32
        wslot = sb("wslot", [P, 2, SLOT])
        rs = sb("rs", [P, T])
        arena_at = -(-nc.sbuf_base // 32) * 32
        arena = sb("arena", [P, ARENA])
        ps = ctx.enter_context(nc.psum_tensor("ps", [P, 8, 512], F32))

        ident = const[:, 0:P]
        ones = const[:, P:2 * P]
        head_ones = const[:, 2 * P:3 * P]

        def pcol(name, n=0):
            return par[:, PAR[name] + n:PAR[name] + n + 1]

        def region(at, *shape):
            n = int(np.prod(shape))
            assert at + n <= ARENA, (at, n)
            v = arena[:, at:at + n]
            if len(shape) == 2:
                v = v.rearrange("p (a b) -> p a b", a=shape[0])
            if len(shape) == 3:
                v = v.rearrange("p (a b c) -> p a b c", a=shape[0], b=shape[1])
            return v

        def parts(name, at, *shape):
            assert at + int(np.prod(shape)) <= ARENA, name
            return nc.alloc_sbuf_tensor_at(name, [P, *shape], F32R, offset=arena_at + 4 * at)

        w_hi, w_lo = ([nc.alloc_sbuf_tensor_at("%s%d" % (name, s), [P, NARROW], F32R,
                                               offset=wslot_at + 4 * (s * SLOT + DEEP + n * NARROW)) for s in range(2)]
                      for n, name in ((0, "w_hi"), (1, "w_lo")))
        d_hi, d_lo = ([parts("%s%d" % (name, s), at + s * DEEP, DEEP) for s in range(2)]
                      for at, name in ((0, "d_hi"), (28176, "d_lo")))

        def pair(s):
            return ps[:, 2 * s:2 * s + 2, 0:HALF]

        def cut(s, a, b):
            return ps[:, 2 * s + a // HALF, a % HALF:a % HALF + b - a]

        gate = sem("gate")
        loaded = sem("loaded")
        w_in = [sem("w_in0"), sem("w_in1")]
        product = sem("product")
        hi_ready = sem("hi_ready")
        lo_ready = sem("lo_ready")
        src_hi, src_lo = sem("src_hi"), sem("src_lo")
        drained = [sem("drained0"), sem("drained1")]
        act_step, dve_step, pool_step = sem("act_step"), sem("dve_step"), sem("pool_step")
        out_done = sem("out_done")

        tiles = []
        split_pairs = {}
        tile_cols = {}

        def stream(dram, first, n, cols, split=False):
            base = sum(t[2] for t in tiles) // 2
            split_pairs[base] = sum(t[2] for t in tiles if t[4]) // 2
            tile_cols[base] = cols
            tiles.append((dram, first, n, cols, split))
            return base

        def take(pe, base, i, s):
            pe.wait_ge(w_in[s], i * 16 + 16 * (base + 1))
            pe.wait_ge(drained[s], i + base + 1)

        def have(eng, base, i, s):
            eng.wait_ge(product, i * 2 + 2 * base + s + 1)

        def tile_parts(base, s):
            return (d_hi[s], d_lo[s]) if tile_cols[base] == DEEP else (w_hi[s], w_lo[s])

        def product_of_parts(base, s, ks, k_all, hi, lo):
            wh, wl = tile_parts(base, s)
            for h in range(2):
                for kk in ks:
                    m = slice(kk * P, (kk + 1) * P)
                    t = slice(h * HALF, (h + 1) * HALF)
                    out = ps[:, 2 * s + h, 0:HALF]
                    nc.tensor.matmul(out, wh[:, m], hi[:, kk, t], start=(kk == 0), stop=False)
                    nc.tensor.matmul(out, wh[:, m], lo[:, kk, t], start=False, stop=False)
                    last = nc.tensor.matmul(out, wl[:, m], hi[:, kk, t], start=False, stop=(kk == k_all - 1))
            return last

        def take_parts(pe, base, i, s):
            pe.wait_ge(lo_ready, i * 2 + (2 * split_pairs[base] + s + 1))
            pe.wait_ge(drained[s], i + base + 1)

        def project_parts_pe(pe, base, n, k, hi, lo, late=None):
            if late:
                take_parts(pe, base, 0, 0)
                product_of_parts(base, 0, range(k - 1), k, hi, lo)
                late()
                product_of_parts(base, 0, [k - 1], k, hi, lo).then_inc(product, 1)
                take_parts(pe, base, 0, 1)
                product_of_parts(base, 1, range(k), k, hi, lo).then_inc(product, 1)
            with pe.Fori(1 if late else 0, n // 2) as i:
                for s in range(2):
                    take_parts(pe, base, i, s)
                    product_of_parts(base, s, range(k), k, hi, lo).then_inc(product, 1)

        def tile_hi(act, base, i, s):
            act.wait_ge(w_in[s], i * 16 + 16 * (base + 1))
            act.wait_ge(product, i * 2 + (2 * base + s - 1))
            nc.scalar.activation(tile_parts(base, s)[0][:, :], wslot[:, s, 0:tile_cols[base]], ACT.Copy).then_inc(hi_ready, 1)

        def tile_lo(pool, base, i, s):
            wh, wl = tile_parts(base, s)
            pool.wait_ge(hi_ready, i * 2 + (2 * split_pairs[base] + s + 1))
            pool.tensor_tensor(wl[:, :], wslot[:, s, 0:tile_cols[base]], wh[:, :], ALU.subtract).then_inc(lo_ready, 1)

        def parts_act(act, base, n, use=None, then=None, st=None, per=0):
            with act.Fori(0, n // 2 - 1) as i:
                if st:
                    st.loop(i, per)
                for s in range(2):
                    tile_hi(act, base, i + 1, s)
                    if use:
                        use(i, s)
                if st:
                    st.end(n // 2 - 1)
            for s in range(2):
                if then is not None:
                    tile_hi(act, then, 0, s)
                if use:
                    use(n // 2 - 1, s)

        def parts_pool(pool, base, n, then=None, use=None):
            with pool.Fori(0, n // 2 - 1) as i:
                for s in range(2):
                    tile_lo(pool, base, i + 1, s)
                if use:
                    use(i)
            if then is not None:
                for s in range(2):
                    tile_lo(pool, then, 0, s)
            if use:
                use(n // 2 - 1)

        h = region(0, KD, T)
        sq = region(5120, KD, T)
        u = region(10240, KA, T)
        vtm = region(12800, NT, AD)
        glu = region(15360, KA, GLU)
        conv = region(18100, KA, CONV)
        ycat = region(20720, KD, T)
        wsT = region(25840, 4, P)
        vrow = region(26352, 2, AD)
        bsrow = region(27376, 4, T)
        sg = region(29936, T)
        lnst = region(30576, NT, 6)
        lnmv = region(30606, NT, 2)
        hid_hi, hid_lo = parts("hid_hi", 10240, KH, T), parts("hid_lo", 17280, KH, T)
        up = region(24320, 2, FFU)
        hid = region(27530, T)
        yv = region(25606, 2, FFU - 2)
        sil = region(26888, FFU - 2)
        h_hi, h_lo = parts("h_hi", 5120, KD, T), parts("h_lo", 31360, KD, T)
        h1_hi, h1_lo = parts("h1_hi", 21760, KD, T), parts("h1_lo", 32000, KD, T)
        y_hi, y_lo = parts("y_hi", 0, KD, T), parts("y_lo", 5120, KD, T)
        y1_hi, y1_lo = parts("y1_hi", 5120, KD, T), parts("y1_lo", 0, KD, T)
        mrow = region(31360, 48 * P)

        mod_base = [None] * DEPTH

        def modulation_tiles(layer):
            mod_base[layer] = stream(io["mod_w"], 24 * layer, 24, KD * 256)

        def modulation_pe(pe, layer):
            with pe.Fori(0, 12) as i:
                for s in range(2):
                    take(pe, mod_base[layer], i, s)
                    w = wslot[:, s, 0:KD * 256].rearrange("p (k m) -> p k m", k=KD)
                    for k in range(KD):
                        last = nc.tensor.matmul(ps[0:2, 2 * s, 0:256], cvec[:, k, :], w[:, k, :],
                                                start=(k == 0), stop=(k == KD - 1))
                    last.then_inc(product, 1)
            pe.wait_ge(mrow_ready, layer + 1)
            for j in range(48):
                last = nc.tensor.transpose(ps[:, 1, 2 * j:2 * j + 2], mrow[0:2, j * P:(j + 1) * P], ident[0:2, 0:2])
            last.then_inc(mcol_ready, 1)

        def modulation_act(act, st, layer):
            with act.Fori(0, 12) as i:
                for s in range(2):
                    have(act, mod_base[layer], i, s)
                    nc.scalar.activation(mrow[0:2, bass.ds(i * 512 + s * 256, 256)], ps[0:2, 2 * s, 0:256],
                                         ACT.Copy).then_inc(drained[s], 1)
            act.drain().then_inc(mrow_ready, 1)

        def modulation_dve(dve, st, layer):
            dve.wait_ge(mcol_ready, layer + 1)
            mod, amul = mods[layer], amuls[layer]
            cols = ps[:, 1, 0:96].rearrange("p (j v) -> p j v", v=2)
            bias = par[:, PAR["mod_b"] + 48 * layer:PAR["mod_b"] + 48 * (layer + 1)]
            for v in range(2):
                st(nc.vector.tensor_tensor(mod[:, :, v], cols[:, :, v], bias, ALU.add))
            st.wait()
            for n, (name, at) in enumerate([("norm1", KD), ("norm2", 4 * KD)]):
                g = par[:, PAR[name] + KD * layer:PAR[name] + KD * (layer + 1)]
                for v in range(2):
                    st(nc.vector.scalar_tensor_tensor(out=amul[:, n, :, v], in0=mod[:, at:at + KD, v], scalar=1.0,
                                                      in1=g, op0=ALU.add, op1=ALU.mult))

        silu_ready, eps_ready = sem("silu_ready"), sem("eps_ready")
        mrow_ready, mcol_ready = sem("mrow_ready"), sem("mcol_ready")

        sq_ready, sum_ready, root_ready, rs_ready = sem("sq_ready"), sem("sum_ready"), sem("root_ready"), sem("rs_ready")
        xn_ready = sem("xn_ready")

        def squares_act(act, squares):
            for o, a in squares:
                last = nc.scalar.activation(o, a, ACT.Square)
            last.then_inc(sq_ready, 1)

        def root_act(act, turn, n, eps):
            act.wait_ge(sum_ready, turn + 1)
            nc.scalar.activation(rs[:, :].rearrange("p (a b) -> p a b", a=2), pair(2), ACT.Sqrt, bias=eps_c[:, eps:eps + 1],
                                 scale=1.0 / (n * P)).then_inc(root_ready, 1)

        x_sq = region(36480, 2, T)
        x_squared = sem("x_squared")

        def square_of_x(act, base, i, s):
            act.wait_ge(drained[s], i + (base + 2))
            nc.scalar.activation(x_sq[:, s, :], x[:, i * 2 + s, :], ACT.Square).then_inc(x_squared, 1)

        def sum_of_x(pe, turn, i, s):
            pe.wait_ge(x_squared, i * 2 + (KD * turn + s + 1))
            for h in range(2):
                last = nc.tensor.matmul(ps[:, 4 + h, 0:HALF], ones, x_sq[:, s, h * HALF:(h + 1) * HALF],
                                        start=isinstance(i, int) and i == 0 and s == 0,
                                        stop=isinstance(i, int) and i == KD // 2 - 1 and s == 1)
            return last

        def last_product_pe(pe, base, k, hi, lo, turn, late=None):
            def tile(i, s):
                take_parts(pe, base, i, s)
                if late and isinstance(i, int) and i == 0 and s == 0:
                    product_of_parts(base, 0, range(k - 1), k, hi, lo)
                    late()
                    product_of_parts(base, 0, [k - 1], k, hi, lo).then_inc(product, 1)
                else:
                    product_of_parts(base, s, range(k), k, hi, lo).then_inc(product, 1)

            tile(0, 0)
            tile(0, 1)
            for s in range(2):
                sum_of_x(pe, turn, 0, s)
                tile(1, s)
            with pe.Fori(2, KD // 2) as i:
                for s in range(2):
                    sum_of_x(pe, turn, i - 1, s)
                    tile(i, s)
            for s in range(2):
                last = sum_of_x(pe, turn, KD // 2 - 1, s)
            last.then_inc(sum_ready, 1)

        def rms_pe(pe, turn, n):
            pe.wait_ge(sq_ready, turn + 1)
            for hh in range(2):
                for k in range(n):
                    last = nc.tensor.matmul(ps[:, 4 + hh, 0:HALF], ones, sq[:, k, hh * HALF:(hh + 1) * HALF],
                                            start=(k == 0), stop=(k == n - 1))
            last.then_inc(sum_ready, 1)

        def rms_dve(dve, st, turn):
            dve.wait_ge(root_ready, turn + 1)
            st(nc.vector.reciprocal(rs[:, :], rs[:, :]))
            st.wait()

        def adaln_act(act, xn, n, hi):
            mod, amul = mods[xn // 2], amuls[xn // 2]
            for k in range(KD):
                act.wait_ge(xn_ready, KD * xn + k + 1)
                for a, b, v in GROUPS:
                    nc.scalar.activation(hi[:, k, a:b], h[:, k, a:b], ACT.Identity, scale=amul[:, n, k, v:v + 1],
                                         bias=mod[:, 3 * KD * n + k, v:v + 1])
                for a, b, v in GROUPS:
                    last = nc.scalar.activation(h[:, k, a:b], h[:, k, a:b], ACT.Identity, scale=amul[:, n, k, v:v + 1],
                                                bias=mod[:, 3 * KD * n + k, v:v + 1])
                last.then_inc(src_hi, 1)

        def source_hi(act, a, hi, ks):
            for k in ks:
                nc.scalar.activation(hi[:, k, :], a[:, k, :], ACT.Copy).then_inc(src_hi, 1)

        def source_lo(eng, turn, a, hi, lo, ks):
            for k in ks:
                eng.wait_ge(src_hi, turn + k + 1)
                eng.tensor_tensor(lo[:, k, :], a[:, k, :], hi[:, k, :], ALU.subtract).then_inc(src_lo, 1)

        def adaln_dve(dve, st, turn, xn):
            rms_dve(dve, st, turn)
            for k in range(KD):
                nc.vector.tensor_tensor(h[:, k, :], x[:, k, :], rs[:, :], ALU.mult).then_inc(xn_ready, 1)

        def residual_dve(dve, base, at):
            mod = mods[0 if base < cd["in"] else 1]
            with dve.Fori(0, KD // 2) as i:
                for s in range(2):
                    have(dve, base, i, s)
                    for n, (a, b, v) in enumerate(CUTS):
                        last = nc.vector.scalar_tensor_tensor(
                            out=x[:, i * 2 + s, a:b], in0=cut(s, a, b), scalar=mod[:, i * 2 + (at + s), v:v + 1],
                            in1=x[:, i * 2 + s, a:b], op0=ALU.mult, op1=ALU.add)
                    last.then_inc(drained[s], 1)

        sg_ready, sg_used = sem("sg_ready"), sem("sg_used")
        vtm_ready, vmul_ready, vln_ready, std_ready = sem("vtm_ready"), sem("vmul_ready"), sem("vln_ready"), sem("std_ready")
        var_ready, glu_ready, conv_ready, mix_ready = sem("var_ready"), sem("glu_ready"), sem("conv_ready"), sem("mix_ready")
        mix_used, yn_ready, pads_ready, u_ready = sem("mix_used"), sem("yn_ready"), sem("pads_ready"), sem("u_ready")
        ab = {}

        def ab_tiles():
            ab["v"] = stream(io["ab_v"], 0, 2, KD * 256)
            ab["glu"] = stream(io["ab_w"], 0, 8, NARROW, split=True)
            ab["u"] = stream(io["ab_w"], 8, 4, NARROW, split=True)
            modulation_tiles(1)
            ab["out"] = stream(io["w_out"], 0, KD, NARROW, split=True)

        def ab_pe(pe):
            for s in range(2):
                pe.wait_ge(w_in[s], 16 * (ab["v"] + 1))
                w = wslot[:, s, 0:KD * 256].rearrange("p (k m) -> p k m", k=KD)
                for t in range(NT):
                    for k in range(KD):
                        last = nc.tensor.matmul(ps[:, 3 + t, s * 256:(s + 1) * 256], h[:, k, t * P:(t + 1) * P], w[:, k, :],
                                                start=(k == 0), stop=(k == KD - 1), skip_group_check=True)
                last.then_inc(product, 1)
            pe.sem_inc(drained[0], 1)
            pe.sem_inc(drained[1], 1)
            pe.wait_ge(vtm_ready, NT)
            project_parts_pe(pe, ab["glu"], 8, KD, h_hi, h_lo)
            project_parts_pe(pe, ab["u"], 4, KD, h_hi, h_lo)
            pe.wait_ge(vln_ready, NT)
            for g in range(4):
                if g == 2:
                    modulation_pe(pe, 1)
                if g >= 2:
                    pe.wait_ge(mix_used, g - 1)
                for t in range(NT):
                    at = (4 + 2 * (g % 2)) * 512 + t * P
                    last = nc.tensor.matmul(ps[:, at // 512, at % 512:at % 512 + P], vtm[:, t, g * P:(g + 1) * P],
                                            wsT[:, g, :], start=True, stop=True)
                last.then_inc(mix_ready, 1)

        def ab_act(act, st):
            tile_hi(act, ab["glu"], 0, 0)
            for t in range(NT):
                if t == 0:
                    act.wait_ge(product, 2 * ab["v"] + 2)
                nc.scalar.activation(vtm[:, t, :], ps[:, 3 + t, :], ACT.Gelu_apprx_tanh).then_inc(vtm_ready, 1)
            tile_hi(act, ab["glu"], 0, 1)
            act.wait_ge(var_ready, 1)
            nc.scalar.activation(lnmv[:, :, 1], lnmv[:, :, 1], ACT.Sqrt, bias=eps_c[:, 0:1]).then_inc(std_ready, 1)

            def gate_of_glu(i, s):
                if s == 0:
                    have(act, ab["glu"], i, 0)
                    act.wait_ge(sg_used, i + 1)
                    nc.scalar.activation(sg.rearrange("p (a b) -> p a b", a=2), pair(0), ACT.Sigmoid).then_inc(sg_ready, 1)

            def gelu_of_u(i, s):
                have(act, ab["u"], i, s)
                nc.scalar.activation(u[:, i * 2 + s, :].rearrange("p (a b) -> p a b", a=2), pair(s),
                                     ACT.Gelu_apprx_tanh).then_inc(drained[s], 1)

            parts_act(act, ab["glu"], 8, gate_of_glu, then=ab["u"])
            parts_act(act, ab["u"], 4, gelu_of_u)
            act.drain().then_inc(u_ready, 1)
            modulation_act(act, st, 1)
            for s in range(2):
                tile_hi(act, ab["out"], 0, s)

        def ab_dve(dve, st):
            dve.sem_inc(sg_used, 1)
            for t in range(NT):
                dve.wait_ge(vtm_ready, t + 1)
                st(nc.vector.bn_stats(lnst[:, t, :], vtm[:, t, :]))
            st.wait()
            for t in range(NT):
                last = st(nc.vector.bn_aggr(lnmv[:, t, :], lnst[:, t, :]))
            st.wait()
            dve.sem_inc(var_ready, 1)
            dve.wait_ge(std_ready, 1)
            st(nc.vector.reciprocal(lnmv[:, :, 1], lnmv[:, :, 1]))
            st.wait()
            for t in range(NT):
                nc.vector.tensor_scalar(vtm[:, t, :], vtm[:, t, :], lnmv[:, t, 0:1], lnmv[:, t, 1:2], ALU.subtract,
                                        ALU.mult).then_inc(vmul_ready, 1)
            dve.wait_ge(pads_ready, 1)
            with dve.Fori(0, 4) as i:
                have(dve, ab["glu"], i, 1)
                dve.wait_ge(sg_ready, i + 1)
                for a, b, v in CUTS:
                    o = PAD + a + PAD * v
                    last = nc.vector.tensor_tensor(glu[:, i, o:o + b - a], cut(1, a, b), sg[:, a:b], ALU.mult)
                last.then_inc(glu_ready, 1)
                dve.wait_ge(glu_ready, i + 1)
                dve.sem_inc(drained[0], 1)
                dve.sem_inc(drained[1], 1)
                dve.sem_inc(sg_used, 1)
            for k in range(KA):
                st(nc.vector.tensor_scalar(conv[:, k, :], glu[:, k, 0:CONV], pcol("b_w", k), pcol("b_b", k), ALU.mult,
                                           ALU.add))
            with dve.Fori(0, TAPS - 1) as i:
                st.loop(i, KA)
                for k in range(KA):
                    st.wait(but=KA - 1)
                    st(nc.vector.scalar_tensor_tensor(
                        out=conv[:, k, :], in0=glu[:, k, bass.ds(i + 1, CONV)],
                        scalar=par[:, bass.ds(i * KA + (PAR["b_w"] + KA + k), 1)], in1=conv[:, k, :], op0=ALU.mult, op1=ALU.add))
                st.end(TAPS - 1)
            st.wait()
            dve.sem_inc(conv_ready, 1)
            dve.wait_ge(u_ready, 1)
            for g in range(4):
                dve.wait_ge(mix_ready, g + 1)
                mixed = ps[:, 4 + 2 * (g % 2):6 + 2 * (g % 2), :].rearrange("p a b -> p (a b)")[:, 0:T]
                st(nc.vector.tensor_tensor(ycat[:, g, :], mixed, bsrow[:, g, :], ALU.add))
                st.wait()
                dve.sem_inc(mix_used, 1)
                st(nc.vector.tensor_tensor(ycat[:, g, :], ycat[:, g, :], u[:, g, :], ALU.mult))
            modulation_dve(dve, st, 1)

        def ab_pool(pool, st):
            pool.memset(glu[:, :, :], 0.0).then_inc(pads_ready, 1)
            for s in range(2):
                tile_lo(pool, ab["glu"], 0, s)
            for t in range(NT):
                pool.wait_ge(vmul_ready, t + 1)
                st(pool.tensor_tensor(vtm[:, t, :], vtm[:, t, :], vrow[:, 0, :], ALU.mult))
                st.wait()
                pool.tensor_tensor(vtm[:, t, :], vtm[:, t, :], vrow[:, 1, :], ALU.add).then_inc(vln_ready, 1)
            parts_pool(pool, ab["glu"], 8, then=ab["u"])
            parts_pool(pool, ab["u"], 4)
            for s in range(2):
                tile_lo(pool, ab["out"], 0, s)

        def yb_act(act, st, turn):
            act.wait_ge(conv_ready, 1)
            squares_act(act, [(sq[:, k, a:b], conv[:, k, a + PAD * v:b + PAD * v]) for k in range(KA) for a, b, v in GROUPS])
            root_act(act, turn, KA, 0)
            for k in range(KA):
                act.wait_ge(yn_ready, k + 1)
                nc.scalar.activation(ycat[:, KA + k, :], ycat[:, KA + k, :], ACT.Silu, scale=pcol("b_norm", k))

        def yb_dve(dve, st, turn):
            rms_dve(dve, st, turn)
            for k in range(KA):
                for a, b, v in GROUPS:
                    last = nc.vector.tensor_tensor(ycat[:, KA + k, a:b], conv[:, k, a + PAD * v:b + PAD * v], rs[:, a:b], ALU.mult)
                last.then_inc(yn_ready, 1)

        up_ready, mid_ready, tap_ready, sil_ready = sem("up_ready"), sem("mid_ready"), sem("tap_ready"), sem("sil_ready")
        hid_ready = sem("hid_ready")
        hid_parts = sem("hid_parts")
        ffn = {}

        def ffn_tiles(layer):
            for half in range(2):
                ffn[layer, half, "up"] = stream(io["ffn_up"], 2 * (KF * layer + KH * half), 2 * KH, NARROW, split=True)
                ffn[layer, half, "down"] = stream(io["ffn_down"], KD * (2 * layer + half), KD, DEEP, split=True)

        def after_ffn_half(layer, half):
            return ffn[layer, 1, "up"] if half == 0 else None

        def ffn_pe(pe, layer):
            for half in range(2):
                project_parts_pe(pe, ffn[layer, half, "up"], 2 * KH, KD, h_hi, h_lo)
                done = KF * layer + KH * (half + 1) + 1
                pe.wait_ge(hid_parts, done - 1)
                late = lambda: pe.wait_ge(hid_parts, done)
                if half == 0:
                    project_parts_pe(pe, ffn[layer, half, "down"], KD, KH, hid_hi, hid_lo, late=late)
                else:
                    last_product_pe(pe, ffn[layer, half, "down"], KH, hid_hi, hid_lo, 2 * layer + 1, late=late)

        def ffn_act(act, st, layer):
            for half in range(2):
                base, n0 = ffn[layer, half, "up"], KF * layer + KH * half
                cw, cb = PAR["conv_w"] + 6 * KF * layer + KH * half, PAR["conv_b"] + 2 * KF * layer + KH * half

                def use(i, s):
                    have(act, base, i, s)
                    act.wait_ge(hid_ready, i + (n0 + 1))
                    for a, b, v in CUTS:
                        last = nc.scalar.activation(up[:, s, 1 + a + v:1 + b + v], cut(s, a, b), ACT.Copy)
                    st(last)
                    st.wait()
                    act.sem_inc(drained[s], 1)
                    nc.scalar.activation(yv[:, s, :], up[:, s, 1:FFU - 1], ACT.Identity,
                                         scale=par[:, bass.ds(i + (cw + 2 * KF + s * KF), 1)],
                                         bias=par[:, bass.ds(i + (cb + s * KF), 1)]).then_inc(mid_ready, 1)
                    if s == 1:
                        act.wait_ge(tap_ready, i * 2 + (2 * n0 + 1))
                        nc.scalar.activation(sil, yv[:, 0, :], ACT.Silu).then_inc(sil_ready, 1)

                parts_act(act, base, 2 * KH, use, then=ffn[layer, half, "down"], st=st, per=2)
                down = ffn[layer, half, "down"]
                parts_act(act, down, KD, then=after_ffn_half(layer, half),
                          use=(lambda i, s: square_of_x(act, down, i, s)) if half == 1 else None)

        def ffn_dve(dve, st, layer):
            if layer == 0:
                dve.sem_inc(hid_ready, 1)
                dve.sem_inc(hid_parts, 1)
            for half in range(2):
                n0 = KF * layer + KH * half
                cw = PAR["conv_w"] + 6 * KF * layer + KH * half
                if half == 1:
                    dve.wait_ge(product, 2 * ffn[layer, 0, "down"] + KD)
                with dve.Fori(0, KH) as i:
                    st.loop(i, 2)
                    for s in range(2):
                        dve.wait_ge(mid_ready, i * 2 + (2 * n0 + s + 1))
                        st(nc.vector.scalar_tensor_tensor(out=yv[:, s, :], in0=up[:, s, 0:FFU - 2],
                                                          scalar=par[:, bass.ds(i + (cw + s * KF), 1)], in1=yv[:, s, :],
                                                          op0=ALU.mult, op1=ALU.add))
                        st.wait()
                        nc.vector.scalar_tensor_tensor(out=yv[:, s, :], in0=up[:, s, 2:FFU],
                                                       scalar=par[:, bass.ds(i + (cw + 4 * KF + s * KF), 1)], in1=yv[:, s, :],
                                                       op0=ALU.mult, op1=ALU.add).then_inc(tap_ready, 1)
                    st.end(KH)
                    dve.wait_ge(sil_ready, i + (n0 + 1))
                    dve.wait_ge(tap_ready, i * 2 + (2 * n0 + 2))
                    dve.wait_ge(hid_parts, i + (n0 + 1))
                    for out in (hid_hi[:, i, :], hid):
                        for a, b, v in GROUPS:
                            last = nc.vector.tensor_tensor(out[:, a:b], sil[:, a + v:b + v], yv[:, 1, a + v:b + v], ALU.mult)
                    last.then_inc(hid_ready, 1)
                residual_dve(dve, ffn[layer, half, "down"], 5 * KD)

        def ffn_parts_pool(pool, layer):
            for half in range(2):
                n0 = KF * layer + KH * half

                def low_of_hid(i):
                    pool.wait_ge(hid_ready, i + (n0 + 2))
                    pool.tensor_tensor(hid_lo[:, i, :], hid, hid_hi[:, i, :], ALU.subtract).then_inc(hid_parts, 1)

                parts_pool(pool, ffn[layer, half, "up"], 2 * KH, then=ffn[layer, half, "down"], use=low_of_hid)
                parts_pool(pool, ffn[layer, half, "down"], KD, then=after_ffn_half(layer, half))

        def ffn_pool(pool, layer):
            for at in (0, 1 + CTX, FFU - 1):
                last = pool.memset(up[:, :, at:at + 1], 0.0)


        rkvq = region(5120, 18, T)
        rkv, qk = rkvq[:, 0:12, :], rkvq[:, 12:18, :]
        dh = region(16640, KD, T)
        ycat1 = region(0, KD, T)
        xmix = [region(26880, KD, T), region(21760, KD, T)]
        lw, la, lg = region(32000, T), region(32640, T), region(33280, T)
        vd = region(33920, NT, P)
        ck = region(34560, 2, P)
        cv = region(34816, P)
        rope = region(16640, 2, LAT)
        hsq = [region(17664, T), region(18944, T)]
        hrs = [region(19584, T), region(20224, T)]
        rtmp = region(18304, LAT)
        prob = region(18944, 3, T)
        probT = region(20864, 2, NT, LAT)
        probC = region(25984, 2, P)
        qs = region(26240, T)
        srow = region(26880, 3, 3)
        shift = region(26912, KA, T)
        kk = region(12800, KA, T)
        U_AT = [15360 + 1280 * n for n in range(13)] + [33920, 35200]
        mats = {n: region(U_AT[j], NC, P) for n, j in
                (("A", 0), ("B", 1), ("K", 2), ("R", 3), ("MT", 4), ("Vb", 4), ("PT", 5), ("NT", 6), ("At", 7), ("AH", 7),
                 ("Bt", 8), ("Kt", 9), ("Vt", 10), ("QT", 11), ("X", 12), ("NV", 12), ("XT", 13), ("Y", 14), ("UV", 14))}
        bacc = wslot[:, 0, NARROW:NARROW + T]
        stage = wslot[:, 0, NARROW + T:NARROW + T + 2 * P]
        stage_g = wslot[:, 0, NARROW + T + 2 * P:NARROW + T + 3 * P]
        state = wslot[:, 0, NARROW + T + 3 * P:NARROW + T + 7 * P].rearrange("p (g b m) -> p g b m", g=2, b=2)
        ubuf = wslot[:, 0, NARROW + T + 7 * P:NARROW + T + 9 * P].rearrange("p (b m) -> p b m", b=2)
        wbuf, abuf = region(36480, T), region(37120, T)
        gbuf = wslot[:, 0, NARROW + T + 9 * P:NARROW + 2 * T + 9 * P]
        e2buf, kdbuf = (wslot[:, 1, NARROW + T + 32 + n * T:NARROW + 2 * T + 32 + n * T] for n in range(2))
        sgbuf = wslot[:, 1, NARROW + 3 * T + 32:NARROW + 3 * T + 32 + P]
        mask01 = wslot[:, 1, NARROW:NARROW + T]
        gend = wslot[:, 1, NARROW + T:NARROW + T + 16][:, 0:NC]
        halves = wslot[:, 1, NARROW + T + 16:NARROW + T + 16 + 4 * KA].rearrange("p (n k) -> p n k", n=2)

        cd = {}
        xmix_ready, mix_done, lora_ready, vd_ready = sem("xmix_ready"), sem("mix_done"), sem("lora_ready"), sem("vd_ready")

        def cd_tiles():
            cd["in"] = stream(io["cd_w"], 0, 18, NARROW, split=True)
            cd["lora"] = stream(io["cd_w"], 18, 4, KD * P)
            cd["out"] = stream(io["w_out"], KD, KD, NARROW, split=True)

        def cd_pe(pe):
            project_parts_pe(pe, cd["in"], 18, KD, h1_hi, h1_lo)
            for j, (i, s) in enumerate([(0, 0), (0, 1), (1, 0)]):
                pe.wait_ge(xmix_ready, j + 1)
                take(pe, cd["lora"], i, s)
                w = wslot[:, s, 0:KD * P].rearrange("p (k m) -> p k m", k=KD)
                for hh in range(2):
                    for k in range(KD):
                        last = nc.tensor.matmul(ps[:, 2 * s + hh, 0:HALF], w[:, k, :],
                                                xmix[j % 2][:, k, hh * HALF:(hh + 1) * HALF], start=(k == 0), stop=(k == KD - 1))
                last.then_inc(product, 1)
            pe.wait_ge(w_in[1], 16 * (cd["lora"] + 2))
            w = wslot[:, 1, 0:KD * P].rearrange("p (k m) -> p k m", k=KD)
            for t in range(NT):
                for k in range(KD):
                    last = nc.tensor.matmul(ps[:, 4 + t // 4, t % 4 * P:(t % 4 + 1) * P], h[:, k, t * P:(t + 1) * P],
                                            w[:, k, :], start=(k == 0), stop=(k == KD - 1))
            last.then_inc(product, 1)
            pe.sem_inc(drained[1], 1)

        def cd_act(act):
            def use(i, s):
                have(act, cd["in"], i, s)
                nc.scalar.activation(rkvq[:, i * 2 + s, :].rearrange("p (a b) -> p a b", a=2), pair(s),
                                     ACT.Copy).then_inc(drained[s], 1)

            for s in range(2):
                tile_hi(act, cd["in"], 0, s)
            parts_act(act, cd["in"], 18, use)
            for i, s, dst, f in ((0, 0, lw, ACT.Tanh), (0, 1, la, ACT.Copy), (1, 0, lg, ACT.Sigmoid)):
                have(act, cd["lora"], i, s)
                nc.scalar.activation(dst.rearrange("p (a b) -> p a b", a=2), pair(s), f).then_inc(drained[s], 1)
            have(act, cd["lora"], 1, 1)
            nc.scalar.activation(vd.rearrange("p t m -> p (t m)"),
                                 ps[:, 4:6, :].rearrange("p a b -> p (a b)")[:, 0:T], ACT.Copy).then_inc(vd_ready, 1)

        def shift_sum(eng, st, out, a):
            n = a.shape[1]
            st(eng.tensor_tensor(out[:, :, 1:T - 1], a[:, :, 0:T - 2], a[:, :, 2:T], ALU.add))
            st.wait()
            for c in range(n):
                st(eng.tensor_copy(out[:, c, 0:CTX + 1:CTX], a[:, c, 1:CTX + 2:CTX]))
                st(eng.tensor_copy(out[:, c, CTX - 1:T:LAT], a[:, c, CTX - 2:T - 1:LAT]))
            st.wait()

        def cd_dve(dve, st):
            shift_sum(dve, st, dh, h)
            st(nc.vector.scalar_tensor_tensor(out=dh[:, :, :], in0=dh[:, :, :], scalar=0.5, in1=h[:, :, :], op0=ALU.mult,
                                              op1=ALU.subtract))
            st.wait()
            for j, mu in enumerate(("mu_w", "mu_a", "mu_g")):
                if j == 1:
                    dve.wait_ge(product, 2 * cd["in"] + 18)
                if j == 2:
                    dve.wait_ge(product, 2 * cd["lora"] + 1)
                for k in range(KD):
                    last = nc.vector.scalar_tensor_tensor(out=xmix[j % 2][:, k, :], in0=dh[:, k, :], scalar=pcol(mu, k),
                                                          in1=h[:, k, :], op0=ALU.mult, op1=ALU.add)
                last.then_inc(xmix_ready, 1)

        hsq_ready, hsum_ready, hroot_ready, qn_ready, perm_ready, perm_read = (
            sem("hsq_ready"), sem("hsum_ready"), sem("hroot_ready"), sem("qn_ready"), sem("perm_ready"), sem("perm_read"))
        NQ = KA + 2

        def qk_act(act):
            for name, dst in (("rope", rope), ("cache_k", ck), ("cache_v", cv)):
                act.dma_start(dst, io[name]).then_inc(loaded, 16)
            for n in range(NQ):
                if n >= 2:
                    act.wait_ge(hsum_ready, n - 1)
                nc.scalar.activation(hsq[n % 2], qk[:, n, :], ACT.Square).then_inc(hsq_ready, 1)
                act.wait_ge(hsum_ready, n + 1)
                if n >= 2:
                    act.wait_ge(qn_ready, n - 1)
                nc.scalar.activation(halves_of(hrs[n % 2]), pair(2 * (n % 2)), ACT.Sqrt, bias=eps_c[:, 0:1],
                                     scale=1.0 / HD).then_inc(hroot_ready, 1)

        def halves_of(a):
            return a.rearrange("p (a b) -> p a b", a=2)

        def head_sums(pe, src, to):
            for hh in range(2):
                last = nc.tensor.matmul(ps[:, 2 * to + hh, 0:HALF], head_ones, src[:, hh * HALF:(hh + 1) * HALF],
                                        start=True, stop=True)
            return last

        def qk_pe(pe):
            for n in range(NQ + 1):
                if n < NQ:
                    pe.wait_ge(hsq_ready, n + 1)
                    if n >= 2:
                        pe.wait_ge(hroot_ready, n - 1)
                    head_sums(pe, hsq[n % 2], 2 * (n % 2)).then_inc(hsum_ready, 1)
                if n >= 1:
                    pe.wait_ge(qn_ready, n)
                    if n >= 3:
                        pe.wait_ge(perm_read, n - 2)
                    nc.tensor.matmul(ps[:, 2 + (n - 1) % 2, 0:LAT], const[:, 3 * P:4 * P], qk[:, n - 1, CTX:T], start=True,
                                     stop=True).then_inc(perm_ready, 1)

        def qk_dve(dve, st):
            dve.wait_ge(loaded, 16 * (LOADS + 3))
            for n in range(NQ + 1):
                if n < NQ:
                    r = hrs[n % 2]
                    dve.wait_ge(hroot_ready, n + 1)
                    st(nc.vector.reciprocal(r, r))
                    st.wait()
                    nc.vector.scalar_tensor_tensor(out=qk[:, n, :], in0=qk[:, n, :], scalar=pcol("qk_g", n), in1=r,
                                                   op0=ALU.mult, op1=ALU.mult).then_inc(qn_ready, 1)
                if n >= 1:
                    a = qk[:, n - 1, CTX:T]
                    st.wait()
                    dve.wait_ge(perm_ready, n)
                    st(nc.vector.tensor_tensor(a, a, rope[:, 0, :], ALU.mult))
                    nc.vector.tensor_tensor(rtmp, ps[:, 2 + (n - 1) % 2, 0:LAT], rope[:, 1, :], ALU.mult).then_inc(perm_read, 1)
                    st.wait()
                    dve.wait_ge(perm_read, n)
                    st(nc.vector.tensor_tensor(a, a, rtmp, ALU.add))

        def shift_pool(pool, st):
            for j, mu in enumerate(("mu_r", "mu_k", "mu_v")):
                a = rkv[:, KA * j:KA * (j + 1), :]
                shift_sum(pool, st, shift, a)
                st(pool.tensor_scalar(shift[:, :, :], shift[:, :, :], 0.5, None, ALU.mult))
                st.wait()
                st(pool.tensor_tensor(shift[:, :, :], shift[:, :, :], a, ALU.subtract))
                st.wait()
                for k in range(KA):
                    st(pool.tensor_scalar(shift[:, k, :], shift[:, k, :], pcol(mu, k), None, ALU.mult))
                st.wait()
                st(pool.tensor_tensor(a, a, shift[:, :, :], ALU.add))
                st.wait()

        qs_ready, qs_used, s_ready, max_ready, p_ready = (
            sem("qs_ready"), sem("qs_used"), sem("s_ready"), sem("max_ready"), sem("p_ready"))
        e_ready, pT_ready, pTs_ready, o_ready, o_used = (
            sem("e_ready"), sem("pT_ready"), sem("pTs_ready"), sem("o_ready"), sem("o_used"))
        UNITS = 2 * NT
        UNIT = [(e, t) for e in range(2) for t in range(NT)]
        SLOTS = 3
        USES = [("unit", n) for n in range(9)] + [("output", 0)] + [("unit", n) for n in range(9, UNITS)] + [("output", 1)]

        def use_banks(kind, n):
            b = 2 * (USES.index((kind, n)) % SLOTS)
            return ps[:, b:b + 2, :].rearrange("p a b -> p (a b)")

        def attn_pe(pe):
            pe.sem_inc(o_ready, 1)
            for g in range(2):
                with pe.Fori(0, 2) as j:
                    def score(n):
                        e, t = UNIT[n]
                        rows = slice(HD * e, HD * e + HD)
                        k = USES.index(("unit", n))
                        before = USES[:k - SLOTS + 1] if k >= SLOTS else []
                        units = sum(kind == "unit" for kind, _ in before)
                        pe.wait_ge(e_ready, j * UNITS + (2 * g * UNITS + units + 1))
                        if n < SLOTS or before[-1][0] == "output":
                            pe.wait_ge(o_used, j * 2 + (4 * g + len(before) - units + 1))
                        q = qs[rows, t * P:(t + 1) * P]
                        out = use_banks("unit", n)
                        if t == 0:
                            last = nc.tensor.matmul(out[:, 0:CTX], q, qk[rows, KA + g, 0:CTX], start=True, stop=True)
                        else:
                            nc.tensor.matmul(out[:, 0:LAT], q, qk[rows, KA + g, CTX:T], start=True, stop=True)
                            last = nc.tensor.matmul(out[:, LAT:T], q, ck[rows, g, :], start=True, stop=True)
                        last.then_inc(s_ready, 1)

                    def turn(n):
                        e, t = UNIT[n]
                        pe.wait_ge(p_ready, j * UNITS + (2 * g * UNITS + n + 1))
                        pe.wait_ge(pTs_ready, j * UNITS + (2 * g * UNITS + n + 1))
                        for b in range(1 if t == 0 else NT):
                            last = nc.tensor.transpose(ps[:, 6 + b // 4, b % 4 * P:(b % 4 + 1) * P],
                                                       prob[:, n % SLOTS, b * P:(b + 1) * P], ident)
                        last.then_inc(pT_ready, 1)

                    def output(e):
                        rows = slice(HD * e, HD * e + HD)
                        vcols = slice(HD * g, HD * g + HD)
                        pe.wait_ge(pTs_ready, j * UNITS + (2 * g * UNITS + NT * (e + 1) + 1))
                        nc.tensor.matmul(use_banks("output", e)[rows, LAT:T], vd[:, 0, vcols], probC[:, e, :], start=True, stop=True)
                        for b in range(NT):
                            v = vd[:, 1 + b, vcols] if b < 4 else cv[:, vcols]
                            last = nc.tensor.matmul(use_banks("output", e)[rows, 0:LAT], v, probT[:, e, b, :], start=(b == 0), stop=(b == NT - 1))
                        last.then_inc(o_ready, 1)

                    pe.wait_ge(qs_ready, j + (2 * g + 1))
                    score(0)
                    score(1)
                    for n in range(UNITS):
                        if n + 2 < UNITS:
                            score(n + 2)
                        turn(n)
                        if n == NT:
                            output(0)
                    output(1)

        def attn_act(act):
            act.sem_inc(e_ready, 1)
            act.sem_inc(pTs_ready, 1)
            for g in range(2):
                with act.Fori(0, 2) as j:
                    act.wait_ge(o_ready, j * 2 + (4 * g + 1))
                    nc.scalar.activation(qs, qk[:, j + 2 * g, :], ACT.Copy).then_inc(qs_ready, 1)

                    def expo(n):
                        e, t = UNIT[n]
                        act.wait_ge(max_ready, j * UNITS + (2 * g * UNITS + n + 1))
                        if n >= SLOTS:
                            act.wait_ge(pT_ready, j * UNITS + (2 * g * UNITS + n - SLOTS + 1))
                        w = P if t == 0 else T
                        src = use_banks("unit", n)[:, 0:w]
                        nc.scalar.activation(prob[:, n % SLOTS, 0:w], src, ACT.Exp, scale=0.125, bias=srow[:, n % SLOTS, 0:1],
                                             accum_out=srow[:, n % SLOTS, 1:2]).then_inc(e_ready, 1)

                    def copy(n):
                        e, t = UNIT[n]
                        act.wait_ge(pT_ready, j * UNITS + (2 * g * UNITS + n + 1))
                        if t == 0:
                            nc.scalar.activation(probC[:, e, :], ps[:, 6, 0:P], ACT.Copy).then_inc(pTs_ready, 1)
                        else:
                            q = slice((t - 1) * P, t * P)
                            nc.scalar.activation(probT[:, e, :, q], ps[:, 6:8, :].rearrange("p a (b q) -> p (a b) q", q=P)[:, 0:NT, :],
                                                 ACT.Copy).then_inc(pTs_ready, 1)

                    expo(0)
                    expo(1)
                    for n in range(UNITS):
                        if n + 2 < UNITS:
                            expo(n + 2)
                        copy(n)

        def attn_dve(dve, st):
            dve.sem_inc(o_used, 1)
            for g in range(2):
                with dve.Fori(0, 2) as j:
                    st.loop(j, 2 * UNITS)

                    def biggest(n):
                        e, t = UNIT[n]
                        w = P if t == 0 else T
                        dve.wait_ge(s_ready, j * UNITS + (2 * g * UNITS + n + 1))
                        src = use_banks("unit", n)[:, 0:w]
                        st(nc.vector.tensor_reduce(srow[:, n % SLOTS, 0:1], src, AX.X, ALU.max))
                        st.wait()
                        nc.vector.tensor_scalar(srow[:, n % SLOTS, 0:1], srow[:, n % SLOTS, 0:1], -0.125, None,
                                                ALU.mult).then_inc(max_ready, 1)

                    def norm(n):
                        e, t = UNIT[n]
                        w = P if t == 0 else T
                        dve.wait_ge(e_ready, j * UNITS + (2 * g * UNITS + n + 2))
                        st(nc.vector.reciprocal(srow[:, n % SLOTS, 2:3], srow[:, n % SLOTS, 1:2]))
                        st.wait()
                        nc.vector.tensor_scalar(prob[:, n % SLOTS, 0:w], prob[:, n % SLOTS, 0:w], srow[:, n % SLOTS, 2:3], None,
                                                ALU.mult).then_inc(p_ready, 1)

                    def out(e):
                        rows = slice(HD * e, HD * e + HD)
                        dve.wait_ge(o_ready, j * 2 + (4 * g + e + 2))
                        nc.vector.tensor_copy(ycat1[rows, j + (KA + 2 * g), 0:CTX], use_banks("output", e)[rows, LAT:T])
                        nc.vector.tensor_copy(ycat1[rows, j + (KA + 2 * g), CTX:T], use_banks("output", e)[rows, 0:LAT]).then_inc(o_used, 1)

                    biggest(0)
                    biggest(1)
                    norm(0)
                    for n in range(UNITS):
                        if n + 2 < UNITS:
                            biggest(n + 2)
                        if n + 1 < UNITS:
                            norm(n + 1)
                        if n == NT + 1:
                            out(0)
                    out(1)
                    st.end(2)

        ones_ready = sem("ones_ready")
        kk_ready, ksq_ready, ksum_ready, kroot_ready, kk_done = (
            sem("kk_ready"), sem("ksq_ready"), sem("ksum_ready"), sem("kroot_ready"), sem("kk_done"))

        def kk_act(act):
            for n in range(KA):
                act.wait_ge(kk_ready, n + 1)
                if n >= 2:
                    act.wait_ge(ksum_ready, n - 1)
                nc.scalar.activation(hsq[n % 2], kk[:, n, :], ACT.Square).then_inc(ksq_ready, 1)
                act.wait_ge(ksum_ready, n + 1)
                if n >= 2:
                    act.wait_ge(kk_done, n - 1)
                nc.scalar.activation(halves_of(hrs[n % 2]), pair(2 * (n % 2)), ACT.Sqrt,
                                     bias=eps_c[:, 2:3]).then_inc(kroot_ready, 1)

        def kk_pe(pe):
            for n in range(KA):
                pe.wait_ge(ksq_ready, n + 1)
                if n >= 2:
                    pe.wait_ge(kroot_ready, n - 1)
                head_sums(pe, hsq[n % 2], 2 * (n % 2)).then_inc(ksum_ready, 1)

        def kk_dve(dve, st):
            def scaled(n):
                nc.vector.tensor_scalar(kk[:, n, :], rkv[:, KA + n, :], pcol("k_k", n), None, ALU.mult).then_inc(kk_ready, 1)

            scaled(0)
            scaled(1)
            for n, name in enumerate(("w0", "a0")):
                st(nc.vector.tensor_scalar(halves[:, n, :], par[:, PAR[name]:PAR[name] + 2 * KA], 0.5, None, ALU.mult))
            for n in range(KA):
                r = hrs[n % 2]
                dve.wait_ge(kroot_ready, n + 1)
                st(nc.vector.reciprocal(r, r))
                if n + 2 < KA:
                    scaled(n + 2)
                st.wait()
                dve.wait_ge(kk_ready, n + 1)
                nc.vector.tensor_tensor(kk[:, n, :], kk[:, n, :], r, ALU.mult).then_inc(kk_done, 1)

        def kk_pool(pool):
            pool.memset(mask01[:, :], 1.0).then_inc(ones_ready, 1)
            pool.wait_ge(ones_ready, 1)
            pool.memset(mask01[:, 0:T:C], 0.0)

        GR = [(0, 4), (4, 8), (8, NC)]
        JOBS = [("At", "act"), ("Bt", "act"), ("Kt", "act"), ("M", "dve"), ("MT", "dve"), ("NT", "dve"),
                ("PT", "dve"), ("QT", "dve")]
        for l in range(1, LEVELS):
            JOBS += [("Y%d" % l, "dve")] + ([("X%d" % l, "dve")] if l < LEVELS - 1 else []) + [("XT%d" % l, "dve")]
        JOBS += [("NV", "act"), ("AH", "act"), ("UV", "act")]
        JOB_BANKS = 6
        VT_BANKS = (7, 3, 6)
        NG = len(GR)
        order, counts = {}, {"act": 0, "dve": 0}
        for name, who in JOBS:
            for g in range(NG):
                counts[who] += 1
                order[name, g] = (len(order), who, counts[who])
        by_number = {v[0]: v for v in order.values()}
        SEQ = [[2, 0, 3, 1, 4, 5, 6, 7, 8, 9], [9, 1, 8, 0, 7, 6, 5, 4, 3, 2]]
        evac = {"act": sem("evac_act"), "dve": sem("evac_dve")}
        job_ready, scan_ready, exp_ready = sem("job_ready"), sem("scan_ready"), sem("exp_ready")
        kd_ready, mult_dve, mult_pool, r_ready, xt_ready, zero_ready = (
            sem("kd_ready"), sem("mult_dve"), sem("mult_pool"), sem("r_ready"), sem("xt_ready"), sem("zero_ready"))
        bg_made, bg_read = sem("bg_made"), sem("bg_read")
        vb_ready, vt_made, vt_read, tail_y, tail_sq = (
            sem("vb_ready"), sem("vt_made"), sem("vt_read"), sem("tail_y"), sem("tail_sq"))
        u_made, u_read, s_made, s_read, y_ready, y_read = (
            sem("u_made"), sem("u_read"), sem("s_made"), sem("s_read"), sem("y_ready"), sem("y_read"))
        wa_in, g_in, state_in, state_out = sem("wa_in"), sem("g_in"), sem("state_in"), sem("state_out")
        pool_passed = sem("pool_passed")
        state_zero = sem("state_zero")

        def per_chunk(a):
            return a.rearrange("p (c t) -> p c t", t=C)

        def mask(n, count):
            a = const[:, 4 * P + n * C:4 * P + (n + 1) * C]
            return a.unsqueeze(1).to_broadcast([P, 2 * count, C])

        def by_head(a):
            return a.rearrange("p c (e t) -> p (c e) t", e=2)

        def ids(count):
            return ident.unsqueeze(1).to_broadcast([P, count, P])

        STRICT, INCL, LEVEL = 0, 2, 4

        def scan_bank(name, g):
            n = order[name, g][0]
            a, b = GR[g]
            return ps[:, n % JOB_BANKS, 0:(b - a) * P].rearrange("p (c m) -> p c m", m=P)

        class Unit:
            def __init__(self, j, o, d, r, prep=True, tail=False):
                self.j, self.o, self.d, self.r, self.prep, self.tail = j, o, d, r, prep, tail

            def i(self, m=1, c=0):
                return self.j * m + (self.o * m + c)

            def u(self, m, c=0):
                return self.j * (2 * m) + ((2 * self.o + self.d) * m + c)

            def round(self, name):
                names = (["bonus", "mean", "var"] if self.tail else []) + (["decay", "rate"] if self.prep else []) + (
                    ["gate"] if self.tail else [])
                return self.j * ROUNDS + (self.r + names.index(name) + 1)

            def rounds_before(self):
                return self.j * ROUNDS + self.r

            def rounds_after(self):
                return self.j * ROUNDS + (self.r + 2 * self.prep + 4 * self.tail)

            def next(self):
                return Unit(self.j, self.o + self.d, 1 - self.d, self.r)

            def last_pair(self):
                return Unit(self.j, self.o - 1, self.d, self.r)

        ROUNDS = 8
        FIRST = Unit(0, 0, 0, 2)
        LAST = Unit(0, HP - 1, 1, 4 + ROUNDS * (HP - 1), prep=False)
        END = Unit(0, HP, 0, 4 + ROUNDS * (HP - 1), prep=False, tail=True)

        def loop_units(j):
            return (Unit(j, 0, 1, 4), Unit(j, 1, 0, 6, tail=True))

        round_banks = ps[:, 6:8, 0:HALF]

        def scan_pe(pe):
            def round_of(v, name, lhs, src):
                pe.wait_ge(bg_read, v.round(name))
                for hh in range(2):
                    last = nc.tensor.matmul(ps[:, 6 + hh, 0:HALF], lhs, src[:, hh * HALF:(hh + 1) * HALF], start=True, stop=True)
                last.then_inc(bg_made, 1)

            def beside(v, name):
                if v.tail:
                    p = v.last_pair()
                    if name == "Bt":
                        if v is END:
                            pe.wait_ge(y_read, v.u(2, 1))
                        else:
                            pe.wait_ge(vt_read, v.i(NG, NG))
                        round_of(v, "bonus", head_ones, rkv[:, p.i(1, KA), :])
                    if name == "Kt":
                        round_of(v, "mean", head_ones, ycat1[:, p.i(), :])
                    if name == "NT":
                        pe.wait_ge(tail_sq, p.i(1, 1))
                        round_of(v, "var", head_ones, rkv[:, p.i(), :])
                    if name == "X2":
                        round_of(v, "gate", stage_g, lg)
                if v.prep:
                    rows = slice(HD * (1 - v.d), HD * (1 - v.d) + HD)
                    if name == "QT":
                        pe.wait_ge(wa_in, v.next().i(16, 16))
                        round_of(v, "decay", stage[rows, 0:P], lw[rows])
                    if name == "X1":
                        round_of(v, "rate", stage[rows, P:2 * P], la[rows])

            def unit(v):
                d = v.d

                def job(name, *args, needs=(), xt=False):
                    for g, (a, b) in enumerate(GR):
                        n = order[name, g][0]
                        before = ([by_number[n - JOB_BANKS]] if n >= JOB_BANKS else []) + [order[need, g] for need in needs]
                        for who in ("act", "dve"):
                            m = max([b[2] for b in before if b[1] == who], default=0)
                            if m:
                                pe.wait_ge(evac[who], v.u(counts[who], m))
                        if xt:
                            pe.wait_ge(xt_ready, v.u(NG, g + 1))
                        bank = scan_bank(name, g)
                        for c in range(a, b):
                            if len(args) == 1:
                                last = nc.tensor.transpose(bank[:, c - a, :], mats[args[0]][:, c, :], ident)
                            else:
                                last = nc.tensor.matmul(bank[:, c - a, :], mats[args[0]][:, c, :],
                                                        mats[args[1]][:, c, :], start=True, stop=True)
                        last.then_inc(job_ready, 1)
                    beside(v, name)

                pe.wait_ge(mult_dve, v.u(4, 4))
                pe.wait_ge(s_read, v.u(NC, 1))
                job("At", "A")
                pe.wait_ge(y_read, v.u(2, 1))
                if d == 0:
                    pe.wait_ge(vb_ready, v.i(1, 1))
                    for g, (a, b) in enumerate(GR):
                        for c in range(a, b):
                            last = nc.tensor.transpose(ps[:, VT_BANKS[g], (c - a) * P:(c - a + 1) * P], mats["Vb"][:, c, :], ident)
                        last.then_inc(vt_made, 1)
                    pe.wait_ge(vt_read, v.i(NG, NG - 1))
                job("Bt", "B")
                if d == 0:
                    pe.wait_ge(vt_read, v.i(NG, NG))
                pe.wait_ge(mult_pool, v.u(1, 1))
                job("Kt", "K")
                job("M", "A", "B")
                job("MT", "B", "A")
                job("NT", "K", "A")
                pe.wait_ge(r_ready, v.u(2, 2))
                job("PT", "B", "R")
                job("QT", "K", "R")
                for l in range(1, LEVELS):
                    xs = ["M"] if l == 1 else ["X%d" % (l - 1)]
                    ts = [] if l == 1 else ["XT%d" % (l - 1)]
                    job("Y%d" % l, "MT", "X", needs=xs + ["MT"])
                    if l < LEVELS - 1:
                        job("X%d" % l, "XT", "Y", needs=["Y%d" % l] + ts, xt=l == 1)
                    job("XT%d" % l, "Y", "XT", needs=["Y%d" % l] + ts)
                job("NV", "NT", "Vt", needs=["NT"])
                job("AH", "At", "XT", needs=["At", "XT%d" % (LEVELS - 1)])
                job("UV", "XT", "NV", needs=["NV"])
                pe.wait_ge(evac["act"], v.u(counts["act"], counts["act"]))
                pe.wait_ge(evac["dve"], v.u(counts["dve"], counts["dve"]))
                pe.wait_ge(bg_read, v.rounds_after() + 1)
                pe.wait_ge(state_in, v.u(16, 16))
                pe.wait_ge(state_zero, v.u(1, 1))
                step = [0, 0]
                for q, c in enumerate(SEQ[d]):
                    grp = 1 if c >= NCC else 0
                    cur = state[:, grp, step[grp] % 2, :]
                    if q >= 1:
                        last_q = q - 1 if q > 4 else q - 2
                        if last_q >= 0:
                            pe.wait_ge(s_read, v.u(NC, last_q + 2))
                    s_bank = ps[:, 2 + q % 2, 0:P]
                    y_bank = ps[:, 4 + c // 4, c % 4 * P:(c % 4 + 1) * P]
                    nc.tensor.matmul(ps[:, q % 2, 0:P], mats["AH"][:, c, :], cur, start=True, stop=True).then_inc(u_made, 1)
                    nc.tensor.matmul(s_bank, mats["Kt"][:, c, :], mats["Vt"][:, c, :], start=True, stop=False)
                    nc.tensor.matmul(y_bank, cur, mats["R"][:, c, :], start=True, stop=False)
                    pe.wait_ge(u_read, v.u(NC, q + 1))
                    uu = ubuf[:, q % 2, :]
                    nc.tensor.matmul(s_bank, mats["Bt"][:, c, :], uu, start=False, stop=True).then_inc(s_made, 1)
                    nc.tensor.matmul(y_bank, uu, mats["PT"][:, c, :], start=False, stop=False)
                    last = nc.tensor.matmul(y_bank, mats["Vt"][:, c, :], mats["QT"][:, c, :], start=False, stop=True)
                    step[grp] += 1
                last.then_inc(y_ready, 1)

            pe.sem_inc(y_ready, 1)
            pe.wait_ge(wa_in, 16)
            pe.wait_ge(bg_read, 1)
            for n, src in enumerate((lw, la)):
                pe.wait_ge(bg_read, n + 1)
                for hh in range(2):
                    last = nc.tensor.matmul(ps[:, 6 + hh, 0:HALF], stage[0:HD, n * P:(n + 1) * P],
                                            src[0:HD, hh * HALF:(hh + 1) * HALF], start=True, stop=True)
                last.then_inc(bg_made, 1)
            unit(FIRST)
            with pe.Fori(0, HP - 1) as j:
                for v in loop_units(j):
                    if v.tail:
                        pe.wait_ge(g_in, v.i(16))
                    unit(v)
            unit(LAST)
            pe.wait_ge(g_in, 16 * HP)
            for name in ("Bt", "Kt", "NT", "X2"):
                beside(END, name)

        def scan_act(act):
            def decay_and_rate(v, n, r):
                act.wait_ge(bg_made, r)
                nc.scalar.activation(halves_of((wbuf, abuf)[n]), round_banks, ACT.Tanh, scale=0.5,
                                     bias=halves[:, n, bass.ds(v.i(1, KA * v.d), 1)]).then_inc(bg_read, 1)

            def exps(v):
                act.wait_ge(scan_ready, v.u(1, 1))
                nc.scalar.activation(wbuf, wbuf, ACT.Exp)
                nc.scalar.activation(e2buf, gbuf, ACT.Exp, scale=-1.0)
                nc.scalar.activation(gbuf, gbuf, ACT.Exp).then_inc(exp_ready, 1)

            def tail_square(v):
                p = v.last_pair()
                act.wait_ge(tail_y, p.i(1, 1))
                nc.scalar.activation(rkv[:, p.i(), :], ycat1[:, p.i(), :], ACT.Square).then_inc(tail_sq, 1)

            def tail_root(v):
                act.wait_ge(bg_made, v.round("var"))
                nc.scalar.activation(halves_of(rs[:, :]), round_banks, ACT.Sqrt, bias=eps_c[:, 1:2],
                                     scale=1.0 / HD).then_inc(bg_read, 1)

            def unit(v):
                for name, who in JOBS:
                    if who != "act":
                        continue
                    if name == "Bt" and v.d == 0:
                        for g, (a, b) in enumerate(GR):
                            act.wait_ge(vt_made, v.i(NG, g + 1))
                            nc.scalar.activation(mats["Vt"][:, a:b, :],
                                                 ps[:, VT_BANKS[g], 0:(b - a) * P].rearrange("p (c m) -> p c m", m=P),
                                                 ACT.Copy).then_inc(vt_read, 1)
                    if name == "NV":
                        if v.tail:
                            tail_square(v)
                            tail_root(v)
                        if v.prep:
                            decay_and_rate(v.next(), 0, v.round("decay"))
                            decay_and_rate(v.next(), 1, v.round("rate"))
                            exps(v.next())
                    for g, (a, b) in enumerate(GR):
                        act.wait_ge(job_ready, v.u(len(order), order[name, g][0] + 1))
                        nc.scalar.activation(mats[name][:, a:b, :], scan_bank(name, g), ACT.Copy,
                                             scale=-1.0 if name in ("AH", "UV") else 1.0).then_inc(evac["act"], 1)

            act.sem_inc(bg_read, 1)
            decay_and_rate(FIRST, 0, 1)
            decay_and_rate(FIRST, 1, 2)
            exps(FIRST)
            unit(FIRST)
            with act.Fori(0, HP - 1) as j:
                for v in loop_units(j):
                    unit(v)
            unit(LAST)
            tail_square(END)
            tail_root(END)

        def scan_dve(dve, st):
            def decays(v, r):
                dve.wait_ge(bg_read, r + 1)
                st(nc.vector.tensor_scalar(wbuf, wbuf, -0.5 * E_HALF, -0.5 * E_HALF, ALU.mult, ALU.add))
                st.wait()
                way = slice(None, None, 1 if v.d == 0 else -1)
                st(nc.vector.tensor_tensor_scan(gbuf[:, way], mask01[:, :], wbuf[:, way], 0.0, ALU.mult, ALU.add))

            def decays_before(v):
                st.wait()
                nc.vector.tensor_tensor(wbuf, gbuf, wbuf, ALU.subtract).then_inc(scan_ready, 1)

            def rates(v, r):
                dve.wait_ge(bg_read, r + 2)
                st(nc.vector.tensor_scalar(abuf, abuf, 0.5, 0.5, ALU.mult, ALU.add))

            def keys_part(v):
                st.wait()
                st(nc.vector.tensor_scalar(kdbuf, abuf, 1.0, par[:, bass.ds(v.i(1, PAR["k_a"]), 1)], ALU.subtract, ALU.mult))
                st(nc.vector.tensor_tensor(abuf, kk[:, v.i(), :], abuf, ALU.mult))

            def keys_done(v):
                st.wait()
                nc.vector.scalar_tensor_tensor(out=kdbuf, in0=kdbuf, scalar=1.0, in1=rkv[:, v.i(1, KA), :], op0=ALU.add,
                                               op1=ALU.mult).then_inc(kd_ready, 1)

            def bonus_part(v):
                dve.wait_ge(kd_ready, v.u(1, 1))
                st(nc.vector.scalar_tensor_tensor(out=bacc if v.d == 0 else rkv[:, v.i(1, KA), :], in0=kdbuf,
                                                  scalar=par[:, bass.ds(v.i(1, PAR["r_k"]), 1)], in1=rkv[:, v.i(), :],
                                                  op0=ALU.mult, op1=ALU.mult))

            def bonus_sum(v):
                st.wait()
                if v.d == 1:
                    k = rkv[:, v.i(1, KA), :]
                    st(nc.vector.tensor_tensor(k, k, bacc, ALU.add))

            def a_and_b(v):
                dve.wait_ge(exp_ready, v.u(1, 1))
                st.wait()
                for e in range(2):
                    rows = slice(HD * e, HD * e + HD)
                    nc.vector.tensor_tensor(mats["A"][rows, :, rows], per_chunk(kk[rows, v.i(), :]), per_chunk(wbuf[rows]),
                                            ALU.mult).then_inc(mult_dve, 1)
                    nc.vector.tensor_tensor(mats["B"][rows, :, rows], per_chunk(abuf[rows]), per_chunk(e2buf[rows]),
                                            ALU.mult).then_inc(mult_dve, 1)

            def tail_bonus(v):
                p = v.last_pair()
                k = halves_of(rkv[:, p.i(1, KA), :])
                dve.wait_ge(bg_made, v.round("bonus"))
                nc.vector.tensor_tensor(k, halves_of(rkv[:, p.i(1, 2 * KA), :]), round_banks, ALU.mult).then_inc(bg_read, 1)

            def tail_mean(v):
                p = v.last_pair()
                y = halves_of(ycat1[:, p.i(), :])
                dve.wait_ge(bg_made, v.round("mean"))
                dve.wait_ge(y_read, v.u(2, 1))
                last = nc.vector.scalar_tensor_tensor(out=y, in0=round_banks, scalar=-1.0 / HD, in1=y, op0=ALU.mult, op1=ALU.add)
                st(last)
                st.wait()
                dve.sem_inc(bg_read, 1)
                dve.sem_inc(tail_y, 1)

            def tail_root(v, part):
                if part == 0:
                    dve.wait_ge(bg_read, v.round("var") + 1)
                a = rs[:, part * (T // 4):(part + 1) * (T // 4)]
                st(nc.vector.reciprocal(a, a))

            def tail_norm(v):
                y = ycat1[:, v.last_pair().i(), :]
                st.wait()
                st(nc.vector.tensor_tensor(y, y, rs[:, :], ALU.mult))

            def tail_affine(v):
                p = v.last_pair()
                y = ycat1[:, p.i(), :]
                st.wait()
                st(nc.vector.tensor_scalar(y, y, par[:, bass.ds(p.i(1, PAR["ln_g"]), 1)],
                                           par[:, bass.ds(p.i(1, PAR["ln_b"]), 1)], ALU.mult, ALU.add))

            def tail_add(v):
                p = v.last_pair()
                y = ycat1[:, p.i(), :]
                st.wait()
                st(nc.vector.tensor_tensor(y, y, rkv[:, p.i(1, KA), :], ALU.add))

            def tail_gate(v):
                y = halves_of(ycat1[:, v.last_pair().i(), :])
                dve.wait_ge(bg_made, v.round("gate"))
                st.wait()
                nc.vector.tensor_tensor(y, y, round_banks, ALU.mult).then_inc(bg_read, 1)

            def beside(v, name):
                if v.tail:
                    if name == "head":
                        tail_bonus(v)
                        tail_mean(v)
                    if name in ("QT", "Y1", "X1", "XT1"):
                        tail_root(v, ("QT", "Y1", "X1", "XT1").index(name))
                    if name == "Y2":
                        tail_norm(v)
                    if name == "X2":
                        tail_affine(v)
                    if name == "XT2":
                        tail_add(v)
                    if name == "X3":
                        tail_gate(v)
                if v.prep:
                    after, r = v.next(), v.round("decay")
                    if name == "Y2":
                        decays(after, r)
                    if name == "X2":
                        decays_before(after)
                    if name == "XT2":
                        rates(after, r)
                    if name == "Y3":
                        keys_part(after)
                    if name == "XT3":
                        keys_done(after)
                    if name == "Y4":
                        bonus_part(after)
                    if name == "X4":
                        bonus_sum(after)
                    if name == "XT%d" % (LEVELS - 1):
                        a_and_b(after)

            def unit(v):
                d = v.d
                st(nc.vector.tensor_copy(gend, gbuf[:, (C - 1 if d == 0 else 0):T:C]))
                for e in range(2):
                    rows = slice(HD * e, HD * e + HD)
                    nc.vector.tensor_tensor(mats["R"][rows, :, rows], per_chunk(rkv[rows, v.i(), :]), per_chunk(gbuf[rows]),
                                            ALU.mult).then_inc(r_ready, 1)
                beside(v, "head")
                for name, who in JOBS:
                    if who != "dve":
                        continue
                    for g, (c0, c1) in enumerate(GR):
                        dve.wait_ge(job_ready, v.u(len(order), order[name, g][0] + 1))
                        bank, n = scan_bank(name, g), c1 - c0
                        if name == "M":
                            xm = mats["X"][:, c0:c1, :]
                            st(nc.vector.tensor_tensor(by_head(xm), by_head(bank), mask(LEVEL + d, n), ALU.mult))
                            st.wait()
                            last = nc.vector.tensor_tensor(xm, xm, ids(n), ALU.add)
                        elif name in ("MT", "NT"):
                            last = nc.vector.tensor_tensor(by_head(mats[name][:, c0:c1, :]), by_head(bank), mask(STRICT + d, n),
                                                           ALU.mult)
                        elif name in ("PT", "QT"):
                            last = nc.vector.tensor_tensor(by_head(mats[name][:, c0:c1, :]), by_head(bank), mask(INCL + d, n),
                                                           ALU.mult)
                        elif name[0] == "Y":
                            last = nc.vector.tensor_tensor(by_head(mats["Y"][:, c0:c1, :]), by_head(bank),
                                                           mask(LEVEL + 2 * int(name[1]) + d, n), ALU.mult)
                        else:
                            xm = mats[name[:-1]][:, c0:c1, :]
                            last = nc.vector.tensor_tensor(xm, xm, bank, ALU.subtract)
                        last.then_inc(evac["dve"], 1)
                    beside(v, name)
                st.wait()
                step = [0, 0]
                for q, c in enumerate(SEQ[d]):
                    grp = 1 if c >= NCC else 0
                    cur, new = state[:, grp, step[grp] % 2, :], state[:, grp, (step[grp] + 1) % 2, :]
                    dve.wait_ge(u_made, v.u(NC, q + 1))
                    if q == 0:
                        dve.wait_ge(evac["act"], v.u(counts["act"], counts["act"]))
                    nc.vector.tensor_tensor(ubuf[:, q % 2, :], ps[:, q % 2, 0:P], mats["UV"][:, c, :],
                                            ALU.add).then_inc(u_read, 1)
                    st(nc.vector.tensor_scalar(sgbuf, cur, gend[:, c:c + 1], None, ALU.mult))
                    dve.wait_ge(s_made, v.u(NC, q + 1))
                    st.wait()
                    nc.vector.scalar_tensor_tensor(out=new, in0=ps[:, 2 + q % 2, 0:P], scalar=gend[:, c:c + 1], in1=sgbuf,
                                                   op0=ALU.mult, op1=ALU.add).then_inc(s_read, 1)
                    dve.wait_ge(s_read, v.u(NC, q + 2))
                    step[grp] += 1
                dve.wait_ge(y_ready, v.u(1, 2))
                if d == 1:
                    dve.wait_ge(y_read, v.u(2, 1))
                for e in range(2):
                    rows = slice(HD * e, HD * e + HD)
                    y = per_chunk(ycat1[rows, v.i(), :])
                    y_banks = ps[rows, 4:7, :].rearrange("p a (c m) -> p (a c) m", m=P)[:, 0:NC, rows]
                    if d == 0:
                        nc.vector.tensor_copy(y, y_banks).then_inc(y_read, 1)
                    else:
                        nc.vector.tensor_tensor(y, y, y_banks, ALU.add).then_inc(y_read, 1)

            dve.sem_inc(y_read, 1)
            dve.sem_inc(s_read, 1)
            dve.wait_ge(zero_ready, 1)
            decays(FIRST, 1)
            decays_before(FIRST)
            rates(FIRST, 1)
            keys_part(FIRST)
            keys_done(FIRST)
            bonus_part(FIRST)
            a_and_b(FIRST)
            unit(FIRST)
            with dve.Fori(0, HP - 1) as j:
                st.loop(j, SCAN_STEPS)
                for v in loop_units(j):
                    unit(v)
                st.end(HP - 1)
            unit(LAST)
            for name in ("head", "QT", "Y1", "X1", "XT1", "Y2", "X2", "XT2", "X3"):
                beside(END, name)

        def scan_pool(pool, st):
            def hold():
                pool.sem_inc(pool_passed, 1)

            def k_matrix(v):
                pool.wait_ge(kd_ready, v.u(1, 1))
                pool.wait_ge(exp_ready, v.u(1, 1))
                for e in range(2):
                    rows = slice(HD * e, HD * e + HD)
                    st(pool.tensor_tensor(mats["K"][rows, :, rows], per_chunk(kdbuf[rows]), per_chunk(e2buf[rows]), ALU.mult))
                    st.wait()
                pool.sem_inc(mult_pool, 1)

            def v_matrix(v):
                for e in range(2):
                    rows = slice(HD * e, HD * e + HD)
                    st(pool.tensor_copy(mats["Vb"][rows, :, rows], per_chunk(rkv[rows, v.i(1, 2 * KA), :])))
                    st.wait()
                    hold()
                pool.sem_inc(vb_ready, 1)

            def unit(v):
                pool.wait_ge(y_ready, v.u(1, 1))
                pool.wait_ge(s_read, v.u(NC, 1))
                hold()
                pool.dma_start(state[:, 1, 0, :], io["state"][v.u(1)]).then_inc(state_in, 16)
                if v is not FIRST:
                    pool.wait_ge(state_out, v.u(16))
                    hold()
                pool.memset(state[:, 0, 0, :], 0.0).then_inc(state_zero, 1)
                if v.d == 1:
                    pool.wait_ge(bg_read, v.rounds_before() + 1)
                    hold()
                    if v.prep:
                        pool.dma_start(stage, io["scan_w"][v.i(1, 1)][:, 0:2 * P]).then_inc(wa_in, 16)
                    pool.dma_start(stage_g, io["scan_w"][v.i()][:, 2 * P:3 * P]).then_inc(g_in, 16)
                for g, (c0, c1) in enumerate(GR):
                    pool.wait_ge(evac["dve"], v.u(counts["dve"], order["MT", g][2]))
                    xt = mats["XT"][:, c0:c1, :]
                    st(pool.tensor_tensor(by_head(xt), by_head(mats["MT"][:, c0:c1, :]), mask(LEVEL + 1 - v.d, c1 - c0), ALU.mult))
                    st.wait()
                    pool.tensor_tensor(xt, xt, ids(c1 - c0), ALU.add).then_inc(xt_ready, 1)
                if v.prep:
                    k_matrix(v.next())
                    if v.d == 1:
                        pool.wait_ge(job_ready, v.u(len(order), order["Y%d" % (LEVELS - 1), NG - 1][0] + 1))
                        hold()
                        v_matrix(v.next())
                pool.wait_ge(y_ready, v.u(1, 2))
                pool.wait_ge(s_read, v.u(NC, NC + 1))
                hold()
                pool.dma_start(io["new_state"][v.u(1)], state[:, 0, 0, :]).then_inc(state_out, 16)

            pool.dma_start(stage, io["scan_w"][0][:, 0:2 * P]).then_inc(wa_in, 16)
            st(pool.memset(region(U_AT[0], 5 * NC * P), 0.0))
            st.wait()
            pool.sem_inc(zero_ready, 1)
            v_matrix(FIRST)
            k_matrix(FIRST)
            unit(FIRST)
            with pool.Fori(0, HP - 1) as j:
                st.loop(j, SCAN_POOL)
                for v in loop_units(j):
                    unit(v)
                st.end(HP - 1)
            unit(LAST)
            pool.wait_ge(state_out, 16 * 2 * HP)

        def pass_gate(eng, n):
            eng.drain().then_inc(gate, 1)
            eng.wait_ge(gate, 4 * n)

        LOADS = 7
        modulation_tiles(0)
        ab_tiles()
        ffn_tiles(0)
        cd_tiles()
        ffn_tiles(1)

        y_out = sem("y_out")

        def final_dve(dve, st, turn):
            rms_dve(dve, st, turn)
            for k in range(KD):
                nc.vector.scalar_tensor_tensor(out=h[:, k, :], in0=x[:, k, :], scalar=pcol("final", k), in1=rs[:, :],
                                               op0=ALU.mult, op1=ALU.mult).then_inc(y_out, 1)

        block = ctx.enter_context(nc.Block())

        @block.sync
        def _(sp):
            for name, dst in (("par", par[:, :]), ("const", const[:, :]), ("cvec", cvec[:, :, :]), ("x_fm", x[:, :, :]),
                              ("ws_t", wsT), ("v_rows", vrow), ("bs_rows", bsrow)):
                sp.dma_start(dst, io[name]).then_inc(loaded, 16)
            at, before = 0, None
            for dram, first, n, cols, split in tiles:

                def free(i, s, split, cols):
                    if split and cols <= DEEP:
                        sp.wait_ge(lo_ready, i * 2 + (2 * parts_at + s - 1))
                    else:
                        sp.wait_ge(product, i * 2 + (2 * at + s - 1))

                parts_at = split_pairs[at]
                for s in range(2):
                    if at:
                        free(0, s, before, cols)
                    sp.dma_start(wslot[:, s, 0:cols], dram[first + s]).then_inc(w_in[s], 16)
                with sp.Fori(1, n // 2) if n > 2 else ExitStack() as i:
                    for s in range(2) if n > 2 else ():
                        free(i, s, split, cols)
                        sp.dma_start(wslot[:, s, 0:cols], dram[i * 2 + (first + s)]).then_inc(w_in[s], 16)
                at, before = at + n // 2, split

        @block.tensor
        def _(pe):
            pe.sem_inc(drained[0], 1)
            pe.sem_inc(drained[1], 1)
            pe.wait_ge(loaded, 16 * LOADS)
            pe.wait_ge(silu_ready, 1)
            rms_pe(pe, 0, KD)
            modulation_pe(pe, 0)
            pass_gate(pe, 1)
            pass_gate(pe, 2)
            ab_pe(pe)
            pass_gate(pe, 3)
            rms_pe(pe, 1, KA)
            pass_gate(pe, 4)
            pe.wait_ge(src_lo, 2 * KD)
            last_product_pe(pe, ab["out"], KD, y_hi, y_lo, 0)
            pass_gate(pe, 5)
            pass_gate(pe, 6)
            ffn_pe(pe, 0)
            pass_gate(pe, 7)
            pass_gate(pe, 8)
            cd_pe(pe)
            pass_gate(pe, 9)
            qk_pe(pe)
            pass_gate(pe, 10)
            attn_pe(pe)
            pass_gate(pe, 11)
            kk_pe(pe)
            pass_gate(pe, 12)
            scan_pe(pe)
            pass_gate(pe, 13)
            pe.wait_ge(src_lo, 5 * KD)
            last_product_pe(pe, cd["out"], KD, y1_hi, y1_lo, 2)
            pass_gate(pe, 14)
            pass_gate(pe, 15)
            ffn_pe(pe, 1)
            pass_gate(pe, 16)

        @block.scalar
        def _(act):
            st = Steps(act, act_step)
            act.wait_ge(loaded, 16 * LOADS)
            nc.scalar.activation(cvec[:, :, :], cvec[:, :, :], ACT.Silu).then_inc(silu_ready, 1)
            act.wait_ge(eps_ready, 3)
            squares_act(act, [(sq[:, k, :], x[:, k, :]) for k in range(KD)])
            root_act(act, 0, KD, 0)
            modulation_act(act, st, 0)
            pass_gate(act, 1)
            adaln_act(act, 0, 0, h_hi)
            pass_gate(act, 2)
            ab_act(act, st)
            pass_gate(act, 3)
            yb_act(act, st, 1)
            pass_gate(act, 4)
            source_hi(act, ycat, y_hi, range(KD))
            parts_act(act, ab["out"], KD, then=ffn[0, 0, "up"], use=lambda i, s: square_of_x(act, ab["out"], i, s))
            pass_gate(act, 5)
            root_act(act, 2, KD, 0)
            adaln_act(act, 1, 1, h_hi)
            pass_gate(act, 6)
            ffn_act(act, st, 0)
            pass_gate(act, 7)
            root_act(act, 3, KD, 0)
            adaln_act(act, 2, 0, h1_hi)
            pass_gate(act, 8)
            cd_act(act)
            pass_gate(act, 9)
            qk_act(act)
            pass_gate(act, 10)
            act.dma_start(io["new_k"], qk[0:HD, KA:KA + 2, 0:CTX]).then_inc(out_done, 16)
            act.dma_start(io["new_v"], vd[:, 0, :]).then_inc(out_done, 16)
            attn_act(act)
            act.wait_ge(out_done, 32)
            pass_gate(act, 11)
            kk_act(act)
            pass_gate(act, 12)
            scan_act(act)
            pass_gate(act, 13)
            for s in range(2):
                tile_hi(act, cd["out"], 0, s)
            source_hi(act, ycat1, y1_hi, range(KD))
            parts_act(act, cd["out"], KD, then=ffn[1, 0, "up"], use=lambda i, s: square_of_x(act, cd["out"], i, s))
            pass_gate(act, 14)
            root_act(act, 4, KD, 0)
            adaln_act(act, 3, 1, h_hi)
            pass_gate(act, 15)
            ffn_act(act, st, 1)
            pass_gate(act, 16)
            root_act(act, 5, KD, 0)
            for k in range(KD):
                act.wait_ge(y_out, k + 1)
                act.dma_start(io["y"][:, k, :], h[:, k, :]).then_inc(out_done, 16)
            act.wait_ge(out_done, 16 * (KD + 2))

        @block.vector
        def _(dve):
            st = Steps(dve, dve_step)
            dve.wait_ge(loaded, 16 * LOADS)
            adaln_dve(dve, st, 0, 0)
            modulation_dve(dve, st, 0)
            pass_gate(dve, 1)
            source_lo(dve, 0, h, h_hi, h_lo, range(1, KD, 2))
            pass_gate(dve, 2)
            ab_dve(dve, st)
            pass_gate(dve, 3)
            yb_dve(dve, st, 1)
            pass_gate(dve, 4)
            source_lo(dve, KD, ycat, y_hi, y_lo, range(KD))
            residual_dve(dve, ab["out"], 2 * KD)
            pass_gate(dve, 5)
            adaln_dve(dve, st, 2, 1)
            source_lo(dve, 2 * KD, h, h_hi, h_lo, range(1, KD, 2))
            pass_gate(dve, 6)
            ffn_dve(dve, st, 0)
            pass_gate(dve, 7)
            adaln_dve(dve, st, 3, 2)
            source_lo(dve, 3 * KD, h, h1_hi, h1_lo, range(1, KD, 2))
            pass_gate(dve, 8)
            cd_dve(dve, st)
            pass_gate(dve, 9)
            qk_dve(dve, st)
            pass_gate(dve, 10)
            attn_dve(dve, st)
            pass_gate(dve, 11)
            kk_dve(dve, st)
            pass_gate(dve, 12)
            scan_dve(dve, st)
            pass_gate(dve, 13)
            source_lo(dve, 4 * KD, ycat1, y1_hi, y1_lo, range(KD))
            residual_dve(dve, cd["out"], 2 * KD)
            pass_gate(dve, 14)
            adaln_dve(dve, st, 4, 3)
            source_lo(dve, 5 * KD, h, h_hi, h_lo, range(1, KD, 2))
            pass_gate(dve, 15)
            ffn_dve(dve, st, 1)
            pass_gate(dve, 16)
            final_dve(dve, st, 5)

        @block.gpsimd
        def _(pool):
            st = Steps(pool, pool_step)
            for n, e in enumerate((EPS, GN_EPS, 1e-12)):
                pool.memset(eps_c[:, n:n + 1], e).then_inc(eps_ready, 1)
            pass_gate(pool, 1)
            source_lo(pool, 0, h, h_hi, h_lo, range(0, KD, 2))
            pass_gate(pool, 2)
            ab_pool(pool, st)
            pass_gate(pool, 3)
            pass_gate(pool, 4)
            parts_pool(pool, ab["out"], KD, then=ffn[0, 0, "up"])
            pass_gate(pool, 5)
            ffn_pool(pool, 0)
            source_lo(pool, 2 * KD, h, h_hi, h_lo, range(0, KD, 2))
            pass_gate(pool, 6)
            ffn_parts_pool(pool, 0)
            pass_gate(pool, 7)
            source_lo(pool, 3 * KD, h, h1_hi, h1_lo, range(0, KD, 2))
            pass_gate(pool, 8)
            for s in range(2):
                tile_lo(pool, cd["in"], 0, s)
            parts_pool(pool, cd["in"], 18)
            pass_gate(pool, 9)
            pass_gate(pool, 10)
            shift_pool(pool, st)
            pass_gate(pool, 11)
            kk_pool(pool)
            pass_gate(pool, 12)
            scan_pool(pool, st)
            pass_gate(pool, 13)
            for s in range(2):
                tile_lo(pool, cd["out"], 0, s)
            parts_pool(pool, cd["out"], KD, then=ffn[1, 0, "up"])
            pass_gate(pool, 14)
            ffn_pool(pool, 1)
            source_lo(pool, 5 * KD, h, h_hi, h_lo, range(0, KD, 2))
            pass_gate(pool, 15)
            ffn_parts_pool(pool, 1)
            pass_gate(pool, 16)



def tile_out(w, k):
    return np.ascontiguousarray(w.reshape(k, P, -1, P).transpose(2, 1, 0, 3)).reshape(-1, P, k * P)


def tile_wide(w):
    return np.ascontiguousarray(w.reshape(KD, P, -1, 256).transpose(2, 1, 0, 3)).reshape(-1, P, KD * 256)


def cols(v):
    return np.asarray(v).reshape(-1, P).T


def constants():
    c = np.zeros((P, NCONST), np.float32)
    c[:, 0:P] = np.eye(P)
    c[:, P:2 * P] = 1
    half = np.arange(P) // HD
    c[:, 2 * P:3 * P] = half[:, None] == half[None, :]
    f = np.arange(P) % 32
    low = f < 16
    src = np.where(low, np.arange(P) + 16, np.arange(P) - 16)
    c[src, 3 * P + np.arange(P)] = np.where(low, -1, 1)
    at = 4 * P
    for m in masks():
        c[:, at:at + C] = np.tile(m, (2, 1))
        at += C
    assert at == NCONST
    return c


def rotation():
    f = np.arange(P) % 32
    inv = np.float32(10000.0) ** (-(f % 16).astype(np.float32) / np.float32(16))
    t = np.arange(LAT)
    pos = np.where(((np.arange(P) % 64) < 32)[:, None], (t // 64)[None, :], (t % 64)[None, :])
    ang = pos.astype(np.float32) * inv.astype(np.float32)[:, None]
    return np.stack([np.cos(ang), np.sin(ang)], 1).astype(np.float32)


def masks():
    i, j = np.arange(C)[:, None], np.arange(C)[None, :]
    out = [i < j, i > j, i <= j, i >= j]
    for l in range(LEVELS):
        b = 1 << l
        m = (i // (2 * b) == j // (2 * b)) & (i // b % 2 == 1) & (j // b % 2 == 0)
        out += [m, m.T]
    out = [m.astype(np.float32) for m in out]
    out[4], out[5] = -out[4], -out[5]
    return out


def kernel(**inputs):
    import concourse.bacc as bacc
    from concourse.bass_utils import run_bass_kernel_spmd

    a = {k: np.asarray(v) for k, v in inputs.items()}
    io = layout(a)
    nc = bacc.Bacc("TRN2", target_bir_lowering=False, num_devices=1)
    aps = {n: nc.dram_tensor("in_" + n, v.shape, mybir.dt.from_np(v.dtype), kind="ExternalInput").ap() for n, v in io.items()}
    for n, shape in OUTS.items():
        aps[n] = nc.dram_tensor("out_" + n, shape, F32, kind="ExternalOutput").ap()
    build(nc, aps)
    r = run_bass_kernel_spmd(nc, [{"in_" + n: v for n, v in io.items()}], core_ids=[0]).results[0]
    return unpack({n: np.asarray(r["out_" + n]) for n in OUTS})


def layout(a):
    io = {}
    io["x_fm"] = np.ascontiguousarray(np.concatenate([a["x_prompt"][0], a["x_sample"][0]], 0).T.reshape(KD, P, T).transpose(1, 0, 2))
    io["cvec"] = np.ascontiguousarray(np.stack([a["c_ctx"], a["c"][0]], 1).reshape(KD, P, 2).transpose(1, 0, 2))
    fields = {
        "norm1": a["norm1_g"], "norm2": a["norm2_g"], "final": a["final_g"], "mod_b": a["mod_b"],
        "conv_w": np.roll(a["ffn_conv_w"].reshape(DEPTH, 3, 2, FF), 1, 2),
        "conv_b": np.roll(a["ffn_conv_b"].reshape(DEPTH, 2, FF), 1, 1),
        "b_w": a["b_conv_w"][0], "b_b": a["b_conv_b"][0], "b_norm": a["b_norm_g"][0],
        "mu_r": a["c_mu_rkv"][0, 0], "mu_k": a["c_mu_rkv"][0, 1], "mu_v": a["c_mu_rkv"][0, 2],
        "mu_w": a["c_mu_wag"][0, 0], "mu_a": a["c_mu_wag"][0, 1], "mu_g": a["c_mu_wag"][0, 2],
        "w0": a["c_w0"][0], "a0": a["c_a0"][0], "k_k": a["c_k_k"][0], "k_a": a["c_k_a"][0], "r_k": a["c_r_k"][0],
        "ln_g": a["c_ln_g"][0], "ln_b": a["c_ln_b"][0],
        "qk_g": np.concatenate([np.tile(a["d_q_g"][0], 2 * KA), np.tile(a["d_k_g"][0], 4)]),
    }
    par = np.empty((P, NPAR), np.float32)
    for n, v in fields.items():
        v = cols(v)
        par[:, PAR[n]:PAR[n] + v.shape[1]] = v
    io["par"] = par
    io["const"] = constants()
    io["mod_w"] = np.concatenate([tile_wide(w) for w in a["mod_w"]])
    w = a["ab_w_in"][0]
    io["ab_v"] = tile_wide(w[:, AD:2 * AD])
    t = tile_out(w, KD)
    io["ab_w"] = np.concatenate([t[[12 + i // 2 if i % 2 == 0 else 8 + i // 2 for i in range(8)]], t[0:4]])
    io["w_out"] = np.concatenate([tile_out(w, KD) for w in a["w_out"]])
    up = [tile_out(w, KD) for w in a["ffn_up"]]
    io["ffn_up"] = np.concatenate([np.stack([u[KF:], u[:KF]], 1).reshape(2 * KF, P, KD * P) for u in up])
    io["ffn_down"] = np.concatenate([tile_out(w, KH) for v in a["ffn_down"] for w in (v[:KH * P], v[KH * P:])])
    io["ws_t"] = np.ascontiguousarray(a["a_ws"][0].transpose(2, 0, 1))
    io["v_rows"] = np.ascontiguousarray(np.broadcast_to(np.stack([a["a_vnorm_g"][0], a["a_vnorm_b"][0]])[None], (P, 2, AD)))
    io["bs_rows"] = np.ascontiguousarray(np.broadcast_to(np.tile(a["a_bs"][0], (1, NT))[None], (P, 4, T)))
    w = a["cd_w_in"][0]
    t = tile_out(w, KD)
    keys = [tile_out(np.concatenate([w[:, 2048 + HD * g:2048 + HD * (g + 1)]] * 2, 1), KD) for g in range(2)]
    lora = [np.concatenate([a["c_w1"][0, 0], a["c_w1"][0, 1]], 1), np.concatenate([a["c_a1"][0, 0], a["c_a1"][0, 1]], 1), a["c_g1"][0]]
    io["cd_w"] = np.concatenate([t[0:16]] + keys + [tile_out(v, KD) for v in lora] + [t[17:18]])
    ckv = a["cache_k"][0, 0].transpose(2, 1, 0)
    io["cache_k"] = np.ascontiguousarray(np.concatenate([ckv, ckv], 0))
    io["cache_v"] = np.ascontiguousarray(a["cache_v"][0, 0].reshape(CTX, P))
    io["rope"] = rotation()
    w2 = a["c_w2"][0].reshape(P, HP, P)
    a2 = a["c_a2"][0].reshape(P, HP, P)
    g2 = a["c_g2"][0].reshape(P, HP, P)
    io["scan_w"] = np.ascontiguousarray(np.stack([w2, a2, g2], 2).transpose(1, 0, 2, 3).reshape(HP, P, 3 * P))
    st = np.zeros((HP, 2, 2, HD, 2, HD), np.float32)
    for d, name in enumerate(("state_wkv_fwd", "state_wkv_bwd")):
        s = a[name][0, 0].reshape(HP, 2, HD, HD)
        for e in range(2):
            st[:, d, e, :, e, :] = s[:, e].transpose(0, 2, 1)
    io["state"] = st.reshape(2 * HP, P, P)
    return io


OUTS = {"y": (P, KD, T), "new_k": (HD, 2, CTX), "new_v": (CTX, P), "new_state": (2 * HP, P, P)}
NCONST = 4 * P + (4 + 2 * LEVELS) * C


def unpack(r):
    y = r["y"].transpose(1, 0, 2).reshape(D, T).T
    k = r["new_k"].transpose(2, 1, 0)[None, None]
    v = r["new_v"].reshape(1, 1, CTX, 2, HD)
    s = r["new_state"].reshape(HP, 2, 2, HD, 2, HD)
    s = np.stack([s[:, :, e, :, e, :] for e in range(2)], 2).transpose(1, 0, 2, 4, 3).reshape(2, 1, 1, HEADS, HD, HD)
    out = (y[None, :CTX], y[None, CTX:], k, v, s[0], s[1])
    return tuple(np.ascontiguousarray(o) for o in out)
```

```python
from contextlib import ExitStack

import numpy as np
import concourse.bass as bass
from concourse import mybir
from concourse.alu_op_type import AluOpType as ALU

F32 = mybir.dt.float32
F32R = mybir.dt.float32r
ACT = mybir.ActivationFunctionType
AX = mybir.AxisListType

P = 128
D = 1024
KD = D // P
CTX, LAT = 128, 512
T = CTX + LAT
NT = T // P
HALF = T // 2
DEPTH = 2
AD = 512
KA = AD // P
TAPS = 31
PAD = TAPS // 2
GLU = PAD + CTX + PAD + LAT + PAD
CONV = GLU - 2 * PAD
FF = 2816
KF = FF // P
EPS = 1e-6
GN_EPS = 64e-5
HD = 64
HP = 4
C = 64
NC = T // C
NCC = CTX // C
HEADS = 8
FFU = 1 + CTX + 1 + LAT + 1
NARROW = KD * P
KH = KF // 2
DEEP = KH * P
SLOT = DEEP + 2 * NARROW
E_HALF = float(np.exp(-0.5))
CUTS = [(0, CTX, 0), (CTX, HALF, 1), (HALF, T, 1)]
GROUPS = [(0, CTX, 0), (CTX, T, 1)]

PAR = {}


def _fields():
    at = 0
    for name, n in [("norm1", DEPTH * KD), ("norm2", DEPTH * KD), ("final", KD), ("mod_b", DEPTH * 48),
                    ("conv_w", DEPTH * 3 * 2 * KF), ("conv_b", DEPTH * 2 * KF), ("b_w", TAPS * KA), ("b_b", KA),
                    ("b_norm", KA), ("mu_r", KA), ("mu_k", KA), ("mu_v", KA), ("mu_w", KD), ("mu_a", KD),
                    ("mu_g", KD), ("w0", 2 * KA), ("a0", 2 * KA), ("k_k", KA), ("k_a", KA), ("r_k", KA),
                    ("ln_g", KA), ("ln_b", KA), ("qk_g", KA + 2)]:
        PAR[name] = at
        at += n
    return at


NPAR = _fields()
CONST = {"ident": 0, "ones": P, "head_ones": 2 * P, "rope_perm": 3 * P, "masks": 4 * P}
LEVELS = 6
ARENA = 37760
SCAN_STEPS = 49
SCAN_POOL = 12


class Steps:

    def __init__(self, eng, sem):
        self.eng, self.sem, self.n, self.turn = eng, sem, 0, None

    def __call__(self, ins):
        ins.then_inc(self.sem, 1)
        self.n += 1
        return ins

    def loop(self, i, per):
        self.turn, self.first, self.per = i, self.n, per

    def end(self, turns):
        assert self.n - self.first == self.per, (self.n - self.first, self.per)
        self.n, self.turn = self.first + self.per * turns, None

    def wait(self, but=0):
        if self.turn is None:
            self.eng.wait_ge(self.sem, self.n - but)
        else:
            self.eng.wait_ge(self.sem, self.turn * self.per + self.n - but)


def build(nc, io):
    ctx = ExitStack()
    with ctx:
        def sb(name, shape, dt=F32):
            return ctx.enter_context(nc.sbuf_tensor(name, shape, dt))

        def sem(name):
            return ctx.enter_context(nc.semaphore(name))

        x = sb("x", [P, KD, T])
        par = sb("par", [P, NPAR])
        const = sb("const", [P, io["const"].shape[1]])
        mods = [sb("mod%d" % layer, [P, 48, 2]) for layer in range(DEPTH)]
        amuls = [sb("amul%d" % layer, [P, 2, KD, 2]) for layer in range(DEPTH)]
        cvec = sb("cvec", [P, KD, 2])
        eps_c = sb("eps_c", [P, 4])
        wslot_at = -(-nc.sbuf_base // 32) * 32
        wslot = sb("wslot", [P, 2, SLOT])
        rs = sb("rs", [P, T])
        arena_at = -(-nc.sbuf_base // 32) * 32
        arena = sb("arena", [P, ARENA])
        ps = ctx.enter_context(nc.psum_tensor("ps", [P, 8, 512], F32))

        ident = const[:, 0:P]
        ones = const[:, P:2 * P]
        head_ones = const[:, 2 * P:3 * P]

        def pcol(name, n=0):
            return par[:, PAR[name] + n:PAR[name] + n + 1]

        def region(at, *shape):
            n = int(np.prod(shape))
            assert at + n <= ARENA, (at, n)
            v = arena[:, at:at + n]
            if len(shape) == 2:
                v = v.rearrange("p (a b) -> p a b", a=shape[0])
            if len(shape) == 3:
                v = v.rearrange("p (a b c) -> p a b c", a=shape[0], b=shape[1])
            return v

        def parts(name, at, *shape):
            assert at + int(np.prod(shape)) <= ARENA, name
            return nc.alloc_sbuf_tensor_at(name, [P, *shape], F32R, offset=arena_at + 4 * at)

        w_hi, w_lo = ([nc.alloc_sbuf_tensor_at("%s%d" % (name, s), [P, NARROW], F32R,
                                               offset=wslot_at + 4 * (s * SLOT + DEEP + n * NARROW)) for s in range(2)]
                      for n, name in ((0, "w_hi"), (1, "w_lo")))
        d_hi, d_lo = ([parts("%s%d" % (name, s), at + s * DEEP, DEEP) for s in range(2)]
                      for at, name in ((0, "d_hi"), (28176, "d_lo")))

        def pair(s):
            return ps[:, 2 * s:2 * s + 2, 0:HALF]

        def cut(s, a, b):
            return ps[:, 2 * s + a // HALF, a % HALF:a % HALF + b - a]

        gate = sem("gate")
        loaded = sem("loaded")
        w_in = [sem("w_in0"), sem("w_in1")]
        product = sem("product")
        hi_ready = sem("hi_ready")
        lo_ready = sem("lo_ready")
        src_hi = sem("src_hi")
        src_lo = {"dve": sem("src_lo_dve"), "pool": sem("src_lo_pool")}
        drained = [sem("drained0"), sem("drained1")]
        act_step, dve_step, pool_step = sem("act_step"), sem("dve_step"), sem("pool_step")
        out_done = sem("out_done")

        tiles = []
        split_pairs = {}
        tile_cols = {}

        def stream(dram, first, n, cols, split=False):
            base = sum(t[2] for t in tiles) // 2
            split_pairs[base] = sum(t[2] for t in tiles if t[4]) // 2
            tile_cols[base] = cols
            tiles.append((dram, first, n, cols, split))
            return base

        def take(pe, base, i, s):
            pe.wait_ge(w_in[s], i * 16 + 16 * (base + 1))
            pe.wait_ge(drained[s], i + base + 1)

        def have(eng, base, i, s):
            eng.wait_ge(product, i * 2 + 2 * base + s + 1)

        def tile_parts(base, s):
            return (d_hi[s], d_lo[s]) if tile_cols[base] == DEEP else (w_hi[s], w_lo[s])

        def product_of_parts(base, s, ks, k_all, hi, lo):
            wh, wl = tile_parts(base, s)
            for h in range(2):
                for kk in ks:
                    m = slice(kk * P, (kk + 1) * P)
                    t = slice(h * HALF, (h + 1) * HALF)
                    out = ps[:, 2 * s + h, 0:HALF]
                    nc.tensor.matmul(out, wh[:, m], hi[:, kk, t], start=(kk == 0), stop=False)
                    nc.tensor.matmul(out, wh[:, m], lo[:, kk, t], start=False, stop=False)
                    last = nc.tensor.matmul(out, wl[:, m], hi[:, kk, t], start=False, stop=(kk == k_all - 1))
            return last

        def take_parts(pe, base, i, s):
            pe.wait_ge(lo_ready, i * 2 + (2 * split_pairs[base] + s + 1))
            pe.wait_ge(drained[s], i + base + 1)

        def first_product(pe, base, k, hi, lo, chunk):
            take_parts(pe, base, 0, 0)
            for kk in range(k):
                chunk(kk)
                last = product_of_parts(base, 0, [kk], k, hi, lo)
            last.then_inc(product, 1)

        def project_parts_pe(pe, base, n, k, hi, lo, chunk=None):
            if chunk:
                first_product(pe, base, k, hi, lo, chunk)
                take_parts(pe, base, 0, 1)
                product_of_parts(base, 1, range(k), k, hi, lo).then_inc(product, 1)
            with pe.Fori(1 if chunk else 0, n // 2) as i:
                for s in range(2):
                    take_parts(pe, base, i, s)
                    product_of_parts(base, s, range(k), k, hi, lo).then_inc(product, 1)

        def tile_hi(act, base, i, s):
            act.wait_ge(w_in[s], i * 16 + 16 * (base + 1))
            act.wait_ge(product, i * 2 + (2 * base + s - 1))
            nc.scalar.activation(tile_parts(base, s)[0][:, :], wslot[:, s, 0:tile_cols[base]], ACT.Copy).then_inc(hi_ready, 1)

        def tile_lo(pool, base, i, s):
            wh, wl = tile_parts(base, s)
            pool.wait_ge(hi_ready, i * 2 + (2 * split_pairs[base] + s + 1))
            pool.tensor_tensor(wl[:, :], wslot[:, s, 0:tile_cols[base]], wh[:, :], ALU.subtract).then_inc(lo_ready, 1)

        def parts_act(act, base, n, use=None, then=None, st=None, per=0):
            with act.Fori(0, n // 2 - 1) as i:
                if st:
                    st.loop(i, per)
                for s in range(2):
                    tile_hi(act, base, i + 1, s)
                    if use:
                        use(i, s)
                if st:
                    st.end(n // 2 - 1)
            for s in range(2):
                if then is not None:
                    tile_hi(act, then, 0, s)
                if use:
                    use(n // 2 - 1, s)

        def parts_pool(pool, base, n, then=None, use=None):
            with pool.Fori(0, n // 2 - 1) as i:
                for s in range(2):
                    tile_lo(pool, base, i + 1, s)
                if use:
                    use(i)
            if then is not None:
                for s in range(2):
                    tile_lo(pool, then, 0, s)
            if use:
                use(n // 2 - 1)

        h = region(0, KD, T)
        sq = region(5120, KD, T)
        u = region(10240, KA, T)
        vtm = region(12800, NT, AD)
        glu = region(15360, KA, GLU)
        conv = region(18100, KA, CONV)
        ycat = region(20720, KD, T)
        wsT = region(25840, 4, P)
        vrow = region(26352, 2, AD)
        bsrow = region(27376, 4, T)
        sg = region(29936, T)
        lnst = region(30576, NT, 6)
        lnmv = region(30606, NT, 2)
        hid_hi, hid_lo = parts("hid_hi", 10240, KH, T), parts("hid_lo", 17280, KH, T)
        up = region(24320, 2, FFU)
        hid = region(27530, T)
        yv = region(25606, 2, FFU - 2)
        sil = region(26888, FFU - 2)
        h_hi, h_lo = parts("h_hi", 5120, KD, T), parts("h_lo", 31360, KD, T)
        h1_hi, h1_lo = parts("h1_hi", 21760, KD, T), parts("h1_lo", 32000, KD, T)
        y_hi, y_lo = parts("y_hi", 0, KD, T), parts("y_lo", 31360, KD, T)
        y1_hi, y1_lo = parts("y1_hi", 5120, KD, T), parts("y1_lo", 0, KD, T)
        mrow = region(31360, 48 * P)

        MOD_TILES = 24
        MOD_SLOTS = 4
        mod_ring = [region(at, MOD_SLOTS, KD * 256) for at in (10240, 0)]
        mod_in = [sem("mod_in%d" % s) for s in range(MOD_SLOTS)]
        mod_used, mod_read = sem("mod_used"), sem("mod_read")

        def modulation_first_sp(sp, layer):
            for s in range(MOD_SLOTS):
                sp.dma_start(mod_ring[layer][:, s, :], io["mod_w"][MOD_TILES * layer + s]).then_inc(mod_in[s], 16)

        def modulation_rest_sp(sp, layer):
            first = MOD_TILES * layer
            with sp.Fori(1, MOD_TILES // MOD_SLOTS) as i:
                for s in range(MOD_SLOTS):
                    sp.wait_ge(mod_used, i * MOD_SLOTS + (first + s + 1 - MOD_SLOTS))
                    sp.dma_start(mod_ring[layer][:, s, :], io["mod_w"][i * MOD_SLOTS + (first + s)]).then_inc(mod_in[s], 16)

        MOD_TURNS = MOD_TILES // MOD_SLOTS

        def modulation_tiles_pe(pe, layer, begin, end):
            first = MOD_TILES * layer
            with pe.Fori(begin, end) as i:
                for s in range(MOD_SLOTS):
                    pe.wait_ge(mod_in[s], i * 16 + (16 * first // MOD_SLOTS + 16))
                    pe.wait_ge(mod_read, i * MOD_SLOTS + (first + s + 1))
                    w = mod_ring[layer][:, s, :].rearrange("p (k m) -> p k m", k=KD)
                    for k in range(KD):
                        last = nc.tensor.matmul(ps[0:2, s, 0:256], cvec[:, k, :], w[:, k, :],
                                                start=(k == 0), stop=(k == KD - 1))
                    last.then_inc(mod_used, 1)

        def modulation_columns_pe(pe, layer):
            pe.wait_ge(mrow_ready, layer + 1)
            for j in range(48):
                last = nc.tensor.transpose(ps[:, 1, 2 * j:2 * j + 2], mrow[0:2, j * P:(j + 1) * P], ident[0:2, 0:2])
            last.then_inc(mcol_ready, 1)

        def modulation_act(act, layer, begin, end):
            first = MOD_TILES * layer
            with act.Fori(begin, end) as i:
                for s in range(MOD_SLOTS):
                    act.wait_ge(mod_used, i * MOD_SLOTS + (first + s + 1))
                    nc.scalar.activation(mrow[0:2, bass.ds(i * (256 * MOD_SLOTS) + s * 256, 256)], ps[0:2, s, 0:256],
                                         ACT.Copy).then_inc(mod_read, 1)
            if end == MOD_TURNS:
                act.drain().then_inc(mrow_ready, 1)

        def modulation_dve(dve, st, layer):
            dve.wait_ge(mcol_ready, layer + 1)
            mod, amul = mods[layer], amuls[layer]
            cols = ps[:, 1, 0:96].rearrange("p (j v) -> p j v", v=2)
            bias = par[:, PAR["mod_b"] + 48 * layer:PAR["mod_b"] + 48 * (layer + 1)]
            for v in range(2):
                st(nc.vector.tensor_tensor(mod[:, :, v], cols[:, :, v], bias, ALU.add))
            st.wait()
            for n, (name, at) in enumerate([("norm1", KD), ("norm2", 4 * KD)]):
                g = par[:, PAR[name] + KD * layer:PAR[name] + KD * (layer + 1)]
                for v in range(2):
                    st(nc.vector.scalar_tensor_tensor(out=amul[:, n, :, v], in0=mod[:, at:at + KD, v], scalar=1.0,
                                                      in1=g, op0=ALU.add, op1=ALU.mult))

        silu_ready, eps_ready = sem("silu_ready"), sem("eps_ready")
        mrow_ready, mcol_ready = sem("mrow_ready"), sem("mcol_ready")

        sq_ready, sum_ready, root_ready = sem("sq_ready"), sem("sum_ready"), sem("root_ready")
        xn_ready = sem("xn_ready")

        def warm(act, f):
            nc.scalar.activation(eps_c[:, 3:4], eps_c[:, 0:1], f)

        def squares_act(act, squares):
            for o, a in squares:
                last = nc.scalar.activation(o, a, ACT.Square)
            last.then_inc(sq_ready, 1)

        def root_act(act, turn, n, eps):
            warm(act, ACT.Sqrt)
            act.wait_ge(sum_ready, turn + 1)
            nc.scalar.activation(rs[:, :].rearrange("p (a b) -> p a b", a=2), pair(2), ACT.Sqrt, bias=eps_c[:, eps:eps + 1],
                                 scale=1.0 / (n * P)).then_inc(root_ready, 1)

        x_sq = region(36480, 2, T)
        x_squared = sem("x_squared")

        def square_of_x(act, base, i, s):
            act.wait_ge(drained[s], i + (base + 2))
            nc.scalar.activation(x_sq[:, s, :], x[:, i * 2 + s, :], ACT.Square).then_inc(x_squared, 1)

        def sum_of_x(pe, turn, i, s):
            pe.wait_ge(x_squared, i * 2 + (KD * turn + s + 1))
            for h in range(2):
                last = nc.tensor.matmul(ps[:, 4 + h, 0:HALF], ones, x_sq[:, s, h * HALF:(h + 1) * HALF],
                                        start=isinstance(i, int) and i == 0 and s == 0,
                                        stop=isinstance(i, int) and i == KD // 2 - 1 and s == 1)
            return last

        def last_product_pe(pe, base, k, hi, lo, turn, chunk):
            def tile(i, s):
                take_parts(pe, base, i, s)
                product_of_parts(base, s, range(k), k, hi, lo).then_inc(product, 1)

            first_product(pe, base, k, hi, lo, chunk)
            tile(0, 1)
            for s in range(2):
                sum_of_x(pe, turn, 0, s)
                tile(1, s)
            with pe.Fori(2, KD // 2) as i:
                for s in range(2):
                    sum_of_x(pe, turn, i - 1, s)
                    tile(i, s)
            for s in range(2):
                last = sum_of_x(pe, turn, KD // 2 - 1, s)
            last.then_inc(sum_ready, 1)

        def rms_pe(pe, turn, n):
            pe.wait_ge(sq_ready, turn + 1)
            for hh in range(2):
                for k in range(n):
                    last = nc.tensor.matmul(ps[:, 4 + hh, 0:HALF], ones, sq[:, k, hh * HALF:(hh + 1) * HALF],
                                            start=(k == 0), stop=(k == n - 1))
            last.then_inc(sum_ready, 1)

        def rms_dve(dve, st, turn):
            dve.wait_ge(root_ready, turn + 1)
            st(nc.vector.reciprocal(rs[:, :], rs[:, :]))
            st.wait()

        BY_ACT = (2, 4, 6)
        BY_POOL = 5
        BY_DVE = tuple(k for k in range(KD) if k not in BY_ACT)
        h_dve, h_act = sem("h_dve"), sem("h_act")

        def adaln_act(act, turn, n, hi):
            mod, amul = mods[turn // 2], amuls[turn // 2]
            for k in range(KD):
                if k in BY_ACT:
                    at = len(BY_ACT) * turn + BY_ACT.index(k) + 1
                    act.wait_ge(xn_ready, at)
                    for a, b, v in GROUPS:
                        last = nc.scalar.activation(h[:, k, a:b], h[:, k, a:b], ACT.Identity, scale=amul[:, n, k, v:v + 1],
                                                    bias=mod[:, 3 * KD * n + k, v:v + 1])
                    last.then_inc(h_act, 1)
                    act.wait_ge(h_act, at)
                else:
                    act.wait_ge(h_dve, len(BY_DVE) * turn + BY_DVE.index(k) + 1)
                nc.scalar.activation(hi[:, k, :], h[:, k, :], ACT.Copy).then_inc(src_hi, 1)

        def chunk_of_h(pe, turn):
            before = (KD - BY_POOL) * turn + KD * ((turn + 1) // 2)

            def chunk(kk):
                if kk < BY_POOL:
                    pe.wait_ge(src_lo["pool"], BY_POOL * turn + kk + 1)
                else:
                    pe.wait_ge(src_lo["dve"], before + kk - BY_POOL + 1)
            return chunk

        def chunk_of_ycat(pe, layer):
            before = (KD - BY_POOL) * (2 * layer + 1) + KD * layer
            return lambda kk: pe.wait_ge(src_lo["dve"], before + kk + 1)

        def source_hi(act, a, hi, ks):
            for k in ks:
                nc.scalar.activation(hi[:, k, :], a[:, k, :], ACT.Copy).then_inc(src_hi, 1)

        def source_lo(eng, who, turn, a, hi, lo, ks):
            for k in ks:
                eng.wait_ge(src_hi, turn + k + 1)
                eng.tensor_tensor(lo[:, k, :], a[:, k, :], hi[:, k, :], ALU.subtract).then_inc(src_lo[who], 1)

        def normed_dve(dve, st, k):
            ins = nc.vector.tensor_tensor(h[:, k, :], x[:, k, :], rs[:, :], ALU.mult)
            if k in BY_ACT:
                ins.then_inc(xn_ready, 1)
            else:
                st(ins)

        def adaln_dve(dve, st, turn, n, normed=False):
            mod, amul = mods[turn // 2], amuls[turn // 2]
            for k in range(KD + 1):
                if k < KD and not normed:
                    normed_dve(dve, st, k)
                if k - 1 in BY_DVE:
                    st.wait(but=1 if k in BY_DVE and not normed else 0)
                    for a, b, v in GROUPS:
                        last = nc.vector.tensor_scalar(h[:, k - 1, a:b], h[:, k - 1, a:b], amul[:, n, k - 1, v:v + 1],
                                                       mod[:, 3 * KD * n + k - 1, v:v + 1], ALU.mult, ALU.add)
                    last.then_inc(h_dve, 1)

        def residual_dve(dve, base, at):
            mod = mods[0 if base < cd["in"] else 1]
            with dve.Fori(0, KD // 2) as i:
                for s in range(2):
                    have(dve, base, i, s)
                    for n, (a, b, v) in enumerate(CUTS):
                        last = nc.vector.scalar_tensor_tensor(
                            out=x[:, i * 2 + s, a:b], in0=cut(s, a, b), scalar=mod[:, i * 2 + (at + s), v:v + 1],
                            in1=x[:, i * 2 + s, a:b], op0=ALU.mult, op1=ALU.add)
                    last.then_inc(drained[s], 1)

        sg_ready, sg_used = sem("sg_ready"), sem("sg_used")
        vtm_ready, vmul_ready, vln_ready, std_ready = sem("vtm_ready"), sem("vmul_ready"), sem("vln_ready"), sem("std_ready")
        var_ready, glu_ready, conv_ready, mix_ready = sem("var_ready"), sem("glu_ready"), sem("conv_ready"), sem("mix_ready")
        mix_used, yn_ready, pads_ready, u_ready = sem("mix_used"), sem("yn_ready"), sem("pads_ready"), sem("u_ready")
        ab = {}

        def ab_tiles():
            ab["v"] = stream(io["ab_v"], 0, 2, KD * 256)
            ab["glu"] = stream(io["ab_w"], 0, 8, NARROW, split=True)
            ab["u"] = stream(io["ab_w"], 8, 4, NARROW, split=True)
            ab["out"] = stream(io["w_out"], 0, KD, NARROW, split=True)

        def ab_pe(pe):
            for s in range(2):
                pe.wait_ge(w_in[s], 16 * (ab["v"] + 1))
                w = wslot[:, s, 0:KD * 256].rearrange("p (k m) -> p k m", k=KD)
                for t in range(NT):
                    for k in range(KD):
                        last = nc.tensor.matmul(ps[:, 3 + t, s * 256:(s + 1) * 256], h[:, k, t * P:(t + 1) * P], w[:, k, :],
                                                start=(k == 0), stop=(k == KD - 1), skip_group_check=True)
                last.then_inc(product, 1)
            pe.sem_inc(drained[0], 1)
            pe.sem_inc(drained[1], 1)
            pe.wait_ge(vtm_ready, 1)
            project_parts_pe(pe, ab["glu"], 8, KD, h_hi, h_lo)
            project_parts_pe(pe, ab["u"], 4, KD, h_hi, h_lo)
            pe.wait_ge(vln_ready, NT)
            for g in range(4):
                if g == 2:
                    for s in range(2):
                        pe.wait_ge(drained[s], ab["out"] + 1)
                    modulation_tiles_pe(pe, 1, 0, MOD_TURNS - 1)
                if g >= 2:
                    pe.wait_ge(mix_used, g - 1)
                for t in range(NT):
                    at = (4 + 2 * (g % 2)) * 512 + t * P
                    last = nc.tensor.matmul(ps[:, at // 512, at % 512:at % 512 + P], vtm[:, t, g * P:(g + 1) * P],
                                            wsT[:, g, :], start=True, stop=True)
                last.then_inc(mix_ready, 1)
            modulation_tiles_pe(pe, 1, MOD_TURNS - 1, MOD_TURNS)
            modulation_columns_pe(pe, 1)

        def ab_act(act, st):
            tile_hi(act, ab["glu"], 0, 0)
            for t in range(NT):
                if t == 0:
                    act.wait_ge(product, 2 * ab["v"] + 2)
                nc.scalar.activation(vtm[:, t, :], ps[:, 3 + t, :], ACT.Gelu_apprx_tanh).then_inc(vtm_ready, 1)
            tile_hi(act, ab["glu"], 0, 1)
            act.wait_ge(var_ready, 1)
            nc.scalar.activation(lnmv[:, :, 1], lnmv[:, :, 1], ACT.Sqrt, bias=eps_c[:, 0:1]).then_inc(std_ready, 1)

            def gate_of_glu(i, s):
                if s == 0:
                    have(act, ab["glu"], i, 0)
                    act.wait_ge(sg_used, i + 1)
                    nc.scalar.activation(sg.rearrange("p (a b) -> p a b", a=2), pair(0), ACT.Sigmoid).then_inc(sg_ready, 1)

            def gelu_of_u(i, s):
                have(act, ab["u"], i, s)
                nc.scalar.activation(u[:, i * 2 + s, :].rearrange("p (a b) -> p a b", a=2), pair(s),
                                     ACT.Gelu_apprx_tanh).then_inc(drained[s], 1)

            warm(act, ACT.Sigmoid)
            parts_act(act, ab["glu"], 8, gate_of_glu, then=ab["u"])
            warm(act, ACT.Gelu_apprx_tanh)
            parts_act(act, ab["u"], 4, gelu_of_u)
            act.drain().then_inc(u_ready, 1)
            for s in range(2):
                tile_hi(act, ab["out"], 0, s)
            modulation_act(act, 1, 0, MOD_TURNS)

        def ab_dve(dve, st):
            dve.sem_inc(sg_used, 1)
            for t in range(NT):
                dve.wait_ge(vtm_ready, t + 1)
                st(nc.vector.bn_stats(lnst[:, t, :], vtm[:, t, :]))
            st.wait()
            for t in range(NT):
                last = st(nc.vector.bn_aggr(lnmv[:, t, :], lnst[:, t, :]))
            st.wait()
            dve.sem_inc(var_ready, 1)
            dve.wait_ge(std_ready, 1)
            st(nc.vector.reciprocal(lnmv[:, :, 1], lnmv[:, :, 1]))
            st.wait()
            for t in range(NT):
                nc.vector.tensor_scalar(vtm[:, t, :], vtm[:, t, :], lnmv[:, t, 0:1], lnmv[:, t, 1:2], ALU.subtract,
                                        ALU.mult).then_inc(vmul_ready, 1)
            dve.wait_ge(pads_ready, 1)
            with dve.Fori(0, 4) as i:
                have(dve, ab["glu"], i, 1)
                dve.wait_ge(sg_ready, i + 1)
                dve.sem_inc(drained[0], 1)
                for a, b, v in CUTS:
                    o = PAD + a + PAD * v
                    last = nc.vector.tensor_tensor(glu[:, i, o:o + b - a], cut(1, a, b), sg[:, a:b], ALU.mult)
                last.then_inc(glu_ready, 1)
                dve.wait_ge(glu_ready, i + 1)
                dve.sem_inc(drained[1], 1)
                dve.sem_inc(sg_used, 1)
            for k in range(KA):
                st(nc.vector.tensor_scalar(conv[:, k, :], glu[:, k, 0:CONV], pcol("b_w", k), pcol("b_b", k), ALU.mult,
                                           ALU.add))
            with dve.Fori(0, TAPS - 1) as i:
                st.loop(i, KA)
                for k in range(KA):
                    st.wait(but=KA - 1)
                    st(nc.vector.scalar_tensor_tensor(
                        out=conv[:, k, :], in0=glu[:, k, bass.ds(i + 1, CONV)],
                        scalar=par[:, bass.ds(i * KA + (PAR["b_w"] + KA + k), 1)], in1=conv[:, k, :], op0=ALU.mult, op1=ALU.add))
                st.end(TAPS - 1)
            st.wait()
            dve.sem_inc(conv_ready, 1)
            dve.wait_ge(u_ready, 1)
            for g in range(4):
                dve.wait_ge(mix_ready, g + 1)
                mixed = ps[:, 4 + 2 * (g % 2):6 + 2 * (g % 2), :].rearrange("p a b -> p (a b)")[:, 0:T]
                st(nc.vector.tensor_tensor(ycat[:, g, :], mixed, bsrow[:, g, :], ALU.add))
                st.wait()
                dve.sem_inc(mix_used, 1)
                st(nc.vector.tensor_tensor(ycat[:, g, :], ycat[:, g, :], u[:, g, :], ALU.mult))
            modulation_dve(dve, st, 1)

        def ab_pool(pool, st):
            pool.memset(glu[:, :, :], 0.0).then_inc(pads_ready, 1)
            for s in range(2):
                tile_lo(pool, ab["glu"], 0, s)
            for t in range(NT):
                pool.wait_ge(vmul_ready, t + 1)
                st(pool.tensor_tensor(vtm[:, t, :], vtm[:, t, :], vrow[:, 0, :], ALU.mult))
                st.wait()
                pool.tensor_tensor(vtm[:, t, :], vtm[:, t, :], vrow[:, 1, :], ALU.add).then_inc(vln_ready, 1)
            parts_pool(pool, ab["glu"], 8, then=ab["u"])
            parts_pool(pool, ab["u"], 4)
            for s in range(2):
                tile_lo(pool, ab["out"], 0, s)

        yb_ready = sem("yb_ready")

        def yb_act(act, st, turn):
            act.wait_ge(conv_ready, 1)
            source_hi(act, ycat, y_hi, range(KA))
            squares_act(act, [(sq[:, k, a:b], conv[:, k, a + PAD * v:b + PAD * v]) for k in range(KA) for a, b, v in GROUPS])
            root_act(act, turn, KA, 0)
            for k in range(KA):
                act.wait_ge(yn_ready, k + 1)
                nc.scalar.activation(ycat[:, KA + k, :], ycat[:, KA + k, :], ACT.Silu,
                                     scale=pcol("b_norm", k)).then_inc(yb_ready, 1)
                act.wait_ge(yb_ready, k + 1)
                nc.scalar.activation(y_hi[:, KA + k, :], ycat[:, KA + k, :], ACT.Copy).then_inc(src_hi, 1)

        def yb_dve(dve, st, turn):
            source_lo(dve, "dve", KD, ycat, y_hi, y_lo, range(KA))
            rms_dve(dve, st, turn)
            for k in range(KA):
                for a, b, v in GROUPS:
                    last = nc.vector.tensor_tensor(ycat[:, KA + k, a:b], conv[:, k, a + PAD * v:b + PAD * v], rs[:, a:b], ALU.mult)
                last.then_inc(yn_ready, 1)
            source_lo(dve, "dve", KD, ycat, y_hi, y_lo, range(KA, KD))

        mid_ready, tap_ready, sil_ready = sem("mid_ready"), sem("tap_ready"), sem("sil_ready")
        hid_ready = sem("hid_ready")
        hid_parts = sem("hid_parts")
        ffn = {}

        def ffn_tiles(layer):
            for half in range(2):
                ffn[layer, half, "up"] = stream(io["ffn_up"], 2 * (KF * layer + KH * half), 2 * KH, NARROW, split=True)
                ffn[layer, half, "down"] = stream(io["ffn_down"], KD * (2 * layer + half), KD, DEEP, split=True)

        def after_ffn_half(layer, half):
            return ffn[layer, 1, "up"] if half == 0 else None

        def ffn_pe(pe, layer):
            for half in range(2):
                project_parts_pe(pe, ffn[layer, half, "up"], 2 * KH, KD, h_hi, h_lo,
                                 chunk=chunk_of_h(pe, 2 * layer + 1) if half == 0 else None)
                done = KF * layer + KH * (half + 1) + 1

                def chunk(kk):
                    pe.wait_ge(hid_parts, done - KH + kk + 1)

                if half == 0:
                    project_parts_pe(pe, ffn[layer, half, "down"], KD, KH, hid_hi, hid_lo, chunk=chunk)
                else:
                    last_product_pe(pe, ffn[layer, half, "down"], KH, hid_hi, hid_lo, 2 * layer + 1, chunk)

        def ffn_act(act, st, layer):
            warm(act, ACT.Silu)
            for half in range(2):
                base, n0 = ffn[layer, half, "up"], KF * layer + KH * half
                cw, cb = PAR["conv_w"] + 6 * KF * layer + KH * half, PAR["conv_b"] + 2 * KF * layer + KH * half

                def use(i, s):
                    have(act, base, i, s)
                    act.wait_ge(hid_ready, i + (n0 + 1))
                    for a, b, v in CUTS:
                        last = nc.scalar.activation(up[:, s, 1 + a + v:1 + b + v], cut(s, a, b), ACT.Copy)
                    st(last)
                    st.wait()
                    act.sem_inc(drained[s], 1)
                    nc.scalar.activation(yv[:, s, :], up[:, s, 1:FFU - 1], ACT.Identity,
                                         scale=par[:, bass.ds(i + (cw + 2 * KF + s * KF), 1)],
                                         bias=par[:, bass.ds(i + (cb + s * KF), 1)]).then_inc(mid_ready, 1)
                    if s == 1:
                        act.wait_ge(tap_ready, i * 2 + (2 * n0 + 1))
                        nc.scalar.activation(sil, yv[:, 0, :], ACT.Silu).then_inc(sil_ready, 1)

                parts_act(act, base, 2 * KH, use, then=ffn[layer, half, "down"], st=st, per=2)
                down = ffn[layer, half, "down"]
                parts_act(act, down, KD, then=after_ffn_half(layer, half),
                          use=(lambda i, s: square_of_x(act, down, i, s)) if half == 1 else None)

        def ffn_dve(dve, st, layer):
            if layer == 0:
                dve.sem_inc(hid_ready, 1)
                dve.sem_inc(hid_parts, 1)
            for half in range(2):
                n0 = KF * layer + KH * half
                cw = PAR["conv_w"] + 6 * KF * layer + KH * half
                if half == 1:
                    dve.wait_ge(product, 2 * ffn[layer, 0, "down"] + KD)
                with dve.Fori(0, KH) as i:
                    st.loop(i, 2)
                    for s in range(2):
                        dve.wait_ge(mid_ready, i * 2 + (2 * n0 + s + 1))
                        st(nc.vector.scalar_tensor_tensor(out=yv[:, s, :], in0=up[:, s, 0:FFU - 2],
                                                          scalar=par[:, bass.ds(i + (cw + s * KF), 1)], in1=yv[:, s, :],
                                                          op0=ALU.mult, op1=ALU.add))
                        st.wait()
                        nc.vector.scalar_tensor_tensor(out=yv[:, s, :], in0=up[:, s, 2:FFU],
                                                       scalar=par[:, bass.ds(i + (cw + 4 * KF + s * KF), 1)], in1=yv[:, s, :],
                                                       op0=ALU.mult, op1=ALU.add).then_inc(tap_ready, 1)
                    st.end(KH)
                    dve.wait_ge(sil_ready, i + (n0 + 1))
                    dve.wait_ge(tap_ready, i * 2 + (2 * n0 + 2))
                    dve.wait_ge(hid_parts, i + (n0 + 1))
                    for out in (hid_hi[:, i, :], hid):
                        for a, b, v in GROUPS:
                            last = nc.vector.tensor_tensor(out[:, a:b], sil[:, a + v:b + v], yv[:, 1, a + v:b + v], ALU.mult)
                    last.then_inc(hid_ready, 1)
                residual_dve(dve, ffn[layer, half, "down"], 5 * KD)

        def ffn_parts_pool(pool, layer):
            for half in range(2):
                n0 = KF * layer + KH * half

                def low_of_hid(i):
                    pool.wait_ge(hid_ready, i + (n0 + 2))
                    pool.tensor_tensor(hid_lo[:, i, :], hid, hid_hi[:, i, :], ALU.subtract).then_inc(hid_parts, 1)

                parts_pool(pool, ffn[layer, half, "up"], 2 * KH, then=ffn[layer, half, "down"], use=low_of_hid)
                parts_pool(pool, ffn[layer, half, "down"], KD, then=after_ffn_half(layer, half))

        def ffn_pool(pool, layer):
            for at in (0, 1 + CTX, FFU - 1):
                last = pool.memset(up[:, :, at:at + 1], 0.0)


        rkvq = region(5120, 18, T)
        rkv, qk = rkvq[:, 0:12, :], rkvq[:, 12:18, :]
        dh = region(16640, KD, T)
        ycat1 = region(0, KD, T)
        xmix = [region(26880, KD, T), region(21760, KD, T)]
        lw, la, lg = region(32000, T), region(32640, T), region(33280, T)
        vd = region(33920, NT, P)
        ck = region(34560, 2, P)
        cv = region(34816, P)
        rope = region(16640, 2, LAT)
        hsq, hrs = ([region(at + n * T, T) for n in range(2)] for at in (34944, 36224))
        rtmp = region(18304, LAT)
        ksq = [region(21760 + n * T, T) for n in range(KA)]
        krs = [ycat1[:, n, :] for n in range(KA)]
        prob = region(18944, 3, T)
        probT = region(20864, 2, NT, LAT)
        probC = region(25984, 2, P)
        qs = region(26240, T)
        srow = region(26880, 3, 3)
        shift = region(26912, KA, T)
        kk = region(12800, KA, T)
        U_AT = [15360 + 1280 * n for n in range(13)] + [33920, 35200]
        mats = {n: region(U_AT[j], NC, P) for n, j in
                (("A", 0), ("B", 1), ("K", 2), ("R", 3), ("MT", 4), ("Vb", 4), ("PT", 5), ("NT", 6), ("At", 7), ("AH", 7),
                 ("Bt", 8), ("Kt", 9), ("Vt", 10), ("QT", 11), ("X", 12), ("NV", 12), ("XT", 13), ("Y", 14), ("UV", 14))}
        bacc = wslot[:, 0, NARROW:NARROW + T]
        stage = wslot[:, 0, NARROW + T:NARROW + T + 2 * P]
        stage_g = wslot[:, 0, NARROW + T + 2 * P:NARROW + T + 3 * P]
        state = wslot[:, 0, NARROW + T + 3 * P:NARROW + T + 7 * P].rearrange("p (g b m) -> p g b m", g=2, b=2)
        ubuf = wslot[:, 0, NARROW + T + 7 * P:NARROW + T + 9 * P].rearrange("p (b m) -> p b m", b=2)
        wbuf, abuf = region(36480, T), region(37120, T)
        gbuf = wslot[:, 0, NARROW + T + 9 * P:NARROW + 2 * T + 9 * P]
        e2buf, kdbuf = (wslot[:, 1, NARROW + T + 32 + n * T:NARROW + 2 * T + 32 + n * T] for n in range(2))
        sgbuf = wslot[:, 1, NARROW + 3 * T + 32:NARROW + 3 * T + 32 + P]
        mask01 = wslot[:, 1, NARROW:NARROW + T]
        gend = wslot[:, 1, NARROW + T:NARROW + T + 16][:, 0:NC]
        halves = wslot[:, 1, NARROW + T + 16:NARROW + T + 16 + 4 * KA].rearrange("p (n k) -> p n k", n=2)

        cd = {}
        xmix_ready, vd_ready = sem("xmix_ready"), sem("vd_ready")

        def cd_tiles():
            cd["in"] = stream(io["cd_w"], 0, 18, NARROW, split=True)
            cd["lora"] = stream(io["cd_w"], 18, 4, KD * P)
            cd["out"] = stream(io["w_out"], KD, KD, NARROW, split=True)

        def cd_pe(pe):
            project_parts_pe(pe, cd["in"], 18, KD, h1_hi, h1_lo, chunk=chunk_of_h(pe, 2))
            qk_sums_pe(pe, 0)
            for j, (i, s) in enumerate([(0, 0), (0, 1), (1, 0)]):
                qk_sums_pe(pe, j + 1)
                pe.wait_ge(xmix_ready, j + 1)
                take(pe, cd["lora"], i, s)
                w = wslot[:, s, 0:KD * P].rearrange("p (k m) -> p k m", k=KD)
                for hh in range(2):
                    for k in range(KD):
                        last = nc.tensor.matmul(ps[:, 2 * s + hh, 0:HALF], w[:, k, :],
                                                xmix[j % 2][:, k, hh * HALF:(hh + 1) * HALF], start=(k == 0), stop=(k == KD - 1))
                last.then_inc(product, 1)
            for n in range(4, NQ):
                qk_sums_pe(pe, n)
            pe.wait_ge(hroot_ready, NQ - 1)
            pe.wait_ge(w_in[1], 16 * (cd["lora"] + 2))
            w = wslot[:, 1, 0:KD * P].rearrange("p (k m) -> p k m", k=KD)
            for t in range(NT):
                for k in range(KD):
                    last = nc.tensor.matmul(ps[:, 4 + t // 4, t % 4 * P:(t % 4 + 1) * P], h[:, k, t * P:(t + 1) * P],
                                            w[:, k, :], start=(k == 0), stop=(k == KD - 1))
            last.then_inc(product, 1)
            pe.sem_inc(drained[1], 1)

        def cd_act(act):
            def use(i, s):
                have(act, cd["in"], i, s)
                nc.scalar.activation(rkvq[:, i * 2 + s, :].rearrange("p (a b) -> p a b", a=2), pair(s),
                                     ACT.Copy).then_inc(drained[s], 1)

            parts_act(act, cd["in"], 18, use)
            qk_square_act(act, 0)
            qk_root_act(act, 0)
            for n, i, s, dst, f in ((1, 0, 0, lw, ACT.Tanh), (2, 0, 1, la, ACT.Copy), (3, 1, 0, lg, ACT.Sigmoid)):
                qk_square_act(act, n)
                qk_root_act(act, n)
                have(act, cd["lora"], i, s)
                nc.scalar.activation(dst.rearrange("p (a b) -> p a b", a=2), pair(s), f).then_inc(drained[s], 1)
            for n in range(4, NQ):
                qk_square_act(act, n)
                qk_root_act(act, n)
            have(act, cd["lora"], 1, 1)
            nc.scalar.activation(vd.rearrange("p t m -> p (t m)"),
                                 ps[:, 4:6, :].rearrange("p a b -> p (a b)")[:, 0:T], ACT.Copy).then_inc(vd_ready, 1)

        def shift_sum(eng, st, out, a):
            n = a.shape[1]
            st(eng.tensor_tensor(out[:, :, 1:T - 1], a[:, :, 0:T - 2], a[:, :, 2:T], ALU.add))
            st.wait()
            for c in range(n):
                st(eng.tensor_copy(out[:, c, 0:CTX + 1:CTX], a[:, c, 1:CTX + 2:CTX]))
                st(eng.tensor_copy(out[:, c, CTX - 1:T:LAT], a[:, c, CTX - 2:T - 1:LAT]))
            st.wait()

        def cd_dve(dve, st):
            shift_sum(dve, st, dh, h)
            st(nc.vector.scalar_tensor_tensor(out=dh[:, :, :], in0=dh[:, :, :], scalar=0.5, in1=h[:, :, :], op0=ALU.mult,
                                              op1=ALU.subtract))
            st.wait()
            for j, mu in enumerate(("mu_w", "mu_a", "mu_g")):
                if j == 1:
                    dve.wait_ge(product, 2 * cd["in"] + 18)
                if j == 2:
                    dve.wait_ge(product, 2 * cd["lora"] + 1)
                for k in range(KD):
                    last = nc.vector.scalar_tensor_tensor(out=xmix[j % 2][:, k, :], in0=dh[:, k, :], scalar=pcol(mu, k),
                                                          in1=h[:, k, :], op0=ALU.mult, op1=ALU.add)
                last.then_inc(xmix_ready, 1)
                if j == 1:
                    qk_norm_dve(dve, st, 0)
            for n in range(1, NQ):
                qk_norm_dve(dve, st, n)

        hsq_ready, hsum_ready, hroot_ready, qn_ready, perm_ready, perm_read = (
            sem("hsq_ready"), sem("hsum_ready"), sem("hroot_ready"), sem("qn_ready"), sem("perm_ready"), sem("perm_read"))
        NQ = KA + 2

        def qk_act(act):
            for name, dst in (("rope", rope), ("cache_k", ck), ("cache_v", cv)):
                act.dma_start(dst, io[name]).then_inc(loaded, 16)

        def qk_square_act(act, n):
            if n >= 2:
                act.wait_ge(hsum_ready, n - 1)
            nc.scalar.activation(hsq[n % 2], qk[:, n, :], ACT.Square).then_inc(hsq_ready, 1)

        def qk_root_act(act, n):
            act.wait_ge(hsum_ready, n + 1)
            if n >= 2:
                act.wait_ge(qn_ready, n - 1)
            nc.scalar.activation(halves_of(hrs[n % 2]), pair(2 + n % 2), ACT.Sqrt, bias=eps_c[:, 0:1],
                                 scale=1.0 / HD).then_inc(hroot_ready, 1)

        def halves_of(a):
            return a.rearrange("p (a b) -> p a b", a=2)

        def head_sums(pe, src, to):
            for hh in range(2):
                last = nc.tensor.matmul(ps[:, 2 * to + hh, 0:HALF], head_ones, src[:, hh * HALF:(hh + 1) * HALF],
                                        start=True, stop=True)
            return last

        def qk_sums_pe(pe, n):
            pe.wait_ge(hsq_ready, n + 1)
            if n >= 2:
                pe.wait_ge(hroot_ready, n - 1)
            head_sums(pe, hsq[n % 2], 2 + n % 2).then_inc(hsum_ready, 1)

        def qk_norm_dve(dve, st, n):
            r = hrs[n % 2]
            dve.wait_ge(hroot_ready, n + 1)
            st(nc.vector.reciprocal(r, r))
            st.wait()
            nc.vector.scalar_tensor_tensor(out=qk[:, n, :], in0=qk[:, n, :], scalar=pcol("qk_g", n), in1=r,
                                           op0=ALU.mult, op1=ALU.mult).then_inc(qn_ready, 1)

        def qk_pe(pe):
            for n in range(NQ):
                if n >= 2:
                    pe.wait_ge(perm_read, n - 1)
                nc.tensor.matmul(ps[:, 2 + n % 2, 0:LAT], const[:, 3 * P:4 * P], qk[:, n, CTX:T], start=True,
                                 stop=True).then_inc(perm_ready, 1)

        def qk_dve(dve, st):
            dve.wait_ge(loaded, 16 * (LOADS + 3))
            for n in range(NQ):
                a = qk[:, n, CTX:T]
                if n:
                    st.wait()
                dve.wait_ge(perm_ready, n + 1)
                st(nc.vector.tensor_tensor(a, a, rope[:, 0, :], ALU.mult))
                nc.vector.tensor_tensor(rtmp, ps[:, 2 + n % 2, 0:LAT], rope[:, 1, :], ALU.mult).then_inc(perm_read, 1)
                st.wait()
                dve.wait_ge(perm_read, n + 1)
                st(nc.vector.tensor_tensor(a, a, rtmp, ALU.add))

        def shift_pool(pool, st):
            for j, mu in enumerate(("mu_r", "mu_k", "mu_v")):
                a = rkv[:, KA * j:KA * (j + 1), :]
                shift_sum(pool, st, shift, a)
                st(pool.tensor_scalar(shift[:, :, :], shift[:, :, :], 0.5, None, ALU.mult))
                st.wait()
                st(pool.tensor_tensor(shift[:, :, :], shift[:, :, :], a, ALU.subtract))
                st.wait()
                for k in range(KA):
                    st(pool.tensor_scalar(shift[:, k, :], shift[:, k, :], pcol(mu, k), None, ALU.mult))
                st.wait()
                st(pool.tensor_tensor(a, a, shift[:, :, :], ALU.add))
                st.wait()

        qs_ready, s_ready, max_ready, p_ready = (
            sem("qs_ready"), sem("s_ready"), sem("max_ready"), sem("p_ready"))
        e_ready, pT_ready, pTs_ready, o_ready, o_used = (
            sem("e_ready"), sem("pT_ready"), sem("pTs_ready"), sem("o_ready"), sem("o_used"))
        UNITS = 2 * NT
        UNIT = [(e, t) for e in range(2) for t in range(NT)]
        SLOTS = 3
        USES = [("unit", n) for n in range(9)] + [("output", 0)] + [("unit", n) for n in range(9, UNITS)] + [("output", 1)]

        def use_banks(kind, n):
            b = 2 * (USES.index((kind, n)) % SLOTS)
            return ps[:, b:b + 2, :].rearrange("p a b -> p (a b)")

        def attn_pe(pe):
            pe.sem_inc(o_ready, 1)
            for g in range(2):
                with pe.Fori(0, 2) as j:
                    def score(n):
                        e, t = UNIT[n]
                        rows = slice(HD * e, HD * e + HD)
                        k = USES.index(("unit", n))
                        before = USES[:k - SLOTS + 1] if k >= SLOTS else []
                        units = sum(kind == "unit" for kind, _ in before)
                        pe.wait_ge(e_ready, j * UNITS + (2 * g * UNITS + units + 1))
                        if n < SLOTS or before[-1][0] == "output":
                            pe.wait_ge(o_used, j * 2 + (4 * g + len(before) - units + 1))
                        q = qs[rows, t * P:(t + 1) * P]
                        out = use_banks("unit", n)
                        if t == 0:
                            last = nc.tensor.matmul(out[:, 0:CTX], q, qk[rows, KA + g, 0:CTX], start=True, stop=True)
                        else:
                            nc.tensor.matmul(out[:, 0:LAT], q, qk[rows, KA + g, CTX:T], start=True, stop=True)
                            last = nc.tensor.matmul(out[:, LAT:T], q, ck[rows, g, :], start=True, stop=True)
                        last.then_inc(s_ready, 1)

                    def turn(n):
                        e, t = UNIT[n]
                        pe.wait_ge(p_ready, j * UNITS + (2 * g * UNITS + n + 1))
                        pe.wait_ge(pTs_ready, j * UNITS + (2 * g * UNITS + n + 1))
                        for b in range(1 if t == 0 else NT):
                            last = nc.tensor.transpose(ps[:, 6 + b // 4, b % 4 * P:(b % 4 + 1) * P],
                                                       prob[:, n % SLOTS, b * P:(b + 1) * P], ident)
                        last.then_inc(pT_ready, 1)

                    def output(e):
                        rows = slice(HD * e, HD * e + HD)
                        vcols = slice(HD * g, HD * g + HD)
                        pe.wait_ge(pTs_ready, j * UNITS + (2 * g * UNITS + NT * (e + 1) + 1))
                        nc.tensor.matmul(use_banks("output", e)[rows, LAT:T], vd[:, 0, vcols], probC[:, e, :], start=True, stop=True)
                        for b in range(NT):
                            v = vd[:, 1 + b, vcols] if b < 4 else cv[:, vcols]
                            last = nc.tensor.matmul(use_banks("output", e)[rows, 0:LAT], v, probT[:, e, b, :], start=(b == 0),
                                                    stop=(b == NT - 1))
                        last.then_inc(o_ready, 1)

                    pe.wait_ge(qs_ready, j + (2 * g + 1))
                    score(0)
                    score(1)
                    for n in range(UNITS):
                        if n + 2 < UNITS:
                            score(n + 2)
                        turn(n)
                        if n == NT:
                            output(0)
                    output(1)

        def attn_act(act):
            warm(act, ACT.Exp)
            act.sem_inc(e_ready, 1)
            act.sem_inc(pTs_ready, 1)
            for g in range(2):
                with act.Fori(0, 2) as j:
                    act.wait_ge(o_ready, j * 2 + (4 * g + 1))
                    nc.scalar.activation(qs, qk[:, j + 2 * g, :], ACT.Copy).then_inc(qs_ready, 1)

                    def expo(n):
                        e, t = UNIT[n]
                        act.wait_ge(max_ready, j * UNITS + (2 * g * UNITS + n + 1))
                        if n >= SLOTS:
                            act.wait_ge(pT_ready, j * UNITS + (2 * g * UNITS + n - SLOTS + 1))
                        w = P if t == 0 else T
                        src = use_banks("unit", n)[:, 0:w]
                        nc.scalar.activation(prob[:, n % SLOTS, 0:w], src, ACT.Exp, scale=0.125, bias=srow[:, n % SLOTS, 0:1],
                                             accum_out=srow[:, n % SLOTS, 1:2]).then_inc(e_ready, 1)

                    def copy(n):
                        e, t = UNIT[n]
                        act.wait_ge(pT_ready, j * UNITS + (2 * g * UNITS + n + 1))
                        if t == 0:
                            nc.scalar.activation(probC[:, e, :], ps[:, 6, 0:P], ACT.Copy).then_inc(pTs_ready, 1)
                        else:
                            q = slice((t - 1) * P, t * P)
                            nc.scalar.activation(probT[:, e, :, q], ps[:, 6:8, :].rearrange("p a (b q) -> p (a b) q", q=P)[:, 0:NT, :],
                                                 ACT.Copy).then_inc(pTs_ready, 1)

                    expo(0)
                    expo(1)
                    for n in range(UNITS):
                        if n + 2 < UNITS:
                            expo(n + 2)
                        copy(n)

        def attn_dve(dve, st):
            dve.sem_inc(o_used, 1)
            for g in range(2):
                with dve.Fori(0, 2) as j:
                    st.loop(j, 2 * UNITS)

                    def biggest(n):
                        e, t = UNIT[n]
                        w = P if t == 0 else T
                        dve.wait_ge(s_ready, j * UNITS + (2 * g * UNITS + n + 1))
                        src = use_banks("unit", n)[:, 0:w]
                        st(nc.vector.tensor_reduce(srow[:, n % SLOTS, 0:1], src, AX.X, ALU.max))
                        st.wait()
                        nc.vector.tensor_scalar(srow[:, n % SLOTS, 0:1], srow[:, n % SLOTS, 0:1], -0.125, None,
                                                ALU.mult).then_inc(max_ready, 1)

                    def norm(n):
                        e, t = UNIT[n]
                        w = P if t == 0 else T
                        dve.wait_ge(e_ready, j * UNITS + (2 * g * UNITS + n + 2))
                        st(nc.vector.reciprocal(srow[:, n % SLOTS, 2:3], srow[:, n % SLOTS, 1:2]))
                        st.wait()
                        nc.vector.tensor_scalar(prob[:, n % SLOTS, 0:w], prob[:, n % SLOTS, 0:w], srow[:, n % SLOTS, 2:3], None,
                                                ALU.mult).then_inc(p_ready, 1)

                    def out(e):
                        rows = slice(HD * e, HD * e + HD)
                        dve.wait_ge(o_ready, j * 2 + (4 * g + e + 2))
                        nc.vector.tensor_copy(ycat1[rows, j + (KA + 2 * g), 0:CTX], use_banks("output", e)[rows, LAT:T])
                        nc.vector.tensor_copy(ycat1[rows, j + (KA + 2 * g), CTX:T],
                                              use_banks("output", e)[rows, 0:LAT]).then_inc(o_used, 1)

                    biggest(0)
                    biggest(1)
                    norm(0)
                    for n in range(UNITS):
                        if n + 2 < UNITS:
                            biggest(n + 2)
                        if n + 1 < UNITS:
                            norm(n + 1)
                        if n == NT + 1:
                            out(0)
                    out(1)
                    st.end(2)

        ones_ready = sem("ones_ready")
        kk_ready, ksq_ready, ksum_ready, kroot_ready = (
            sem("kk_ready"), sem("ksq_ready"), sem("ksum_ready"), sem("kroot_ready"))

        def kk_act(act):
            for n in range(KA):
                act.wait_ge(kk_ready, n + 1)
                nc.scalar.activation(ksq[n], kk[:, n, :], ACT.Square).then_inc(ksq_ready, 1)
            for n in range(KA):
                act.wait_ge(ksum_ready, n + 1)
                nc.scalar.activation(halves_of(krs[n]), pair(n), ACT.Sqrt, bias=eps_c[:, 2:3]).then_inc(kroot_ready, 1)

        def kk_pe(pe):
            for n in range(KA):
                pe.wait_ge(ksq_ready, n + 1)
                head_sums(pe, ksq[n], n).then_inc(ksum_ready, 1)

        def kk_dve(dve, st):
            for n in range(KA):
                nc.vector.tensor_scalar(kk[:, n, :], rkv[:, KA + n, :], pcol("k_k", n), None, ALU.mult).then_inc(kk_ready, 1)
            for n, name in enumerate(("w0", "a0")):
                last = nc.vector.tensor_scalar(halves[:, n, :], par[:, PAR[name]:PAR[name] + 2 * KA], 0.5, None, ALU.mult)
            last.then_inc(kk_ready, 1)
            kk_root_dve(dve, st, 0, 0, 4)
            kk_norm_dve(dve, st, 0)

        def kk_root_dve(dve, st, n, begin, end):
            dve.wait_ge(kroot_ready, n + 1)
            a = krs[n][:, begin * (T // 4):end * (T // 4)]
            st(nc.vector.reciprocal(a, a))

        def kk_norm_dve(dve, st, n):
            st.wait()
            dve.wait_ge(kk_ready, KA)
            st(nc.vector.tensor_tensor(kk[:, n, :], kk[:, n, :], krs[n], ALU.mult))

        def kk_pool(pool):
            pool.memset(mask01[:, :], 1.0).then_inc(ones_ready, 1)
            pool.wait_ge(ones_ready, 1)
            pool.memset(mask01[:, 0:T:C], 0.0).then_inc(ones_ready, 1)

        GR = [(0, 4), (4, 8), (8, NC)]
        JOBS = [("At", "act"), ("Bt", "act"), ("Kt", "act"), ("M", "dve"), ("MT", "dve"), ("NT", "dve"),
                ("PT", "dve"), ("QT", "dve")]
        for l in range(1, LEVELS):
            JOBS += [("Y%d" % l, "dve")] + ([("X%d" % l, "dve")] if l < LEVELS - 1 else []) + [("XT%d" % l, "dve")]
        JOBS += [("NV", "act"), ("AH", "act"), ("UV", "act")]
        JOB_BANKS = 6
        VT_BANKS = (7, 3, 6)
        NG = len(GR)
        order, counts = {}, {"act": 0, "dve": 0}
        for name, who in JOBS:
            for g in range(NG):
                counts[who] += 1
                order[name, g] = (len(order), who, counts[who])
        by_number = {v[0]: v for v in order.values()}
        SEQ = [[2, 0, 3, 1, 4, 5, 6, 7, 8, 9], [9, 1, 8, 0, 7, 6, 5, 4, 3, 2]]
        evac = {"act": sem("evac_act"), "dve": sem("evac_dve")}
        job_ready, scan_ready, exp_ready = sem("job_ready"), sem("scan_ready"), sem("exp_ready")
        kd_ready, mult_dve, mult_pool, r_ready, xt_ready, zero_ready = (
            sem("kd_ready"), sem("mult_dve"), sem("mult_pool"), sem("r_ready"), sem("xt_ready"), sem("zero_ready"))
        bg_made, bg_read = sem("bg_made"), sem("bg_read")
        vb_ready, vt_made, vt_read, tail_y, tail_sq = (
            sem("vb_ready"), sem("vt_made"), sem("vt_read"), sem("tail_y"), sem("tail_sq"))
        u_made, u_read, s_made, s_read, y_ready, y_read = (
            sem("u_made"), sem("u_read"), sem("s_made"), sem("s_read"), sem("y_ready"), sem("y_read"))
        wa_in, g_in, state_in, state_out = sem("wa_in"), sem("g_in"), sem("state_in"), sem("state_out")
        pool_passed = sem("pool_passed")
        state_zero = sem("state_zero")

        def per_chunk(a):
            return a.rearrange("p (c t) -> p c t", t=C)

        def mask(n, count):
            a = const[:, 4 * P + n * C:4 * P + (n + 1) * C]
            return a.unsqueeze(1).to_broadcast([P, 2 * count, C])

        def by_head(a):
            return a.rearrange("p c (e t) -> p (c e) t", e=2)

        def ids(count):
            return ident.unsqueeze(1).to_broadcast([P, count, P])

        STRICT, INCL, LEVEL = 0, 2, 4

        def scan_bank(name, g):
            n = order[name, g][0]
            a, b = GR[g]
            return ps[:, n % JOB_BANKS, 0:(b - a) * P].rearrange("p (c m) -> p c m", m=P)

        class Unit:
            def __init__(self, j, o, d, r, prep=True, tail=False):
                self.j, self.o, self.d, self.r, self.prep, self.tail = j, o, d, r, prep, tail

            def i(self, m=1, c=0):
                return self.j * m + (self.o * m + c)

            def u(self, m, c=0):
                return self.j * (2 * m) + ((2 * self.o + self.d) * m + c)

            def round(self, name):
                names = (["bonus", "mean", "var"] if self.tail else []) + (["decay", "rate"] if self.prep else []) + (
                    ["gate"] if self.tail else [])
                return self.j * ROUNDS + (self.r + names.index(name) + 1)

            def rounds_before(self):
                return self.j * ROUNDS + self.r

            def rounds_after(self):
                return self.j * ROUNDS + (self.r + 2 * self.prep + 4 * self.tail)

            def next(self):
                return Unit(self.j, self.o + self.d, 1 - self.d, self.r)

            def last_pair(self):
                return Unit(self.j, self.o - 1, self.d, self.r)

        ROUNDS = 8
        FIRST = Unit(0, 0, 0, 2)
        LAST = Unit(0, HP - 1, 1, 4 + ROUNDS * (HP - 1), prep=False)
        END = Unit(0, HP, 0, 4 + ROUNDS * (HP - 1), prep=False, tail=True)

        def loop_units(j):
            return (Unit(j, 0, 1, 4), Unit(j, 1, 0, 6, tail=True))

        round_banks = ps[:, 6:8, 0:HALF]

        def scan_pe(pe):
            def round_of(v, name, lhs, src):
                pe.wait_ge(bg_read, v.round(name))
                for hh in range(2):
                    last = nc.tensor.matmul(ps[:, 6 + hh, 0:HALF], lhs, src[:, hh * HALF:(hh + 1) * HALF], start=True, stop=True)
                last.then_inc(bg_made, 1)

            def beside(v, name):
                if v.tail:
                    p = v.last_pair()
                    if name == "Bt":
                        if v is END:
                            pe.wait_ge(y_read, v.u(2, 1))
                        else:
                            pe.wait_ge(vt_read, v.i(NG, NG))
                        round_of(v, "bonus", head_ones, rkv[:, p.i(1, KA), :])
                    if name == "Kt":
                        round_of(v, "mean", head_ones, ycat1[:, p.i(), :])
                    if name == "NT":
                        pe.wait_ge(tail_sq, p.i(1, 1))
                        round_of(v, "var", head_ones, rkv[:, p.i(), :])
                    if name == "X2":
                        round_of(v, "gate", stage_g, lg)
                if v.prep:
                    rows = slice(HD * (1 - v.d), HD * (1 - v.d) + HD)
                    if name == "QT":
                        pe.wait_ge(wa_in, v.next().i(16, 16))
                        round_of(v, "decay", stage[rows, 0:P], lw[rows])
                    if name == "X1":
                        round_of(v, "rate", stage[rows, P:2 * P], la[rows])

            def unit(v):
                d = v.d

                def job(name, *args, needs=(), xt=False):
                    for g, (a, b) in enumerate(GR):
                        n = order[name, g][0]
                        before = ([by_number[n - JOB_BANKS]] if n >= JOB_BANKS else []) + [order[need, g] for need in needs]
                        for who in ("act", "dve"):
                            m = max([b[2] for b in before if b[1] == who], default=0)
                            if m:
                                pe.wait_ge(evac[who], v.u(counts[who], m))
                        if xt:
                            pe.wait_ge(xt_ready, v.u(NG, g + 1))
                        bank = scan_bank(name, g)
                        for c in range(a, b):
                            if len(args) == 1:
                                last = nc.tensor.transpose(bank[:, c - a, :], mats[args[0]][:, c, :], ident)
                            else:
                                last = nc.tensor.matmul(bank[:, c - a, :], mats[args[0]][:, c, :],
                                                        mats[args[1]][:, c, :], start=True, stop=True)
                        last.then_inc(job_ready, 1)
                    beside(v, name)

                pe.wait_ge(mult_dve, v.u(4, 4))
                pe.wait_ge(s_read, v.u(NC, 1))
                job("At", "A")
                pe.wait_ge(y_read, v.u(2, 1))
                if d == 0:
                    pe.wait_ge(vb_ready, v.i(1, 1))
                    for g, (a, b) in enumerate(GR):
                        for c in range(a, b):
                            last = nc.tensor.transpose(ps[:, VT_BANKS[g], (c - a) * P:(c - a + 1) * P], mats["Vb"][:, c, :], ident)
                        last.then_inc(vt_made, 1)
                    pe.wait_ge(vt_read, v.i(NG, NG - 1))
                job("Bt", "B")
                if d == 0:
                    pe.wait_ge(vt_read, v.i(NG, NG))
                pe.wait_ge(mult_pool, v.u(1, 1))
                job("Kt", "K")
                job("M", "A", "B")
                job("MT", "B", "A")
                job("NT", "K", "A")
                pe.wait_ge(r_ready, v.u(2, 2))
                job("PT", "B", "R")
                job("QT", "K", "R")
                for l in range(1, LEVELS):
                    xs = ["M"] if l == 1 else ["X%d" % (l - 1)]
                    ts = [] if l == 1 else ["XT%d" % (l - 1)]
                    job("Y%d" % l, "MT", "X", needs=xs + ["MT"])
                    if l < LEVELS - 1:
                        job("X%d" % l, "XT", "Y", needs=["Y%d" % l] + ts, xt=l == 1)
                    job("XT%d" % l, "Y", "XT", needs=["Y%d" % l] + ts)
                job("NV", "NT", "Vt", needs=["NT"])
                job("AH", "At", "XT", needs=["At", "XT%d" % (LEVELS - 1)])
                job("UV", "XT", "NV", needs=["NV"])
                pe.wait_ge(evac["act"], v.u(counts["act"], counts["act"]))
                pe.wait_ge(evac["dve"], v.u(counts["dve"], counts["dve"]))
                pe.wait_ge(bg_read, v.rounds_after() + 1)
                pe.wait_ge(state_in, v.u(16, 16))
                pe.wait_ge(state_zero, v.u(1, 1))
                step = [0, 0]
                for q, c in enumerate(SEQ[d]):
                    grp = 1 if c >= NCC else 0
                    cur = state[:, grp, step[grp] % 2, :]
                    if q >= 1:
                        last_q = q - 1 if q > 4 else q - 2
                        if last_q >= 0:
                            pe.wait_ge(s_read, v.u(NC, last_q + 2))
                    s_bank = ps[:, 2 + q % 2, 0:P]
                    y_bank = ps[:, 4 + c // 4, c % 4 * P:(c % 4 + 1) * P]
                    nc.tensor.matmul(ps[:, q % 2, 0:P], mats["AH"][:, c, :], cur, start=True, stop=True).then_inc(u_made, 1)
                    nc.tensor.matmul(s_bank, mats["Kt"][:, c, :], mats["Vt"][:, c, :], start=True, stop=False)
                    nc.tensor.matmul(y_bank, cur, mats["R"][:, c, :], start=True, stop=False)
                    pe.wait_ge(u_read, v.u(NC, q + 1))
                    uu = ubuf[:, q % 2, :]
                    nc.tensor.matmul(s_bank, mats["Bt"][:, c, :], uu, start=False, stop=True).then_inc(s_made, 1)
                    nc.tensor.matmul(y_bank, uu, mats["PT"][:, c, :], start=False, stop=False)
                    last = nc.tensor.matmul(y_bank, mats["Vt"][:, c, :], mats["QT"][:, c, :], start=False, stop=True)
                    step[grp] += 1
                last.then_inc(y_ready, 1)

            pe.sem_inc(y_ready, 1)
            pe.wait_ge(wa_in, 16)
            pe.wait_ge(kroot_ready, KA)
            pe.wait_ge(bg_read, 1)
            for n, src in enumerate((lw, la)):
                pe.wait_ge(bg_read, n + 1)
                for hh in range(2):
                    last = nc.tensor.matmul(ps[:, 6 + hh, 0:HALF], stage[0:HD, n * P:(n + 1) * P],
                                            src[0:HD, hh * HALF:(hh + 1) * HALF], start=True, stop=True)
                last.then_inc(bg_made, 1)
            unit(FIRST)
            with pe.Fori(0, HP - 1) as j:
                for v in loop_units(j):
                    if v.tail:
                        pe.wait_ge(g_in, v.i(16))
                    unit(v)
            unit(LAST)
            pe.wait_ge(g_in, 16 * HP)
            for name in ("Bt", "Kt", "NT", "X2"):
                beside(END, name)

        def scan_act(act):
            def decay_and_rate(v, n, r):
                act.wait_ge(bg_made, r)
                nc.scalar.activation(halves_of((wbuf, abuf)[n]), round_banks, ACT.Tanh, scale=0.5,
                                     bias=halves[:, n, bass.ds(v.i(1, KA * v.d), 1)]).then_inc(bg_read, 1)

            def exps(v):
                act.wait_ge(scan_ready, v.u(1, 1))
                nc.scalar.activation(wbuf, wbuf, ACT.Exp)
                nc.scalar.activation(e2buf, gbuf, ACT.Exp, scale=-1.0)
                nc.scalar.activation(gbuf, gbuf, ACT.Exp).then_inc(exp_ready, 1)

            def tail_square(v):
                p = v.last_pair()
                act.wait_ge(tail_y, p.i(1, 1))
                nc.scalar.activation(rkv[:, p.i(), :], ycat1[:, p.i(), :], ACT.Square).then_inc(tail_sq, 1)

            def tail_root(v):
                act.wait_ge(bg_made, v.round("var"))
                nc.scalar.activation(halves_of(rs[:, :]), round_banks, ACT.Sqrt, bias=eps_c[:, 1:2],
                                     scale=1.0 / HD).then_inc(bg_read, 1)

            def unit(v):
                for name, who in JOBS:
                    if who != "act":
                        continue
                    if name == "Bt" and v.d == 0:
                        for g, (a, b) in enumerate(GR):
                            act.wait_ge(vt_made, v.i(NG, g + 1))
                            nc.scalar.activation(mats["Vt"][:, a:b, :],
                                                 ps[:, VT_BANKS[g], 0:(b - a) * P].rearrange("p (c m) -> p c m", m=P),
                                                 ACT.Copy).then_inc(vt_read, 1)
                    if name == "NV":
                        if v.tail:
                            tail_square(v)
                            tail_root(v)
                        if v.prep:
                            decay_and_rate(v.next(), 0, v.round("decay"))
                            decay_and_rate(v.next(), 1, v.round("rate"))
                            exps(v.next())
                    for g, (a, b) in enumerate(GR):
                        act.wait_ge(job_ready, v.u(len(order), order[name, g][0] + 1))
                        nc.scalar.activation(mats[name][:, a:b, :], scan_bank(name, g), ACT.Copy,
                                             scale=-1.0 if name in ("AH", "UV") else 1.0).then_inc(evac["act"], 1)

            warm(act, ACT.Tanh)
            act.wait_ge(kk_ready, KA + 1)
            act.sem_inc(bg_read, 1)
            decay_and_rate(FIRST, 0, 1)
            decay_and_rate(FIRST, 1, 2)
            exps(FIRST)
            unit(FIRST)
            with act.Fori(0, HP - 1) as j:
                for v in loop_units(j):
                    unit(v)
            unit(LAST)
            tail_square(END)
            tail_root(END)

        def scan_dve(dve, st):
            def decays(v, r):
                dve.wait_ge(bg_read, r + 1)
                st(nc.vector.tensor_scalar(wbuf, wbuf, -0.5 * E_HALF, -0.5 * E_HALF, ALU.mult, ALU.add))
                st.wait()
                way = slice(None, None, 1 if v.d == 0 else -1)
                st(nc.vector.tensor_tensor_scan(gbuf[:, way], mask01[:, :], wbuf[:, way], 0.0, ALU.mult, ALU.add))

            def decays_before(v):
                st.wait()
                nc.vector.tensor_tensor(wbuf, gbuf, wbuf, ALU.subtract).then_inc(scan_ready, 1)

            def rates(v, r):
                dve.wait_ge(bg_read, r + 2)
                st(nc.vector.tensor_scalar(abuf, abuf, 0.5, 0.5, ALU.mult, ALU.add))

            def keys_part(v):
                st.wait()
                st(nc.vector.tensor_scalar(kdbuf, abuf, 1.0, par[:, bass.ds(v.i(1, PAR["k_a"]), 1)], ALU.subtract, ALU.mult))
                st(nc.vector.tensor_tensor(abuf, kk[:, v.i(), :], abuf, ALU.mult))

            def keys_done(v):
                st.wait()
                nc.vector.scalar_tensor_tensor(out=kdbuf, in0=kdbuf, scalar=1.0, in1=rkv[:, v.i(1, KA), :], op0=ALU.add,
                                               op1=ALU.mult).then_inc(kd_ready, 1)

            def bonus_part(v):
                dve.wait_ge(kd_ready, v.u(1, 1))
                st(nc.vector.scalar_tensor_tensor(out=bacc if v.d == 0 else rkv[:, v.i(1, KA), :], in0=kdbuf,
                                                  scalar=par[:, bass.ds(v.i(1, PAR["r_k"]), 1)], in1=rkv[:, v.i(), :],
                                                  op0=ALU.mult, op1=ALU.mult))

            def bonus_sum(v):
                st.wait()
                if v.d == 1:
                    k = rkv[:, v.i(1, KA), :]
                    st(nc.vector.tensor_tensor(k, k, bacc, ALU.add))

            def a_and_b(v):
                dve.wait_ge(exp_ready, v.u(1, 1))
                st.wait()
                for e in range(2):
                    rows = slice(HD * e, HD * e + HD)
                    nc.vector.tensor_tensor(mats["A"][rows, :, rows], per_chunk(kk[rows, v.i(), :]), per_chunk(wbuf[rows]),
                                            ALU.mult).then_inc(mult_dve, 1)
                    nc.vector.tensor_tensor(mats["B"][rows, :, rows], per_chunk(abuf[rows]), per_chunk(e2buf[rows]),
                                            ALU.mult).then_inc(mult_dve, 1)

            def tail_bonus(v):
                p = v.last_pair()
                k = halves_of(rkv[:, p.i(1, KA), :])
                dve.wait_ge(bg_made, v.round("bonus"))
                nc.vector.tensor_tensor(k, halves_of(rkv[:, p.i(1, 2 * KA), :]), round_banks, ALU.mult).then_inc(bg_read, 1)

            def tail_mean(v):
                p = v.last_pair()
                y = halves_of(ycat1[:, p.i(), :])
                dve.wait_ge(bg_made, v.round("mean"))
                dve.wait_ge(y_read, v.u(2, 1))
                last = nc.vector.scalar_tensor_tensor(out=y, in0=round_banks, scalar=-1.0 / HD, in1=y, op0=ALU.mult, op1=ALU.add)
                st(last)
                st.wait()
                dve.sem_inc(bg_read, 1)
                dve.sem_inc(tail_y, 1)

            def tail_root(v, part):
                if part == 0:
                    dve.wait_ge(bg_read, v.round("var") + 1)
                a = rs[:, part * (T // 4):(part + 1) * (T // 4)]
                st(nc.vector.reciprocal(a, a))

            def tail_norm(v):
                y = ycat1[:, v.last_pair().i(), :]
                st.wait()
                st(nc.vector.tensor_tensor(y, y, rs[:, :], ALU.mult))

            def tail_affine(v):
                p = v.last_pair()
                y = ycat1[:, p.i(), :]
                st.wait()
                st(nc.vector.tensor_scalar(y, y, par[:, bass.ds(p.i(1, PAR["ln_g"]), 1)],
                                           par[:, bass.ds(p.i(1, PAR["ln_b"]), 1)], ALU.mult, ALU.add))

            def tail_add(v):
                p = v.last_pair()
                y = ycat1[:, p.i(), :]
                st.wait()
                st(nc.vector.tensor_tensor(y, y, rkv[:, p.i(1, KA), :], ALU.add))

            def tail_gate(v):
                y = halves_of(ycat1[:, v.last_pair().i(), :])
                dve.wait_ge(bg_made, v.round("gate"))
                st.wait()
                nc.vector.tensor_tensor(y, y, round_banks, ALU.mult).then_inc(bg_read, 1)

            def beside(v, name):
                if v is FIRST:
                    if name == "head":
                        for n in (1, 2):
                            kk_root_dve(dve, st, n, 0, 4)
                            kk_norm_dve(dve, st, n)
                    if name in ("QT", "Y1", "X1", "XT1"):
                        part = ("QT", "Y1", "X1", "XT1").index(name)
                        kk_root_dve(dve, st, 3, part, part + 1)
                    if name == "Y2":
                        kk_norm_dve(dve, st, 3)
                if v.tail:
                    if name == "head":
                        tail_bonus(v)
                        tail_mean(v)
                    if name in ("QT", "Y1", "X1", "XT1"):
                        tail_root(v, ("QT", "Y1", "X1", "XT1").index(name))
                    if name == "Y2":
                        tail_norm(v)
                    if name == "X2":
                        tail_affine(v)
                    if name == "XT2":
                        tail_add(v)
                    if name == "X3":
                        tail_gate(v)
                if v.prep:
                    after, r = v.next(), v.round("decay")
                    if name == "Y2":
                        decays(after, r)
                    if name == "X2":
                        decays_before(after)
                    if name == "XT2":
                        rates(after, r)
                    if name == "Y3":
                        keys_part(after)
                    if name == "XT3":
                        keys_done(after)
                    if name == "Y4":
                        bonus_part(after)
                    if name == "X4":
                        bonus_sum(after)
                    if name == "XT%d" % (LEVELS - 1):
                        a_and_b(after)

            def unit(v):
                d = v.d
                st(nc.vector.tensor_copy(gend, gbuf[:, (C - 1 if d == 0 else 0):T:C]))
                for e in range(2):
                    rows = slice(HD * e, HD * e + HD)
                    nc.vector.tensor_tensor(mats["R"][rows, :, rows], per_chunk(rkv[rows, v.i(), :]), per_chunk(gbuf[rows]),
                                            ALU.mult).then_inc(r_ready, 1)
                beside(v, "head")
                for name, who in JOBS:
                    if who != "dve":
                        continue
                    for g, (c0, c1) in enumerate(GR):
                        dve.wait_ge(job_ready, v.u(len(order), order[name, g][0] + 1))
                        bank, n = scan_bank(name, g), c1 - c0
                        if name == "M":
                            xm = mats["X"][:, c0:c1, :]
                            st(nc.vector.tensor_tensor(by_head(xm), by_head(bank), mask(LEVEL + d, n), ALU.mult))
                            st.wait()
                            last = nc.vector.tensor_tensor(xm, xm, ids(n), ALU.add)
                        elif name in ("MT", "NT"):
                            last = nc.vector.tensor_tensor(by_head(mats[name][:, c0:c1, :]), by_head(bank), mask(STRICT + d, n),
                                                           ALU.mult)
                        elif name in ("PT", "QT"):
                            last = nc.vector.tensor_tensor(by_head(mats[name][:, c0:c1, :]), by_head(bank), mask(INCL + d, n),
                                                           ALU.mult)
                        elif name[0] == "Y":
                            last = nc.vector.tensor_tensor(by_head(mats["Y"][:, c0:c1, :]), by_head(bank),
                                                           mask(LEVEL + 2 * int(name[1]) + d, n), ALU.mult)
                        else:
                            xm = mats[name[:-1]][:, c0:c1, :]
                            last = nc.vector.tensor_tensor(xm, xm, bank, ALU.subtract)
                        last.then_inc(evac["dve"], 1)
                    beside(v, name)
                st.wait()
                step = [0, 0]
                for q, c in enumerate(SEQ[d]):
                    grp = 1 if c >= NCC else 0
                    cur, new = state[:, grp, step[grp] % 2, :], state[:, grp, (step[grp] + 1) % 2, :]
                    dve.wait_ge(u_made, v.u(NC, q + 1))
                    if q == 0:
                        dve.wait_ge(evac["act"], v.u(counts["act"], counts["act"]))
                    nc.vector.tensor_tensor(ubuf[:, q % 2, :], ps[:, q % 2, 0:P], mats["UV"][:, c, :],
                                            ALU.add).then_inc(u_read, 1)
                    st(nc.vector.tensor_scalar(sgbuf, cur, gend[:, c:c + 1], None, ALU.mult))
                    dve.wait_ge(s_made, v.u(NC, q + 1))
                    st.wait()
                    nc.vector.scalar_tensor_tensor(out=new, in0=ps[:, 2 + q % 2, 0:P], scalar=gend[:, c:c + 1], in1=sgbuf,
                                                   op0=ALU.mult, op1=ALU.add).then_inc(s_read, 1)
                    dve.wait_ge(s_read, v.u(NC, q + 2))
                    step[grp] += 1
                dve.wait_ge(y_ready, v.u(1, 2))
                if d == 1:
                    dve.wait_ge(y_read, v.u(2, 1))
                for e in range(2):
                    rows = slice(HD * e, HD * e + HD)
                    y = per_chunk(ycat1[rows, v.i(), :])
                    y_banks = ps[rows, 4:7, :].rearrange("p a (c m) -> p (a c) m", m=P)[:, 0:NC, rows]
                    if d == 0:
                        nc.vector.tensor_copy(y, y_banks).then_inc(y_read, 1)
                    else:
                        nc.vector.tensor_tensor(y, y, y_banks, ALU.add).then_inc(y_read, 1)

            dve.sem_inc(y_read, 1)
            dve.sem_inc(s_read, 1)
            dve.wait_ge(ones_ready, 2)
            st.wait()
            decays(FIRST, 1)
            decays_before(FIRST)
            rates(FIRST, 1)
            keys_part(FIRST)
            keys_done(FIRST)
            bonus_part(FIRST)
            dve.wait_ge(zero_ready, 1)
            a_and_b(FIRST)
            unit(FIRST)
            with dve.Fori(0, HP - 1) as j:
                st.loop(j, SCAN_STEPS)
                for v in loop_units(j):
                    unit(v)
                st.end(HP - 1)
            unit(LAST)
            for name in ("head", "QT", "Y1", "X1", "XT1", "Y2", "X2", "XT2", "X3"):
                beside(END, name)

        def scan_pool(pool, st):
            def hold():
                pool.sem_inc(pool_passed, 1)

            def k_matrix(v):
                pool.wait_ge(kd_ready, v.u(1, 1))
                pool.wait_ge(exp_ready, v.u(1, 1))
                for e in range(2):
                    rows = slice(HD * e, HD * e + HD)
                    st(pool.tensor_tensor(mats["K"][rows, :, rows], per_chunk(kdbuf[rows]), per_chunk(e2buf[rows]), ALU.mult))
                    st.wait()
                pool.sem_inc(mult_pool, 1)

            def v_matrix(v):
                for e in range(2):
                    rows = slice(HD * e, HD * e + HD)
                    st(pool.tensor_copy(mats["Vb"][rows, :, rows], per_chunk(rkv[rows, v.i(1, 2 * KA), :])))
                    st.wait()
                    hold()
                pool.sem_inc(vb_ready, 1)

            def unit(v):
                pool.wait_ge(y_ready, v.u(1, 1))
                pool.wait_ge(s_read, v.u(NC, 1))
                hold()
                pool.dma_start(state[:, 1, 0, :], io["state"][v.u(1)]).then_inc(state_in, 16)
                if v is not FIRST:
                    pool.wait_ge(state_out, v.u(16))
                    hold()
                pool.memset(state[:, 0, 0, :], 0.0).then_inc(state_zero, 1)
                if v.d == 1:
                    pool.wait_ge(bg_read, v.rounds_before() + 1)
                    hold()
                    if v.prep:
                        pool.dma_start(stage, io["scan_w"][v.i(1, 1)][:, 0:2 * P]).then_inc(wa_in, 16)
                    pool.dma_start(stage_g, io["scan_w"][v.i()][:, 2 * P:3 * P]).then_inc(g_in, 16)
                for g, (c0, c1) in enumerate(GR):
                    pool.wait_ge(evac["dve"], v.u(counts["dve"], order["MT", g][2]))
                    xt = mats["XT"][:, c0:c1, :]
                    st(pool.tensor_tensor(by_head(xt), by_head(mats["MT"][:, c0:c1, :]), mask(LEVEL + 1 - v.d, c1 - c0), ALU.mult))
                    st.wait()
                    pool.tensor_tensor(xt, xt, ids(c1 - c0), ALU.add).then_inc(xt_ready, 1)
                if v.prep:
                    k_matrix(v.next())
                    if v.d == 1:
                        pool.wait_ge(job_ready, v.u(len(order), order["Y%d" % (LEVELS - 1), NG - 1][0] + 1))
                        hold()
                        v_matrix(v.next())
                pool.wait_ge(y_ready, v.u(1, 2))
                pool.wait_ge(s_read, v.u(NC, NC + 1))
                hold()
                pool.dma_start(io["new_state"][v.u(1)], state[:, 0, 0, :]).then_inc(state_out, 16)

            pool.dma_start(stage, io["scan_w"][0][:, 0:2 * P]).then_inc(wa_in, 16)
            st(pool.memset(region(U_AT[0], 5 * NC * P), 0.0))
            st.wait()
            pool.sem_inc(zero_ready, 1)
            v_matrix(FIRST)
            k_matrix(FIRST)
            unit(FIRST)
            with pool.Fori(0, HP - 1) as j:
                st.loop(j, SCAN_POOL)
                for v in loop_units(j):
                    unit(v)
                st.end(HP - 1)
            unit(LAST)
            pool.wait_ge(state_out, 16 * 2 * HP)

        def pass_gate(eng, n):
            eng.drain().then_inc(gate, 1)
            eng.wait_ge(gate, 4 * n)

        LOADS = 5
        ab_tiles()
        ffn_tiles(0)
        cd_tiles()
        ffn_tiles(1)

        y_out = sem("y_out")
        start_in = sem("start_in")
        EARLY = 1

        def final_dve(dve, st, turn):
            rms_dve(dve, st, turn)
            for k in range(KD):
                nc.vector.scalar_tensor_tensor(out=h[:, k, :], in0=x[:, k, :], scalar=pcol("final", k), in1=rs[:, :],
                                               op0=ALU.mult, op1=ALU.mult).then_inc(y_out, 1)

        block = ctx.enter_context(nc.Block())

        @block.sync
        def _(sp):
            for name, dst in (("cvec", cvec[:, :, :]), ("const", const[:, :])):
                sp.dma_start(dst, io[name]).then_inc(start_in, 16)
            modulation_first_sp(sp, 0)
            for name, dst in (("x_fm", x[:, :, :]), ("par", par[:, :]), ("ws_t", wsT), ("v_rows", vrow), ("bs_rows", bsrow)):
                sp.dma_start(dst, io[name]).then_inc(loaded, 16)
            modulation_rest_sp(sp, 0)
            at, before = 0, None
            for dram, first, n, cols, split in tiles:

                def free(i, s, split, cols):
                    if split and cols <= DEEP:
                        sp.wait_ge(lo_ready, i * 2 + (2 * parts_at + s - 1))
                    else:
                        sp.wait_ge(product, i * 2 + (2 * at + s - 1))

                parts_at = split_pairs[at]
                for s in range(2):
                    if at:
                        free(0, s, before, cols)
                    sp.dma_start(wslot[:, s, 0:cols], dram[first + s]).then_inc(w_in[s], 16)
                if at == ab["out"]:
                    sp.wait_ge(product, 2 * at)
                    modulation_first_sp(sp, 1)
                    modulation_rest_sp(sp, 1)
                with sp.Fori(1, n // 2) if n > 2 else ExitStack() as i:
                    for s in range(2) if n > 2 else ():
                        free(i, s, split, cols)
                        sp.dma_start(wslot[:, s, 0:cols], dram[i * 2 + (first + s)]).then_inc(w_in[s], 16)
                at, before = at + n // 2, split

        @block.tensor
        def _(pe):
            pe.sem_inc(drained[0], 1)
            pe.sem_inc(drained[1], 1)
            pe.wait_ge(start_in, 32)
            pe.wait_ge(silu_ready, 1)
            modulation_tiles_pe(pe, 0, 0, EARLY)
            pe.wait_ge(loaded, 16 * LOADS)
            rms_pe(pe, 0, KD)
            modulation_tiles_pe(pe, 0, EARLY, MOD_TURNS)
            modulation_columns_pe(pe, 0)
            pass_gate(pe, 1)
            pass_gate(pe, 2)
            ab_pe(pe)
            pass_gate(pe, 3)
            rms_pe(pe, 1, KA)
            pass_gate(pe, 4)
            last_product_pe(pe, ab["out"], KD, y_hi, y_lo, 0, chunk_of_ycat(pe, 0))
            pass_gate(pe, 5)
            ffn_pe(pe, 0)
            pass_gate(pe, 6)
            cd_pe(pe)
            pass_gate(pe, 7)
            qk_pe(pe)
            pass_gate(pe, 8)
            attn_pe(pe)
            pass_gate(pe, 9)
            kk_pe(pe)
            scan_pe(pe)
            pass_gate(pe, 10)
            last_product_pe(pe, cd["out"], KD, y1_hi, y1_lo, 2, chunk_of_ycat(pe, 1))
            pass_gate(pe, 11)
            ffn_pe(pe, 1)
            pass_gate(pe, 12)

        @block.scalar
        def _(act):
            st = Steps(act, act_step)
            act.wait_ge(start_in, 32)
            nc.scalar.activation(cvec[:, :, :], cvec[:, :, :], ACT.Silu).then_inc(silu_ready, 1)
            act.wait_ge(eps_ready, 3)
            act.sem_inc(mod_read, MOD_SLOTS)
            modulation_act(act, 0, 0, EARLY)
            act.wait_ge(loaded, 16 * LOADS)
            squares_act(act, [(sq[:, k, :], x[:, k, :]) for k in range(KD)])
            root_act(act, 0, KD, 0)
            modulation_act(act, 0, EARLY, MOD_TURNS)
            pass_gate(act, 1)
            adaln_act(act, 0, 0, h_hi)
            pass_gate(act, 2)
            ab_act(act, st)
            pass_gate(act, 3)
            yb_act(act, st, 1)
            pass_gate(act, 4)
            parts_act(act, ab["out"], KD, then=ffn[0, 0, "up"], use=lambda i, s: square_of_x(act, ab["out"], i, s))
            pass_gate(act, 5)
            root_act(act, 2, KD, 0)
            adaln_act(act, 1, 1, h_hi)
            ffn_act(act, st, 0)
            pass_gate(act, 6)
            for s in range(2):
                tile_hi(act, cd["in"], 0, s)
            root_act(act, 3, KD, 0)
            adaln_act(act, 2, 0, h1_hi)
            cd_act(act)
            pass_gate(act, 7)
            qk_act(act)
            pass_gate(act, 8)
            act.dma_start(io["new_k"], qk[0:HD, KA:KA + 2, 0:CTX]).then_inc(out_done, 16)
            act.dma_start(io["new_v"], vd[:, 0, :]).then_inc(out_done, 16)
            attn_act(act)
            act.wait_ge(out_done, 32)
            pass_gate(act, 9)
            kk_act(act)
            scan_act(act)
            pass_gate(act, 10)
            tile_hi(act, cd["out"], 0, 0)
            source_hi(act, ycat1, y1_hi, range(KD))
            tile_hi(act, cd["out"], 0, 1)
            parts_act(act, cd["out"], KD, then=ffn[1, 0, "up"], use=lambda i, s: square_of_x(act, cd["out"], i, s))
            pass_gate(act, 11)
            root_act(act, 4, KD, 0)
            adaln_act(act, 3, 1, h_hi)
            ffn_act(act, st, 1)
            pass_gate(act, 12)
            root_act(act, 5, KD, 0)
            for k in range(KD):
                act.wait_ge(y_out, k + 1)
                act.dma_start(io["y"][:, k, :], h[:, k, :]).then_inc(out_done, 16)
            act.wait_ge(out_done, 16 * (KD + 2))

        @block.vector
        def _(dve):
            st = Steps(dve, dve_step)
            dve.wait_ge(loaded, 16 * LOADS)
            rms_dve(dve, st, 0)
            for k in range(KD):
                normed_dve(dve, st, k)
            modulation_dve(dve, st, 0)
            pass_gate(dve, 1)
            adaln_dve(dve, st, 0, 0, normed=True)
            source_lo(dve, "dve", 0, h, h_hi, h_lo, range(BY_POOL, KD))
            pass_gate(dve, 2)
            ab_dve(dve, st)
            pass_gate(dve, 3)
            yb_dve(dve, st, 1)
            pass_gate(dve, 4)
            residual_dve(dve, ab["out"], 2 * KD)
            pass_gate(dve, 5)
            rms_dve(dve, st, 2)
            adaln_dve(dve, st, 1, 1)
            source_lo(dve, "dve", 2 * KD, h, h_hi, h_lo, range(BY_POOL, KD))
            ffn_dve(dve, st, 0)
            pass_gate(dve, 6)
            rms_dve(dve, st, 3)
            adaln_dve(dve, st, 2, 0)
            source_lo(dve, "dve", 3 * KD, h, h1_hi, h1_lo, range(BY_POOL, KD))
            cd_dve(dve, st)
            pass_gate(dve, 7)
            qk_dve(dve, st)
            pass_gate(dve, 8)
            attn_dve(dve, st)
            pass_gate(dve, 9)
            kk_dve(dve, st)
            scan_dve(dve, st)
            pass_gate(dve, 10)
            source_lo(dve, "dve", 4 * KD, ycat1, y1_hi, y1_lo, range(KD))
            residual_dve(dve, cd["out"], 2 * KD)
            pass_gate(dve, 11)
            rms_dve(dve, st, 4)
            adaln_dve(dve, st, 3, 1)
            source_lo(dve, "dve", 5 * KD, h, h_hi, h_lo, range(BY_POOL, KD))
            ffn_dve(dve, st, 1)
            pass_gate(dve, 12)
            final_dve(dve, st, 5)

        @block.gpsimd
        def _(pool):
            st = Steps(pool, pool_step)
            for n, e in enumerate((EPS, GN_EPS, 1e-12)):
                pool.memset(eps_c[:, n:n + 1], e).then_inc(eps_ready, 1)
            pass_gate(pool, 1)
            source_lo(pool, "pool", 0, h, h_hi, h_lo, range(BY_POOL))
            pass_gate(pool, 2)
            ab_pool(pool, st)
            pass_gate(pool, 3)
            pass_gate(pool, 4)
            parts_pool(pool, ab["out"], KD, then=ffn[0, 0, "up"])
            pass_gate(pool, 5)
            ffn_pool(pool, 0)
            source_lo(pool, "pool", 2 * KD, h, h_hi, h_lo, range(BY_POOL))
            ffn_parts_pool(pool, 0)
            pass_gate(pool, 6)
            for s in range(2):
                tile_lo(pool, cd["in"], 0, s)
            source_lo(pool, "pool", 3 * KD, h, h1_hi, h1_lo, range(BY_POOL))
            parts_pool(pool, cd["in"], 18)
            pass_gate(pool, 7)
            pass_gate(pool, 8)
            shift_pool(pool, st)
            pass_gate(pool, 9)
            kk_pool(pool)
            scan_pool(pool, st)
            pass_gate(pool, 10)
            for s in range(2):
                tile_lo(pool, cd["out"], 0, s)
            parts_pool(pool, cd["out"], KD, then=ffn[1, 0, "up"])
            pass_gate(pool, 11)
            ffn_pool(pool, 1)
            source_lo(pool, "pool", 5 * KD, h, h_hi, h_lo, range(BY_POOL))
            ffn_parts_pool(pool, 1)
            pass_gate(pool, 12)



def tile_out(w, k):
    return np.ascontiguousarray(w.reshape(k, P, -1, P).transpose(2, 1, 0, 3)).reshape(-1, P, k * P)


def tile_wide(w):
    return np.ascontiguousarray(w.reshape(KD, P, -1, 256).transpose(2, 1, 0, 3)).reshape(-1, P, KD * 256)


def cols(v):
    return np.asarray(v).reshape(-1, P).T


def constants():
    c = np.zeros((P, NCONST), np.float32)
    c[:, 0:P] = np.eye(P)
    c[:, P:2 * P] = 1
    half = np.arange(P) // HD
    c[:, 2 * P:3 * P] = half[:, None] == half[None, :]
    f = np.arange(P) % 32
    low = f < 16
    src = np.where(low, np.arange(P) + 16, np.arange(P) - 16)
    c[src, 3 * P + np.arange(P)] = np.where(low, -1, 1)
    at = 4 * P
    for m in masks():
        c[:, at:at + C] = np.tile(m, (2, 1))
        at += C
    assert at == NCONST
    return c


def rotation():
    f = np.arange(P) % 32
    inv = np.float32(10000.0) ** (-(f % 16).astype(np.float32) / np.float32(16))
    t = np.arange(LAT)
    pos = np.where(((np.arange(P) % 64) < 32)[:, None], (t // 64)[None, :], (t % 64)[None, :])
    ang = pos.astype(np.float32) * inv.astype(np.float32)[:, None]
    return np.stack([np.cos(ang), np.sin(ang)], 1).astype(np.float32)


def masks():
    i, j = np.arange(C)[:, None], np.arange(C)[None, :]
    out = [i < j, i > j, i <= j, i >= j]
    for l in range(LEVELS):
        b = 1 << l
        m = (i // (2 * b) == j // (2 * b)) & (i // b % 2 == 1) & (j // b % 2 == 0)
        out += [m, m.T]
    out = [m.astype(np.float32) for m in out]
    out[4], out[5] = -out[4], -out[5]
    return out


def kernel(**inputs):
    import concourse.bacc as bacc
    from concourse.bass_utils import run_bass_kernel_spmd

    a = {k: np.asarray(v) for k, v in inputs.items()}
    io = layout(a)
    nc = bacc.Bacc("TRN2", target_bir_lowering=False, num_devices=1)
    aps = {n: nc.dram_tensor("in_" + n, v.shape, mybir.dt.from_np(v.dtype), kind="ExternalInput").ap() for n, v in io.items()}
    for n, shape in OUTS.items():
        aps[n] = nc.dram_tensor("out_" + n, shape, F32, kind="ExternalOutput").ap()
    build(nc, aps)
    r = run_bass_kernel_spmd(nc, [{"in_" + n: v for n, v in io.items()}], core_ids=[0]).results[0]
    return unpack({n: np.asarray(r["out_" + n]) for n in OUTS})


def layout(a):
    io = {}
    io["x_fm"] = np.ascontiguousarray(np.concatenate([a["x_prompt"][0], a["x_sample"][0]], 0).T.reshape(KD, P, T).transpose(1, 0, 2))
    io["cvec"] = np.ascontiguousarray(np.stack([a["c_ctx"], a["c"][0]], 1).reshape(KD, P, 2).transpose(1, 0, 2))
    fields = {
        "norm1": a["norm1_g"], "norm2": a["norm2_g"], "final": a["final_g"], "mod_b": a["mod_b"],
        "conv_w": np.roll(a["ffn_conv_w"].reshape(DEPTH, 3, 2, FF), 1, 2),
        "conv_b": np.roll(a["ffn_conv_b"].reshape(DEPTH, 2, FF), 1, 1),
        "b_w": a["b_conv_w"][0], "b_b": a["b_conv_b"][0], "b_norm": a["b_norm_g"][0],
        "mu_r": a["c_mu_rkv"][0, 0], "mu_k": a["c_mu_rkv"][0, 1], "mu_v": a["c_mu_rkv"][0, 2],
        "mu_w": a["c_mu_wag"][0, 0], "mu_a": a["c_mu_wag"][0, 1], "mu_g": a["c_mu_wag"][0, 2],
        "w0": a["c_w0"][0], "a0": a["c_a0"][0], "k_k": a["c_k_k"][0], "k_a": a["c_k_a"][0], "r_k": a["c_r_k"][0],
        "ln_g": a["c_ln_g"][0], "ln_b": a["c_ln_b"][0],
        "qk_g": np.concatenate([np.tile(a["d_q_g"][0], 2 * KA), np.tile(a["d_k_g"][0], 4)]),
    }
    par = np.empty((P, NPAR), np.float32)
    for n, v in fields.items():
        v = cols(v)
        par[:, PAR[n]:PAR[n] + v.shape[1]] = v
    io["par"] = par
    io["const"] = constants()
    io["mod_w"] = np.concatenate([tile_wide(w) for w in a["mod_w"]])
    w = a["ab_w_in"][0]
    io["ab_v"] = tile_wide(w[:, AD:2 * AD])
    t = tile_out(w, KD)
    io["ab_w"] = np.concatenate([t[[12 + i // 2 if i % 2 == 0 else 8 + i // 2 for i in range(8)]], t[0:4]])
    io["w_out"] = np.concatenate([tile_out(w, KD) for w in a["w_out"]])
    up = [tile_out(w, KD) for w in a["ffn_up"]]
    io["ffn_up"] = np.concatenate([np.stack([u[KF:], u[:KF]], 1).reshape(2 * KF, P, KD * P) for u in up])
    io["ffn_down"] = np.concatenate([tile_out(w, KH) for v in a["ffn_down"] for w in (v[:KH * P], v[KH * P:])])
    io["ws_t"] = np.ascontiguousarray(a["a_ws"][0].transpose(2, 0, 1))
    io["v_rows"] = np.ascontiguousarray(np.broadcast_to(np.stack([a["a_vnorm_g"][0], a["a_vnorm_b"][0]])[None], (P, 2, AD)))
    io["bs_rows"] = np.ascontiguousarray(np.broadcast_to(np.tile(a["a_bs"][0], (1, NT))[None], (P, 4, T)))
    w = a["cd_w_in"][0]
    t = tile_out(w, KD)
    keys = [tile_out(np.concatenate([w[:, 2048 + HD * g:2048 + HD * (g + 1)]] * 2, 1), KD) for g in range(2)]
    lora = [np.concatenate([a["c_w1"][0, 0], a["c_w1"][0, 1]], 1), np.concatenate([a["c_a1"][0, 0], a["c_a1"][0, 1]], 1), a["c_g1"][0]]
    io["cd_w"] = np.concatenate([t[0:16]] + keys + [tile_out(v, KD) for v in lora] + [t[17:18]])
    ckv = a["cache_k"][0, 0].transpose(2, 1, 0)
    io["cache_k"] = np.ascontiguousarray(np.concatenate([ckv, ckv], 0))
    io["cache_v"] = np.ascontiguousarray(a["cache_v"][0, 0].reshape(CTX, P))
    io["rope"] = rotation()
    w2 = a["c_w2"][0].reshape(P, HP, P)
    a2 = a["c_a2"][0].reshape(P, HP, P)
    g2 = a["c_g2"][0].reshape(P, HP, P)
    io["scan_w"] = np.ascontiguousarray(np.stack([w2, a2, g2], 2).transpose(1, 0, 2, 3).reshape(HP, P, 3 * P))
    st = np.zeros((HP, 2, 2, HD, 2, HD), np.float32)
    for d, name in enumerate(("state_wkv_fwd", "state_wkv_bwd")):
        s = a[name][0, 0].reshape(HP, 2, HD, HD)
        for e in range(2):
            st[:, d, e, :, e, :] = s[:, e].transpose(0, 2, 1)
    io["state"] = st.reshape(2 * HP, P, P)
    return io


OUTS = {"y": (P, KD, T), "new_k": (HD, 2, CTX), "new_v": (CTX, P), "new_state": (2 * HP, P, P)}
NCONST = 4 * P + (4 + 2 * LEVELS) * C


def unpack(r):
    y = r["y"].transpose(1, 0, 2).reshape(D, T).T
    k = r["new_k"].transpose(2, 1, 0)[None, None]
    v = r["new_v"].reshape(1, 1, CTX, 2, HD)
    s = r["new_state"].reshape(HP, 2, 2, HD, 2, HD)
    s = np.stack([s[:, :, e, :, e, :] for e in range(2)], 2).transpose(1, 0, 2, 4, 3).reshape(2, 1, 1, HEADS, HD, HD)
    out = (y[None, :CTX], y[None, CTX:], k, v, s[0], s[1])
    return tuple(np.ascontiguousarray(o) for o in out)
```
